# Optimizing a Trainium2 kernel written in Bass

```python
import jax, jax.numpy as jnp
from jax import lax
import numpy as np

D_MODEL = 1024
BATCH = 1
SEQ = 1024
DEPTH = 1

LRU_HEADS = 16
LRU_HEAD_DIM = 64
D_LRU = LRU_HEADS * LRU_HEAD_DIM
SC_GROUPS = 8
SC_GROUP_DIM = 64
D_SC = SC_GROUPS * SC_GROUP_DIM
D_MIX = D_LRU + D_SC
D_IN = 2 * D_LRU + 3 * D_SC
LRU_CONV_WIDTH = 4
SC_CONV_WIDTH = 3
RG_C = 8.0
D_FF = 3 * D_MODEL
FFN_CONV_WIDTH = 3
EPS = 1e-6


def rms_norm(x, g):
    xf = x.astype(jnp.float32)
    y = xf * lax.rsqrt(jnp.mean(xf * xf, axis=-1, keepdims=True) + EPS)
    return (y * g.astype(jnp.float32)).astype(x.dtype)

def causal_dwconv(x, w):
    k_width = w.shape[0]
    s = x.shape[1]
    xp = jnp.pad(x, ((0, 0), (k_width - 1, 0), (0, 0)))
    y = xp[:, 0:s] * w[0]
    for k in range(1, k_width):
        y = y + xp[:, k:k + s] * w[k]
    return y

def rg_lru(x, wa, ba, wx, bx, lam):
    bsz, s, c = x.shape
    xh = x.reshape(bsz, s, LRU_HEADS, LRU_HEAD_DIM)
    r = jax.nn.sigmoid(jnp.einsum('bshi,hij->bshj', xh, wa).reshape(bsz, s, c) + ba)
    i = jax.nn.sigmoid(jnp.einsum('bshi,hij->bshj', xh, wx).reshape(bsz, s, c) + bx)
    log_a = -RG_C * r.astype(jnp.float32) * jax.nn.softplus(-lam.astype(jnp.float32))
    a = jnp.exp(log_a)
    mult = jnp.sqrt(-jnp.expm1(2.0 * log_a))
    b = mult * (i * x).astype(jnp.float32)

    def combine(left, right):
        a1, b1 = left
        a2, b2 = right
        return a1 * a2, a2 * b1 + b2

    _, h = lax.associative_scan(combine, (a, b), axis=1)
    return h.astype(x.dtype)

def first_inputs(seed: int = 0) -> dict:
    key = jax.random.key(seed)
    ks = jax.random.split(key, 20)
    f32 = jnp.float32
    res_scale = (2.0 * DEPTH) ** -0.5
    x = jax.random.normal(ks[0], (BATCH, SEQ, D_MODEL), f32)
    norm1_g = 1.0 + 0.02 * jax.random.normal(ks[1], (DEPTH, D_MODEL), f32)
    w_in = jax.random.normal(ks[2], (DEPTH, D_MODEL, D_IN), f32) * D_MODEL ** -0.5
    lru_conv_w = jax.random.normal(ks[3], (DEPTH, LRU_CONV_WIDTH, D_LRU), f32) * LRU_CONV_WIDTH ** -0.5
    lru_conv_b = 0.02 * jax.random.normal(ks[4], (DEPTH, D_LRU), f32)
    lru_wa = jax.random.normal(ks[5], (DEPTH, LRU_HEADS, LRU_HEAD_DIM, LRU_HEAD_DIM), f32) * LRU_HEAD_DIM ** -0.5
    lru_ba = 0.02 * jax.random.normal(ks[6], (DEPTH, D_LRU), f32)
    lru_wx = jax.random.normal(ks[7], (DEPTH, LRU_HEADS, LRU_HEAD_DIM, LRU_HEAD_DIM), f32) * LRU_HEAD_DIM ** -0.5
    lru_bx = 0.02 * jax.random.normal(ks[8], (DEPTH, D_LRU), f32)
    u = jax.random.uniform(ks[9], (DEPTH, D_LRU), f32, minval=0.9, maxval=0.999)
    a0 = u ** (1.0 / RG_C)
    lru_lambda = jnp.log(a0) - jnp.log1p(-a0)
    sc_conv_w = jax.random.normal(ks[10], (DEPTH, SC_CONV_WIDTH, D_SC), f32) * SC_CONV_WIDTH ** -0.5
    w_out = jax.random.normal(ks[11], (DEPTH, D_MIX, D_MODEL), f32) * D_MIX ** -0.5 * res_scale
    norm2_g = 1.0 + 0.02 * jax.random.normal(ks[12], (DEPTH, D_MODEL), f32)
    w_up = jax.random.normal(ks[13], (DEPTH, D_MODEL, 2 * D_FF), f32) * D_MODEL ** -0.5
    ffn_conv_w = jax.random.normal(ks[14], (DEPTH, FFN_CONV_WIDTH, 2 * D_FF), f32) * FFN_CONV_WIDTH ** -0.5
    w_down = jax.random.normal(ks[15], (DEPTH, D_FF, D_MODEL), f32) * D_FF ** -0.5 * res_scale
    final_g = 1.0 + 0.02 * jax.random.normal(ks[16], (D_MODEL,), f32)
    return {"x": x, "norm1_g": norm1_g, "w_in": w_in, "lru_conv_w": lru_conv_w,
            "lru_conv_b": lru_conv_b, "lru_wa": lru_wa, "lru_ba": lru_ba, "lru_wx": lru_wx,
            "lru_bx": lru_bx, "lru_lambda": lru_lambda, "sc_conv_w": sc_conv_w, "w_out": w_out,
            "norm2_g": norm2_g, "w_up": w_up, "ffn_conv_w": ffn_conv_w, "w_down": w_down,
            "final_g": final_g}

def first_block(x, norm1_g, w_in, lru_conv_w, lru_conv_b, lru_wa, lru_ba, lru_wx, lru_bx,
              lru_lambda, sc_conv_w, w_out, norm2_g, w_up, ffn_conv_w, w_down, final_g):
    splits = [D_LRU, 2 * D_LRU, 2 * D_LRU + D_SC, 2 * D_LRU + 2 * D_SC]
    for l in range(DEPTH):
        h = rms_norm(x, norm1_g[l])
        z = jnp.einsum('bsd,de->bse', h, w_in[l])
        lru_x, lru_gate, sc_b, sc_c, sc_x = jnp.split(z, splits, axis=-1)
        lru_x = causal_dwconv(lru_x, lru_conv_w[l]) + lru_conv_b[l]
        y_lru = rg_lru(lru_x, lru_wa[l], lru_ba[l], lru_wx[l], lru_bx[l], lru_lambda[l]) \
            * jax.nn.gelu(lru_gate)
        y_sc = sc_b * causal_dwconv(sc_c * sc_x, sc_conv_w[l])
        y_mix = jnp.concatenate([y_lru, y_sc], axis=-1)
        x = x + jnp.einsum('bse,ed->bsd', y_mix, w_out[l])
        h = rms_norm(x, norm2_g[l])
        u = causal_dwconv(jnp.einsum('bsd,df->bsf', h, w_up[l]), ffn_conv_w[l])
        gate, up = jnp.split(u, 2, axis=-1)
        x = x + jnp.einsum('bsf,fd->bsd', jax.nn.gelu(gate) * up, w_down[l])
    return rms_norm(x, final_g)


MLA_HEADS = 4
QK_NOPE_DIM = 128
QK_ROPE_DIM = 64
QK_DIM = QK_NOPE_DIM + QK_ROPE_DIM
V_HEAD_DIM = 128
Q_LORA_RANK = 512
KV_LORA_RANK = 256
MLA_WIDTH = MLA_HEADS * V_HEAD_DIM
ROPE_THETA = 10000.0
Q_BLOCK = 128
POOL_WINDOWS = (2, 4, 8, 16)
POOL_GROUPS = len(POOL_WINDOWS)
POOL_WIDTH = D_MODEL - MLA_WIDTH
POOL_GROUP_DIM = POOL_WIDTH // POOL_GROUPS
MIX_WIDTH = MLA_WIDTH + POOL_WIDTH
IN_SPLITS = (Q_LORA_RANK, KV_LORA_RANK, QK_ROPE_DIM, MLA_WIDTH, POOL_WIDTH, POOL_WIDTH)
IN_WIDTH = sum(IN_SPLITS)
RMS_EPS = 1e-6
LN_EPS = 1e-5


def rms_norm_2(x, g):
    xf = x.astype(jnp.float32)
    inv = lax.rsqrt(jnp.mean(xf * xf, axis=-1, keepdims=True) + RMS_EPS)
    return (xf * inv).astype(x.dtype) * g

def layer_norm(x, g, b):
    xf = x.astype(jnp.float32)
    mu = jnp.mean(xf, axis=-1, keepdims=True)
    var = jnp.mean(jnp.square(xf - mu), axis=-1, keepdims=True)
    return ((xf - mu) * lax.rsqrt(var + LN_EPS)).astype(x.dtype) * g + b

def rope_cos_sin(positions, dtype):
    half = QK_ROPE_DIM // 2
    inv_freq = ROPE_THETA ** (-jnp.arange(half, dtype=jnp.float32) / half)
    ang = positions.astype(jnp.float32)[..., None] * inv_freq
    return jnp.cos(ang).astype(dtype), jnp.sin(ang).astype(dtype)

def apply_rope(t, cos, sin):
    t1, t2 = jnp.split(t, 2, axis=-1)
    return jnp.concatenate([t1 * cos - t2 * sin, t1 * sin + t2 * cos], axis=-1)

def mla_branch(x_q, x_kv, k_rope_raw, positions, q_norm_g, w_uq, kv_norm_g, w_ukv):
    B, S, _ = x_q.shape
    cos, sin = rope_cos_sin(positions, x_q.dtype)
    q = (rms_norm_2(x_q, q_norm_g) @ w_uq).reshape(B, S, MLA_HEADS, QK_DIM)
    q_nope, q_rope = q[..., :QK_NOPE_DIM], q[..., QK_NOPE_DIM:]
    q_rope = apply_rope(q_rope, cos[:, :, None, :], sin[:, :, None, :])
    kv = (rms_norm_2(x_kv, kv_norm_g) @ w_ukv).reshape(B, S, MLA_HEADS, QK_NOPE_DIM + V_HEAD_DIM)
    k_nope, v = kv[..., :QK_NOPE_DIM], kv[..., QK_NOPE_DIM:]
    k_rope = apply_rope(k_rope_raw, cos, sin)
    scale = QK_DIM ** -0.5
    nb = S // Q_BLOCK
    qn_b = q_nope.reshape(B, nb, Q_BLOCK, MLA_HEADS, QK_NOPE_DIM).transpose(1, 0, 2, 3, 4)
    qr_b = q_rope.reshape(B, nb, Q_BLOCK, MLA_HEADS, QK_ROPE_DIM).transpose(1, 0, 2, 3, 4)
    pos_b = positions.reshape(B, nb, Q_BLOCK).transpose(1, 0, 2)
    neg = jnp.finfo(jnp.float32).min

    def attend(args):
        qn, qr, pq = args
        s = (jnp.einsum('bqhd,bkhd->bhqk', qn, k_nope)
             + jnp.einsum('bqhr,bkr->bhqk', qr, k_rope)).astype(jnp.float32) * scale
        mask = pq[:, None, :, None] >= positions[:, None, None, :]
        p = jax.nn.softmax(jnp.where(mask, s, neg), axis=-1)
        return jnp.einsum('bhqk,bkhd->bqhd', p.astype(v.dtype), v)

    o = lax.map(attend, (qn_b, qr_b, pos_b))
    return o.transpose(1, 0, 2, 3, 4).reshape(B, S, MLA_WIDTH)

def pool_branch(u, pool_w, pool_scale):
    B, S, _ = u.shape
    uf = u.astype(jnp.float32).reshape(B, S, POOL_GROUPS, POOL_GROUP_DIM)
    cs = jnp.concatenate([jnp.zeros((B, 1, POOL_GROUPS, POOL_GROUP_DIM), jnp.float32),
                          jnp.cumsum(uf, axis=1)], axis=1)
    hi = jnp.arange(S) + 1
    means = []
    for g, w in enumerate(POOL_WINDOWS):
        lo = jnp.maximum(hi - w, 0)
        cnt = (hi - lo).astype(jnp.float32)[None, :, None]
        means.append((cs[:, hi, g] - cs[:, lo, g]) / cnt)
    pooled = jnp.stack(means, axis=2) - uf
    mixed = jnp.einsum('bsgc,gcd->bsgd', pooled.astype(u.dtype), pool_w)
    return mixed.reshape(B, S, POOL_WIDTH) * pool_scale

def second_inputs(seed: int = 0) -> dict:
    key = jax.random.key(seed)
    ks = jax.random.split(key, 12)
    beta = (8.0 * DEPTH) ** -0.25
    nrm = jax.random.normal
    return {
        "x": nrm(ks[0], (BATCH, SEQ, D_MODEL), jnp.float32),
        "positions": jnp.broadcast_to(jnp.arange(SEQ, dtype=jnp.int32), (BATCH, SEQ)),
        "w_in": nrm(ks[1], (D_MODEL, IN_WIDTH), jnp.float32) * D_MODEL ** -0.5,
        "q_norm_g": 1.0 + 0.05 * nrm(ks[2], (Q_LORA_RANK,), jnp.float32),
        "w_uq": nrm(ks[3], (Q_LORA_RANK, MLA_HEADS * QK_DIM), jnp.float32) * Q_LORA_RANK ** -0.5,
        "kv_norm_g": 1.0 + 0.05 * nrm(ks[4], (KV_LORA_RANK,), jnp.float32),
        "w_ukv": nrm(ks[5], (KV_LORA_RANK, MLA_HEADS * (QK_NOPE_DIM + V_HEAD_DIM)), jnp.float32) * KV_LORA_RANK ** -0.5,
        "pool_w": nrm(ks[6], (POOL_GROUPS, POOL_GROUP_DIM, POOL_GROUP_DIM), jnp.float32) * POOL_GROUP_DIM ** -0.5,
        "pool_scale": 1.0 + 0.1 * nrm(ks[7], (POOL_WIDTH,), jnp.float32),
        "w_out": nrm(ks[8], (MIX_WIDTH, D_MODEL), jnp.float32) * (MIX_WIDTH ** -0.5) * beta,
        "ln_g": 1.0 + 0.05 * nrm(ks[9], (DEPTH, D_MODEL), jnp.float32),
        "ln_b": 0.02 * nrm(ks[10], (DEPTH, D_MODEL), jnp.float32),
    }

def second_block(x, positions, w_in, q_norm_g, w_uq, kv_norm_g, w_ukv, pool_w, pool_scale, w_out, ln_g, ln_b):
    alpha = (2.0 * DEPTH) ** 0.25
    splits = [int(c) for c in np.cumsum(IN_SPLITS)[:-1]]
    for layer in range(DEPTH):
        h = x @ w_in
        x_q, x_kv, k_rope_raw, gate_a, u_pool, gate_b = jnp.split(h, splits, axis=-1)
        y_a = mla_branch(x_q, x_kv, k_rope_raw, positions, q_norm_g, w_uq, kv_norm_g, w_ukv) * jax.nn.silu(gate_a)
        y_b = pool_branch(u_pool, pool_w, pool_scale) * jax.nn.silu(gate_b)
        mix = jnp.concatenate([y_a, y_b], axis=-1) @ w_out
        x = layer_norm(alpha * x + mix, ln_g[layer], ln_b[layer])
    return x


def setup_inputs(seed=0):
    out = dict(first_inputs(seed))
    for name, value in second_inputs(seed + 1).items():
        if name != "x":
            out[name + "_2"] = value
    return out


def reference(
    x, norm1_g, w_in, lru_conv_w, lru_conv_b, lru_wa, lru_ba, lru_wx, lru_bx, lru_lambda,
    sc_conv_w, w_out, norm2_g, w_up, ffn_conv_w, w_down, final_g, positions_2, w_in_2,
    q_norm_g_2, w_uq_2, kv_norm_g_2, w_ukv_2, pool_w_2, pool_scale_2, w_out_2, ln_g_2, ln_b_2,
):
    x = first_block(
        x, norm1_g, w_in, lru_conv_w, lru_conv_b, lru_wa, lru_ba, lru_wx, lru_bx, lru_lambda,
        sc_conv_w, w_out, norm2_g, w_up, ffn_conv_w, w_down, final_g,
    )
    return second_block(
        x, positions_2, w_in_2, q_norm_g_2, w_uq_2, kv_norm_g_2, w_ukv_2, pool_w_2,
        pool_scale_2, w_out_2, ln_g_2, ln_b_2,
    )


_drawn_inputs = setup_inputs


def setup_inputs(seed=0):
    import zlib

    import numpy as np

    out = dict(_drawn_inputs(seed))
    spreads = {}
    factors = {'norm1_g': 3.446,
     'lru_ba': 8.0,
     'lru_bx': 8.0,
     'norm2_g': 5.073,
     'final_g': 2.819,
     'q_norm_g_2': 8.0,
     'kv_norm_g_2': 8.0,
     'pool_scale_2': 3.38,
     'ln_b_2': 2.869}
    for name, (base, spread) in spreads.items():
        noise = np.random.default_rng([zlib.crc32(name.encode()), seed]).standard_normal(out[name].shape)
        drawn = base * np.exp(spread * noise) if base else spread * noise
        out[name] = __import__('jax').numpy.asarray(drawn.astype(out[name].dtype))
    for name, factor in factors.items():
        out[name] = (out[name] * factor).astype(out[name].dtype)
    return out
```

```python
from contextlib import ExitStack, contextmanager

import numpy as np
import concourse.bass as bass
from concourse import mybir

P = 128
SEQ = 1024
D = 1024
KT = D // P
NT = SEQ // P
LRU_TILES = 8
SC_TILES = 4
FF_TILES = 24
FF_GROUP = 8
GROUPS = FF_TILES // FF_GROUP
HEADS = 4
NOPE, ROPE, VDIM = 128, 64, 128
QK = NOPE + ROPE
Q_TILES, KV_TILES = 4, 2
HALF = 512
EPS = 1e-6
LN_EPS = 1e-5
ALPHA = 2.0 ** 0.25
SCALE = float(QK) ** -0.5
MASKED = -1.0e30
WINDOWS = (2, 4, 8, 16)
TILE = SEQ * 4

V_NORM1, V_CONVW, V_CONVB, V_BA, V_BX, V_LAM = 0, 8, 40, 48, 56, 64
V_SCW, V_NORM2, V_FINAL, V_QN, V_KVN, V_POOL = 72, 84, 92, 100, 104, 106
V_ROWS = 110
FFN_ROWS = 144
V_FFN = V_ROWS
V_POS = V_FFN + FFN_ROWS
V_COLS = V_POS + NT

N_SC = 0
N_LRU = N_SC + 3 * SC_TILES
N_OUT = N_LRU + 2 * LRU_TILES
N_FF = N_OUT + 12
GROUP_BLOCKS = 2 * FF_GROUP + KT
N_IN2 = N_FF + GROUPS * GROUP_BLOCKS
N_POOL = N_IN2 + Q_TILES + KV_TILES
N_GATE = N_POOL + 2 * len(WINDOWS)
N_KR = N_GATE + HEADS
N_UKV = N_KR + 1
N_UQ = N_UKV + 2
N_BLOCKS = N_UQ + 3

UNITS = HEADS * NT

TWO_PI_A = 6.28125
TWO_PI_B = float(np.float32(np.floor((2 * np.pi - 6.28125) * 2 ** 20) / 2 ** 20))
TWO_PI_C = float(np.float32(2 * np.pi - 6.28125 - TWO_PI_B))
ROUND = 12582912.0


class Steps:

    def __init__(self, eng, sem):
        self.eng, self.sem, self.n, self.run = eng, sem, 0, 0

    def __call__(self, instruction):
        instruction.then_inc(self.sem, 1)
        self.n += 1
        self.eng.wait_ge(self.sem, self.n + self.run)

    @contextmanager
    def loop(self, count):
        start, outer, per = self.n, self.run, self.per
        with self.eng.Fori(0, count) as i:
            self.run = outer + i * per
            yield i
        assert self.n == start + per, (self.n - start, per)
        self.n, self.run = start + per * count, outer

    def of(self, per):
        self.per = per
        return self


def program(nc, x, norm1_g, w_in, lru_conv_w, lru_conv_b, lru_wa, lru_ba, lru_wx, lru_bx, lru_lambda,
            sc_conv_w, w_out, norm2_g, w_up, ffn_conv_w, w_down, final_g, positions_2, w_in_2,
            q_norm_g_2, w_uq_2, kv_norm_g_2, w_ukv_2, pool_w_2, pool_scale_2, w_out_2, ln_g_2,
            ln_b_2, rope_freq, out):
    f32, f32r, i32 = mybir.dt.float32, mybir.dt.float32r, mybir.dt.int32
    ALU, ACT = mybir.AluOpType, mybir.ActivationFunctionType
    ctx = ExitStack()
    with ctx:
        base = (nc.sbuf_base + 31) // 32 * 32
        W0, H0 = base, base + 6 * TILE
        X0 = H0 + 16 * TILE
        G0 = X0 + 8 * TILE
        S0 = G0 + 16 * TILE
        C0 = S0 + 5 * TILE

        def at(name, offset, shape, dt=f32):
            return nc.alloc_sbuf_tensor_at(name, [P] + list(shape), dt, offset=offset)

        def tile(name, offset, n, dt=f32, count=None):
            return at(name, offset + n * TILE, [SEQ] if count is None else [count, SEQ], dt)

        w_raw = [tile(f"w_raw{s}", W0, s) for s in range(2)]
        w_hi = [tile(f"w_hi{s}", W0, 2 + s, f32r) for s in range(2)]
        w_lo = [tile(f"w_lo{s}", W0, 4 + s, f32r) for s in range(2)]
        h_hi = tile("h_hi", H0, 0, f32r, 8)
        h_lo = tile("h_lo", H0, 8, f32r, 8)
        xs = tile("xs", X0, 0, f32, 8)
        x_tok = tile("x_tok", G0, 0, f32, 8)
        ysc_hi = tile("ysc_hi", G0, 0, f32r, 4)
        ysc_lo = tile("ysc_lo", G0, 4, f32r, 4)
        bd_raw = at("bd_raw", G0 + 8 * TILE, [2, LRU_TILES, P])
        bd_hi = at("bd_hi", G0 + 10 * TILE, [2, P], f32r)
        bd_lo = at("bd_lo", G0 + 11 * TILE, [2, P], f32r)
        xc_hi = tile("xc_hi", G0, 12, f32r)
        xc_lo = tile("xc_lo", G0, 13, f32r)
        root = tile("root", G0, 14)
        gelu_gate = tile("gelu_gate", G0, 15)
        square_dve = tile("square_dve", G0, 15)
        gu_hi = tile("gu_hi", G0, 0, f32r, 8)
        gu_lo = tile("gu_lo", G0, 8, f32r, 8)
        lat = tile("lat", G0, 0, f32, 6)
        kr_hi = tile("kr_hi", G0, 6, f32r)
        kr_lo = tile("kr_lo", G0, 7, f32r)
        acc_q = tile("acc_q", G0, 8)
        acc_kv = tile("acc_kv", G0, 9)
        pw_raw = at("pw_raw", G0 + 10 * TILE, [4, P])
        pw_hi = at("pw_hi", G0 + 10 * TILE + 2048, [P], f32r)
        pw_lo = at("pw_lo", G0 + 10 * TILE + 2560, [P], f32r)
        pooled_hi = tile("pooled_hi", G0, 11, f32r)
        pooled_lo = tile("pooled_lo", G0, 12, f32r)
        square2 = tile("square2", G0, 13)
        sin_t = tile("sin_t", G0, 14)
        cos_t = tile("cos_t", G0, 15)
        v_hi = at("v_hi", G0, [NT, HEADS * VDIM], f32r)
        v_lo = at("v_lo", G0 + 8 * TILE, [NT, HEADS * VDIM], f32r)
        qr_hi = tile("qr_hi", G0, 4, f32r, 2)
        qr_lo = tile("qr_lo", G0, 12, f32r, 2)
        kn_hi = tile("kn_hi", X0, 0, f32r, 4)
        kn_lo = tile("kn_lo", X0, 4, f32r, 4)
        kvn_hi = tile("kvn_hi", H0, 8, f32r, 2)
        kvn_lo = tile("kvn_lo", H0, 10, f32r, 2)
        qn_hi = tile("qn_hi", H0, 0, f32r, 4)
        qn_lo = tile("qn_lo", H0, 4, f32r, 4)
        qh_hi = tile("qh_hi", H0, 8, f32r, 4)
        qh_lo = tile("qh_lo", H0, 12, f32r, 4)
        pt_hi = at("pt_hi", H0, [NT, HALF], f32r)
        pt_lo = at("pt_lo", H0 + 4 * TILE, [NT, HALF], f32r)
        prob = [tile(f"prob{s}", W0, s) for s in range(3)]
        mask = [tile(f"mask{s}", W0, 3 + s) for s in range(2)]
        gate_in = [at(f"gate_in{s}", S0 + s * 2048, [HALF]) for s in range(2)]
        ya_out = [at(f"ya_out{s}", S0 + TILE + s * 2048, [HALF]) for s in range(2)]
        z_hi = tile("z_hi", H0, 0, f32r, 8)
        z_lo = tile("z_lo", H0, 8, f32r, 8)
        wo_hi = tile("wo_hi", G0, 0, f32r, 8)
        wo_lo = tile("wo_lo", G0, 8, f32r, 8)
        resid = tile("resid", X0, 0, f32, 8)
        zin = [tile(f"zin{s}", W0, s) for s in range(4)]
        ln_g = tile("ln_g", S0, 0)
        ln_b = tile("ln_b", S0, 1)
        ln_sq = tile("ln_sq", S0, 2)
        ln_v = [tile(f"ln_v{s}", S0, 3 + s) for s in range(2)]
        scr = [tile(f"scr{s}", S0, s) for s in range(5)]
        pos_f = tile("pos_f", S0, 4)
        pos_i = at("pos_i", S0 + 4 * TILE, [SEQ], i32)
        at_c = [C0]

        def const(name, cols, dt=f32):
            t = at(name, at_c[0], [cols], dt)
            at_c[0] += (cols * 4 + 31) // 32 * 32
            return t

        vec = const("vec", V_COLS)
        ident = const("ident", P)
        meanw = const("meanw", 3)
        rc = const("rc", 16)
        eps = const("eps", 2)
        half_ba = const("half_ba", 8)
        half_bx = const("half_bx", 8)
        half_ps = const("half_ps", 4)
        kh = const("kh", 8)
        kx = const("kx", 8)
        small = const("small", 48)
        rstd = const("rstd", 8)
        freq = const("freq", 1)
        sign = const("sign", 1)
        stat = const("stat", 16)
        assert at_c[0] <= nc.sbuf_usable_end, at_c[0]

        ps = [ctx.enter_context(nc.psum_tensor(f"ps{s}", [P, SEQ], f32)) for s in range(4)]

        x_park = nc.dram_tensor("x_park", (KT, P, SEQ), f32, kind="Internal").ap()
        res_park = nc.dram_tensor("res_park", (NT, P, D), f32, kind="Internal").ap()
        gate_park = nc.dram_tensor("gate_park", (HEADS, P, SEQ), f32, kind="Internal").ap()
        y_park = nc.dram_tensor("y_park", (KT, P, SEQ), f32, kind="Internal").ap()

        def sem(name):
            return ctx.enter_context(nc.semaphore(name))

        rows_in, x_in = sem("rows_in"), [sem(f"x_in{n}") for n in range(4)]
        bd_in, pw_in, pos_in, freq_in = sem("bd_in"), sem("pw_in"), sem("pos_in"), sem("freq_in")
        w_in_sem = [sem(f"w_loaded{s}") for s in range(2)]
        x_parked, x_back = sem("x_parked"), [sem(f"x_back{s}") for s in range(2)]
        res_parked = [sem(f"res_parked{q}") for q in range(2)]
        gate_parked = [sem(f"gate_parked{q}") for q in range(2)]
        ya_parked = [sem(f"ya_parked{q}") for q in range(2)]
        y_parked = sem("y_parked")
        gate_back = [sem(f"gate_back{s}") for s in range(2)]
        z_loaded = [sem(f"z_loaded{s}") for s in range(4)]
        res_back, ln_in = sem("res_back"), sem("ln_in")
        stored = [sem(f"stored{q}") for q in range(2)]
        w_hi_done, w_lo_done, block_done = sem("w_hi_done"), sem("w_lo_done"), sem("block_done")
        dve_step, pool_step = sem("dve_step"), sem("pool_step")
        ident_done, bd_zeroed, const_done = sem("ident_done"), sem("bd_zeroed"), sem("const_done")
        sign_done = sem("sign_done")
        pos_f_done, vec_t, vec_done = sem("pos_f_done"), sem("vec_t"), sem("vec_done")
        lam_abs, lam_exp, params_done = sem("lam_abs"), sem("lam_exp"), sem("params_done")
        sumsq_dve = sem("sumsq_dve")
        sumsq, ms_done, root_done, rstd_done, rb_done = (sem("sumsq"), sem("ms_done"),
            sem("root_done"), sem("rstd_done"), sem("rb_done"))
        sq_done, acc_done = sem("sq_done"), sem("acc_done")
        xt_done, xt_copied = sem("xt_done"), sem("xt_copied")
        v_done, hi_done = sem("normed"), sem("normed_hi")
        lo_dve, lo_pool = sem("normed_lo_dve"), sem("normed_lo_pool")
        sc_c, sc_p, sc_base, sc_y, sc_hi, sc_lo = (sem("sc_c"), sem("sc_p"), sem("sc_base"),
            sem("sc_y"), sem("sc_hi"), sem("sc_lo"))
        conv_base, conv_done, xc_hi_done, xc_lo_done = (sem("conv_base"), sem("conv_done"),
            sem("xc_hi_done"), sem("xc_lo_done"))
        bd_hi_done, ri_done, rt_done, it_done = (sem("bd_hi_done"), sem("ri_done"), sem("rt_done"),
            sem("it_done"))
        gelu_done, ex_done, s_done, root_s, y_done = (sem("gelu_done"), sem("ex_done"),
            sem("s_done"), sem("root_s"), sem("y_done"))
        x1_done = sem("x1_done")
        ff_base = [sem(f"ff_base{s}") for s in range(4)]
        ff_conv = [sem(f"ff_conv{s}") for s in range(4)]
        ff_gelu = [sem(f"ff_gelu{q}") for q in range(2)]
        ff_v = [sem(f"ff_v{q}") for q in range(2)]
        ff_hi = [sem(f"ff_hi{q}") for q in range(2)]
        ff_lo = [sem(f"ff_lo{q}") for q in range(2)]
        dn_done = [sem(f"dn_done{s}") for s in range(4)]
        tok_t, tok_copied = sem("tok_t"), sem("tok_copied")
        lat_done, acc_q_done, acc_kv_done = sem("lat_done"), sem("acc_q_done"), sem("acc_kv_done")
        sq2_done = sem("sq2_done")
        red_done, trig_done = sem("red_done"), sem("trig_done")
        u_done, pl_done, pl_hi, pl_lo, pw_hi_done, pool_mm = (sem("u_done"), sem("pl_done"),
            sem("pl_hi"), sem("pl_lo"), sem("pw_hi_done"), sem("pool_mm"))
        gb_done = sem("gb_done")
        th_done, yb_done = sem("th_done"), sem("yb_done")
        ga_th, ga_done = sem("ga_th"), sem("ga_done")
        ms2_done, root2_done, rstd2_done, rb2_done = (sem("ms2_done"), sem("root2_done"),
            sem("rstd2_done"), sem("rb2_done"))
        latn_done, latn_hi, latn_lo_d, latn_lo_p = (sem("latn_done"), sem("latn_hi"),
            sem("latn_lo_d"), sem("latn_lo_p"))
        rope_sw, rope_a, rope_v, rope_hi, rope_lo = (sem("rope_sw"),
            sem("rope_a"), sem("rope_v"), sem("rope_hi"), sem("rope_lo"))
        nope_hi, nope_lo = sem("nope_hi"), sem("nope_lo")
        mask_done, score_done, smax_done, nmax_done, exp_done, p_done = (sem("mask_done"),
            sem("score_done"), sem("smax_done"), sem("nmax_done"), sem("exp_done"), sem("p_done"))
        pt_done, pt_hi_done, pt_lo_done, pv_done, ya_done = (sem("pt_done"), sem("pt_hi_done"),
            sem("pt_lo_done"), sem("pv_done"), sem("ya_done"))
        z_hi_done, z_lo_done, zp_lo_done, mix_done = (sem("z_hi_done"), sem("z_lo_done"),
            sem("zp_lo_done"), sem("mix_done"))
        ln_sum, ln_mean, ln_ssq, ln_root, ln_gs, ln_out = (sem("ln_sum"), sem("ln_mean"),
            sem("ln_ssq"), sem("ln_root"), sem("ln_gs"), sem("ln_out"))

        block = ctx.enter_context(nc.Block())
        rows0, rows1, rows2 = scr[0], scr[1], scr[2]
        pos_rows_i = at("pos_rows_i", S0 + 3 * TILE, [P], i32)
        pos_rows = at("pos_rows", S0 + 3 * TILE + 512, [P])

        @block.sync
        def _(sp):
            x_v = x.rearrange("o (n p) d -> p (o n) d", p=P)
            for n in range(4):
                sp.dma_start(x_tok[:, :, 256 * n:256 * n + 256], x_v[:, :, 256 * n:256 * n + 256]).then_inc(x_in[n], 16)

            def load(n, h, *views):
                if n >= 2:
                    sp.wait_ge(w_lo_done, n - 1 + 2 * h)
                for dst, src in views:
                    sp.dma_start(dst, src).then_inc(w_in_sem[n % 2], 16)

            def cols(n, k, w):
                return w_raw[n % 2][:, 0:k * w].rearrange("p (k n) -> p k n", n=w)

            w_in_v = w_in.rearrange("o (k p) n -> p (o k) n", p=P)
            sc0 = 2 * LRU_TILES * P
            for j in range(SC_TILES):
                for b, part in enumerate((1, 2, 0)):
                    n = N_SC + 3 * j + b
                    load(n, 0, (cols(n, 8, P), w_in_v[:, :, sc0 + part * 512 + j * P:sc0 + part * 512 + (j + 1) * P]))
                if j == 0:
                    sp.wait_ge(bd_zeroed, 1)
                    for which, wg in enumerate((lru_wa, lru_wx)):
                        heads = wg.rearrange("o (c e) i j -> (o e) i c j", e=2)
                        for e in range(2):
                            sp.dma_start(bd_raw[64 * e:64 * e + 64, which, :, 64 * e:64 * e + 64],
                                         heads[e]).then_inc(bd_in, 16)
            sp.wait_ge(xt_copied, KT)
            sp.dma_start(x_park.rearrange("c p t -> p c t"), xs[:, :, :]).then_inc(x_parked, 16)
            with sp.Fori(0, LRU_TILES) as c:
                for b in range(2):
                    load(N_LRU + b, c, (cols(b, 8, P), w_in_v[:, :, bass.ds(b * D + c * P, P)]))
            w_lru = w_out[0, 0:D, :].rearrange("(k p) n -> p k n", p=P)
            w_sc = w_out[0, D:D + 512, :].rearrange("(k p) n -> p k n", p=P)
            sp.wait_ge(x_parked, 16)
            with sp.Fori(1, 3) as r1:
                r = r1 - 1
                for b in range(6):
                    src = w_sc[:, :, bass.ds(r1 * 512 - 512 + b * 256, 256)] if b < 2 else \
                        w_lru[:, :, bass.ds(r1 * 512 - 512 + (b - 2) * P, P)]
                    load(N_OUT + b, 3 * r, (cols(b, 4, 256) if b < 2 else cols(b, 8, P), src))
                    if b >= 2:
                        if b == 2:
                            sp.wait_ge(y_done, LRU_TILES)
                        s = b % 2
                        sp.wait_ge(x1_done, (3 * r if b == 2 else 4 * r + b - 3) + 1)
                        sp.dma_start(scr[s][:, :], x_park[bass.ds(4 * r + b - 2, 1)].rearrange("o p t -> p (o t)")
                                     ).then_inc(x_back[s], 16)
            w_up_v = w_up.rearrange("o (k p) n -> p (o k) n", p=P)
            w_dn_v = w_down.rearrange("o (k p) n -> p (o k) n", p=P)
            with sp.Fori(0, GROUPS) as g:
                with sp.Fori(0, FF_GROUP // 2) as fp:
                    for b in range(4):
                        col = (b % 2) * 3072 + g * (FF_GROUP * P) + fp * 256 + (b // 2) * P
                        load(N_FF + b, g * (GROUP_BLOCKS // 2) + fp * 2,
                             (cols(b, 8, P), w_up_v[:, :, bass.ds(col, P)]))
                with sp.Fori(0, 2) as dp:
                    for b in range(4):
                        load(N_FF + 2 * FF_GROUP + b, g * (GROUP_BLOCKS // 2) + dp * 2,
                             (cols(b, 8, P), w_dn_v[:, bass.ds(g * FF_GROUP, FF_GROUP), bass.ds(dp * 512 + b * P, P)]))
            w2_v = w_in_2.rearrange("(k p) n -> p k n", p=P)
            order = [i * P for i in range(Q_TILES + KV_TILES)]
            for g in range(4):
                order += [1344 + g * P, 1856 + g * P]
            order += [832 + h * P for h in range(HEADS)]
            for i, col in enumerate(order):
                n = N_IN2 + i
                load(n, 0, (cols(n, 8, P), w2_v[:, :, col:col + P]))
                if i == 2:
                    sp.wait_ge(block_done, N_IN2)
                    sp.dma_start(pw_raw[:, :, :], pool_w_2.rearrange("g c d -> c g d")).then_inc(pw_in, 16)
                    sp.wait_ge(ms_done, 2)
                    sp.dma_start(pos_i[:, :], positions_2.broadcast_to([P, SEQ])).then_inc(pos_in, 16)
            n = N_KR
            load(n, 0, (cols(n, 8, P)[:, :, 0:64], w2_v[:, :, 768:832]),
                 (cols(n, 8, P)[:, :, 64:128], w2_v[:, :, 768:832]))
            ukv = w_ukv_2.rearrange("(k p) (h e n) -> p k h e n", p=P, h=HEADS, e=2)
            for part in range(2):
                n = N_UKV + part
                dst = w_raw[n % 2][:, :].rearrange("p (k h n) -> p k h n", k=2, h=HEADS)
                load(n, 0, *[(dst[:, k], ukv[:, k, :, part, :]) for k in range(2)])
            uq = w_uq_2.rearrange("(k p) (h n) -> p k h n", p=P, h=HEADS)
            for b in range(2):
                n = N_UQ + b
                dst = w_raw[n % 2][:, :].rearrange("p (k h n) -> p k h n", k=4, h=2)
                load(n, 0, *[(dst[:, :, e, :], uq[:, :, 2 * b + e, 0:NOPE]) for e in range(2)])
            n = N_UQ + 2
            dst = w_raw[n % 2][:, :].rearrange("p (k h n) -> p k h n", k=4, h=HEADS)
            load(n, 0, *[(dst[:, :, h, :], uq[:, :, h, NOPE:QK]) for h in range(HEADS)])
            for q in range(2):
                sp.wait_ge(gate_parked[q], 16 * HEADS // 2)
            for i in range(2 * HEADS):
                if i >= 2:
                    sp.wait_ge(ya_done, i - 1)
                if i == 0:
                    sp.wait_ge(rope_lo, 3)
                sp.dma_start(gate_in[i % 2][:, :], gate_park[i // 2][:, (i % 2) * HALF:(i % 2 + 1) * HALF]
                             ).then_inc(gate_back[i % 2], 16)
                if i >= 1:
                    j = i - 1
                    sp.wait_ge(ya_done, j + 1)
                    sp.dma_start(y_park[j // 2][:, (j % 2) * HALF:(j % 2 + 1) * HALF], ya_out[j % 2][:, :]
                                 ).then_inc(ya_parked[j % 2], 16)
            j = 2 * HEADS - 1
            sp.wait_ge(ya_done, j + 1)
            sp.dma_start(y_park[j // 2][:, (j % 2) * HALF:(j % 2 + 1) * HALF], ya_out[j % 2][:, :]
                         ).then_inc(ya_parked[j % 2], 16)
            for q in range(2):
                sp.wait_ge(res_parked[q], 16 * NT // 2)
            sp.wait_ge(pt_done, UNITS)
            sp.dma_start(resid[:, :, :], res_park.rearrange("n p d -> p n d")).then_inc(res_back, 16)
            for i in range(16):
                if i >= 4:
                    sp.wait_ge(z_lo_done if i % 2 == 0 else zp_lo_done, (i - 4) // 2 + 1)
                if i == 1:
                    sp.wait_ge(y_parked, 16 * 4)
                if i == 9:
                    for q in range(2):
                        sp.wait_ge(ya_parked[q], 16 * HEADS)
                k = i // 2
                k = (k + 4) % 8
                src = w_out_2[k * P:(k + 1) * P, :] if i % 2 == 0 else y_park[k]
                sp.dma_start(zin[i % 4][:, :], src).then_inc(z_loaded[i % 4], 16)
            sp.dma_start(ln_g[:, :], ln_g_2.broadcast_to([P, D])).then_inc(ln_in, 16)
            sp.dma_start(ln_b[:, :], ln_b_2.broadcast_to([P, D])).then_inc(ln_in, 16)
            out_v = out.rearrange("o (n p) d -> (o n) p d", p=P)
            for t in range(NT):
                sp.wait_ge(ln_out, t + 1)
                sp.dma_start(out_v[t], ln_v[t % 2][:, :]).then_inc(stored[t % 2], 16)
            for q in range(2):
                sp.wait_ge(stored[q], 16 * NT // 2)

        def latents():
            return [(kvn_hi[:, i, :], kvn_lo[:, i, :]) for i in range(KV_TILES)] + \
                   [(qn_hi[:, i, :], qn_lo[:, i, :]) for i in range(Q_TILES)]

        def lat_tile(i):
            return lat[:, (i + Q_TILES) % (Q_TILES + KV_TILES), :]

        def raw_loads(n):
            parts = {N_KR: 2, N_UKV: 2, N_UKV + 1: 2, N_UQ: 2, N_UQ + 1: 2, N_UQ + 2: 4}
            return n // 2 + 1 + sum(k - 1 for m, k in parts.items() if m <= n and m % 2 == n % 2)

        def read(sem_n, h=0):
            return sem_n + 1 + 2 * h

        def matmul3(pe, out_ap, w_h, w_l, x_h, x_l, first, last):
            halves = [slice(0, HALF), slice(HALF, SEQ)]
            for w, x, a, b in ((w_h, x_h, first, False), (w_h, x_l, False, False),
                               (w_l, x_h, False, last)):
                for t in halves:
                    mm = nc.tensor.matmul(out_ap[:, t], w, x[:, t], start=a, stop=b)
            return mm

        @block.gpsimd
        def _(pool):
            step = Steps(pool, pool_step)
            for free in (acc_done, *ff_lo):
                nc.gpsimd.sem_inc(free, 1)
            step(nc.gpsimd.memset(ident[:, :], 0.0))
            nc.gpsimd.affine_select(out=ident[:, :], in_=ident[:, :], compare_op=ALU.not_equal, fill=1.0,
                                    base=0, pattern=[[-1, P]], channel_multiplier=1).then_inc(ident_done, 1)
            nc.gpsimd.memset(bd_raw[:, :, :, :], 0.0).then_inc(bd_zeroed, 1)
            for i, n in enumerate((D, Q_TILES * P, KV_TILES * P)):
                nc.gpsimd.memset(meanw[:, i:i + 1], 1.0 / n).then_inc(const_done, 1)
            nc.gpsimd.memset(eps[:, 0:1], EPS).then_inc(const_done, 1)
            nc.gpsimd.memset(eps[:, 1:2], LN_EPS).then_inc(const_done, 1)
            for t in range(16):
                nc.gpsimd.memset(rc[:, t:t + 1], 1.0 / (t + 1)).then_inc(const_done, 1)

            def low(n, h=0):
                if n >= N_BLOCKS:
                    return
                s = n % 2
                pool.wait_ge(w_hi_done, n + 1 + 2 * h)
                nc.gpsimd.tensor_tensor(w_lo[s][:, :], w_raw[s][:, :], w_hi[s][:, :].bitcast(f32),
                                        ALU.subtract).then_inc(w_lo_done, 1)

            def odd_lows(i, src):
                for c in range(1, KT, 2):
                    pool.wait_ge(hi_done, 8 * i + c + 1)
                    nc.gpsimd.tensor_tensor(h_lo[:, c, :], src(c), h_hi[:, c, :].bitcast(f32),
                                            ALU.subtract).then_inc(lo_pool, 1)

            low(0)
            low(1)
            odd_lows(0, lambda c: scr[c % 2][:, :])
            for j in range(SC_TILES):
                low(3 * j + 2)
                low(3 * j + 3)
                low(3 * j + 4)
                pool.wait_ge(sc_hi, j + 1)
                nc.gpsimd.tensor_tensor(ysc_lo[:, j, :], scr[3][:, :], ysc_hi[:, j, :].bitcast(f32),
                                        ALU.subtract).then_inc(sc_lo, 1)
            with pool.Fori(0, LRU_TILES) as c:
                low(N_LRU + 2, c)
                low(N_LRU + 3, c)
            pool.wait_ge(y_done, LRU_TILES)
            nc.gpsimd.memset(scr[4][:, :], 0.0).then_inc(acc_done, 1)
            odd_lows(1, lambda c: xs[:, c, :])
            with pool.Fori(0, 2) as r:
                for b in range(6):
                    low(N_OUT + b + 2, 3 * r)
                    if b >= 2:
                        pool.wait_ge(sq_done, 4 * r + b - 1)
                        pool.wait_ge(acc_done, 4 * r + b - 1 + 1)
                        nc.gpsimd.tensor_tensor(scr[4][:, :], scr[4][:, :], scr[2 + b % 2][:, :],
                                                ALU.add).then_inc(acc_done, 1)
            odd_lows(2, lambda c: scr[c % 2][:, :])

            def ff_up(g, h0):
                with pool.Fori(0, FF_GROUP // 2) as fp:
                    for q in range(2):
                        low(N_FF + 2 * q + 2, h0 + 2 * fp)
                        low(N_FF + 2 * q + 3, h0 + 2 * fp)
                        pool.wait_ge(ff_hi[q], 4 * g + fp + 1)
                        f = bass.ds(2 * fp + q, 1)
                        nc.gpsimd.tensor_tensor(gu_lo[:, f, :], scr[2 + q][:, :].unsqueeze(1), gu_hi[:, f, :].bitcast(f32),
                                                ALU.subtract).then_inc(ff_lo[q], 1)

            with pool.Fori(0, GROUPS - 1) as g:
                ff_up(g, 12 * g)
                with pool.Fori(0, 2) as dp:
                    for b in range(4):
                        low(N_FF + 16 + b + 2, 12 * g + 2 * dp)
            g = GROUPS - 1
            ff_up(g, 12 * g)
            pool.wait_ge(lo_dve, 12)
            nc.gpsimd.memset(scr[4][:, :], 0.0).then_inc(acc_done, 1)
            with pool.Fori(0, 2) as dp:
                for b in range(4):
                    low(N_FF + 16 + b + 2, 12 * g + 2 * dp)
                    pool.wait_ge(sq_done, 8 + 4 * dp + b + 1)
                    pool.wait_ge(acc_done, 10 + 4 * dp + b + 1)
                    nc.gpsimd.tensor_tensor(scr[4][:, :], scr[4][:, :], scr[2 + b % 2][:, :],
                                            ALU.add).then_inc(acc_done, 1)
            pool.wait_ge(block_done, N_IN2)
            nc.gpsimd.memset(acc_q[:, :], 0.0).then_inc(acc_q_done, 1)
            nc.gpsimd.memset(acc_kv[:, :], 0.0).then_inc(acc_kv_done, 1)
            odd_lows(3, lambda c: xs[:, c, :])
            for i in range(Q_TILES + KV_TILES):
                low(N_IN2 + i + 2)
                pool.wait_ge(sq2_done, i + 1)
                acc, done, k = (acc_q, acc_q_done, i) if i < Q_TILES else (acc_kv, acc_kv_done, i - Q_TILES)
                pool.wait_ge(done, k + 1)
                nc.gpsimd.tensor_tensor(acc[:, :], acc[:, :], square2[:, :], ALU.add).then_inc(done, 1)
            for g in range(len(WINDOWS)):
                low(N_POOL + 2 * g + 2)
                low(N_POOL + 2 * g + 3)
                pool.wait_ge(pl_hi, g + 1)
                nc.gpsimd.tensor_tensor(pooled_lo[:, :], scr[3][:, :], pooled_hi[:, :].bitcast(f32),
                                        ALU.subtract).then_inc(pl_lo, 1)
            for h in range(HEADS):
                low(N_GATE + h + 2)
            low(N_KR + 2)
            for i, (hi, lo) in enumerate(latents()):
                if i % 2 == 1:
                    pool.wait_ge(latn_hi, i + 1)
                    nc.gpsimd.tensor_tensor(lo, lat_tile(i), hi.bitcast(f32), ALU.subtract).then_inc(latn_lo_p, 1)
            for n in range(N_UKV, N_BLOCKS):
                low(n + 2)
            for i in range(1, 16, 2):
                pool.wait_ge(z_hi_done, i + 1)
                k = (i // 2 + 4) % 8
                nc.gpsimd.tensor_tensor(z_lo[:, k, :], zin[i % 4][:, :], z_hi[:, k, :].bitcast(f32),
                                        ALU.subtract).then_inc(zp_lo_done, 1)

        @block.scalar
        def _(act):
            def col(c):
                return vec[:, c:c + 1] if isinstance(c, int) else vec[:, bass.ds(c, 1)]

            def high(n, h=0):
                if n >= N_BLOCKS:
                    return
                s = n % 2
                act.wait_ge(w_in_sem[s], 16 * raw_loads(n) + 16 * h)
                if n >= 2:
                    act.wait_ge(block_done, n - 1 + 2 * h)
                nc.scalar.copy(w_hi[s][:, :], w_raw[s][:, :]).then_inc(w_hi_done, 1)

            def highs(src, waits):
                for c in range(KT):
                    act.wait_ge(*waits(c))
                    nc.scalar.copy(h_hi[:, c, :], src(c)).then_inc(hi_done, 1)

            row = 0
            for v in (norm1_g.rearrange("o (c p) -> (o c) p", p=P),
                      lru_conv_w.rearrange("o k (c p) -> (o k c) p", p=P),
                      lru_conv_b.rearrange("o (c p) -> (o c) p", p=P),
                      lru_ba.rearrange("o (c p) -> (o c) p", p=P),
                      lru_bx.rearrange("o (c p) -> (o c) p", p=P),
                      lru_lambda.rearrange("o (c p) -> (o c) p", p=P),
                      sc_conv_w.rearrange("o k (c p) -> (o k c) p", p=P),
                      norm2_g.rearrange("o (c p) -> (o c) p", p=P),
                      final_g.rearrange("(c p) -> c p", p=P),
                      q_norm_g_2.rearrange("(c p) -> c p", p=P),
                      kv_norm_g_2.rearrange("(c p) -> c p", p=P),
                      pool_scale_2.rearrange("(c p) -> c p", p=P)):
                n = v.shape[0]
                act.dma_start(rows0[row:row + n, 0:P], v).then_inc(rows_in, 16)
                row += n
            assert row == V_ROWS
            ffn_rows = ffn_conv_w.rearrange("o k (c p) -> (o k c) p", p=P)
            act.dma_start(rows1[0:72, 0:P], ffn_rows[0:72, :]).then_inc(rows_in, 16)
            act.dma_start(rows2[0:72, 0:P], ffn_rows[72:144, :]).then_inc(rows_in, 16)
            act.dma_start(pos_rows_i[0:NT, :], positions_2.rearrange("o (n p) -> (o n) p", p=P)
                         ).then_inc(rows_in, 16)
            act.dma_start(freq[:, :], rope_freq).then_inc(freq_in, 16)
            def xt_copy(c):
                act.wait_ge(xt_done, c + 1)
                nc.scalar.copy(xs[:, c, :], ps[c % 3][:, :]).then_inc(xt_copied, 1)

            for c in range(6):
                xt_copy(c)
            for n in range(4):
                act.wait_ge(x_in[n], 16)
            for n in range(5, NT):
                if n >= 6:
                    act.wait_ge(sumsq, n - 5)
                nc.scalar.activation(scr[4][:, :], x_tok[:, n, :], ACT.Square,
                                     accum_out=small[:, n:n + 1]).then_inc(sumsq, 1)
            act.wait_ge(sumsq, NT - 5)
            act.wait_ge(sumsq_dve, 5)
            act.wait_ge(const_done, 5)
            nc.scalar.activation(small[:, 8:16], small[:, 0:8], ACT.Sqrt, bias=eps[:, 0:1],
                                 scale=1.0 / D).then_inc(root_done, 1)
            xt_copy(6)
            xt_copy(7)
            act.wait_ge(vec_t, 1)
            nc.scalar.copy(vec[:, :], ps[3][:, 0:V_COLS]).then_inc(vec_done, 1)
            high(0)
            high(1)
            highs(lambda c: scr[c % 2][:, :], lambda c: (v_done, c + 1))
            act.wait_ge(lam_abs, 1)
            nc.scalar.activation(small[:, 24:32], small[:, 16:24], ACT.Exp).then_inc(lam_exp, 1)

            for j in range(SC_TILES):
                act.wait_ge(block_done, read(3 * j))
                if j >= 1:
                    act.wait_ge(sc_p, j)
                nc.scalar.copy(scr[0][:, :], ps[(3 * j) % 4][:, :]).then_inc(sc_c, 1)
                high(3 * j + 2)
                high(3 * j + 3)
                act.wait_ge(sc_p, j + 1)
                if j >= 1:
                    act.wait_ge(sc_y, j)
                nc.scalar.activation(scr[2][:, :], scr[1][:, :], ACT.Identity,
                                     scale=col(V_SCW + 8 + j)).then_inc(sc_base, 1)
                high(3 * j + 4)
                act.wait_ge(sc_y, j + 1)
                nc.scalar.copy(ysc_hi[:, j, :], scr[3][:, :]).then_inc(sc_hi, 1)

            act.wait_ge(params_done, 1)
            act.wait_ge(bd_in, 64)
            act.wait_ge(sc_lo, SC_TILES)
            act.wait_ge(x_parked, 16)

            def conv_first(c, one):
                act.wait_ge(block_done, read(N_LRU, c))
                nc.scalar.activation(xs[:, one, :], ps[0][:, :].unsqueeze(1), ACT.Identity,
                                     scale=col(V_CONVW + 24 + c), bias=col(V_CONVB + c)).then_inc(conv_base, 1)
                high(N_LRU + 2, c)

            def gate_weights(c, one):
                nc.scalar.copy(bd_hi[:, :, :], bd_raw[:, :, one, :].rearrange("p w o n -> p w (o n)")
                               ).then_inc(bd_hi_done, 1)

            def gate_curves(c, one):
                act.wait_ge(ri_done, 2 * c + 1)
                nc.scalar.activation(scr[1][:, :], ps[2][:, :], ACT.Tanh, scale=0.5,
                                     bias=half_ba[:, one]).then_inc(rt_done, 1)
                act.wait_ge(ri_done, 2 * c + 2)
                nc.scalar.activation(scr[2][:, :], ps[3][:, :], ACT.Tanh, scale=0.5,
                                     bias=half_bx[:, one]).then_inc(it_done, 1)
                act.wait_ge(rt_done, c + 1)
                nc.scalar.activation(scr[4][:, :], scr[1][:, :], ACT.Tanh, scale=kh[:, one],
                                     bias=kh[:, one]).then_inc(s_done, 1)
                nc.scalar.activation(scr[3][:, :], scr[1][:, :], ACT.Exp, scale=kx[:, one],
                                     bias=kx[:, one]).then_inc(ex_done, 1)
                act.wait_ge(s_done, c + 1)
                nc.scalar.activation(root[:, :], scr[4][:, :], ACT.Sqrt).then_inc(root_s, 1)

            def gate_gelu(c, one):
                act.wait_ge(conv_done, c + 1)
                act.wait_ge(block_done, read(N_LRU + 1, c))
                high(N_LRU + 3, c)
                nc.scalar.copy(xc_hi[:, :].unsqueeze(1), xs[:, one, :]).then_inc(xc_hi_done, 1)
                if not isinstance(c, int):
                    act.wait_ge(y_done, c)
                nc.scalar.activation(gelu_gate[:, :], ps[1][:, :], ACT.Gelu_apprx_tanh).then_inc(gelu_done, 1)

            first = slice(0, 1)
            conv_first(0, first)
            gate_weights(0, first)
            gate_gelu(0, first)
            with act.Fori(1, LRU_TILES) as c:
                conv_first(c, bass.ds(c, 1))
                gate_curves(c - 1, bass.ds(c - 1, 1))
                gate_weights(c, bass.ds(c, 1))
                gate_gelu(c, bass.ds(c, 1))
            gate_curves(LRU_TILES - 1, slice(LRU_TILES - 1, LRU_TILES))

            act.wait_ge(block_done, N_OUT)
            highs(lambda c: xs[:, c, :], lambda c: (y_done, c + 1))
            with act.Fori(0, 2) as r:
                for b in range(6):
                    act.wait_ge(block_done, read(N_OUT + b, 3 * r))
                    high(N_OUT + b + 2, 3 * r)
                    if b >= 2:
                        act.wait_ge(x1_done, 4 * r + b - 1 + 1)
                        act.wait_ge(acc_done, 4 * r + b - 2 + 1)
                        nc.scalar.activation(scr[2 + b % 2][:, :].unsqueeze(1), xs[:, bass.ds(4 * r + b - 2, 1), :],
                                             ACT.Square).then_inc(sq_done, 1)

            def norm_root(i):
                act.wait_ge(ms_done, i)
                nc.scalar.activation(small[:, 8:16], ps[2][:, 0:NT], ACT.Sqrt, bias=eps[:, 0:1]
                                     ).then_inc(root_done, 1)

            norm_root(1)
            highs(lambda c: scr[c % 2][:, :], lambda c: (v_done, 8 + c + 1))
            act.wait_ge(lo_dve, 12)
            act.wait_ge(lo_pool, 12)

            def ff_up(g, h0):
                with act.Fori(0, FF_GROUP // 2) as fp:
                    for q in range(2):
                        n, h, turn = N_FF + 2 * q, h0 + 2 * fp, 4 * g + fp
                        f = 8 * g + 2 * fp + q
                        act.wait_ge(block_done, read(n, h))
                        act.wait_ge(ff_v[q], turn + 1)
                        nc.scalar.activation(scr[q][:, :], ps[2 * q][:, :], ACT.Identity,
                                             scale=col(V_FFN + 96 + f)).then_inc(ff_base[2 * q], 1)
                        high(n + 2, h)
                        act.wait_ge(block_done, read(n + 1, h))
                        act.wait_ge(ff_lo[q], turn + 1)
                        nc.scalar.activation(scr[2 + q][:, :], ps[2 * q + 1][:, :], ACT.Identity,
                                             scale=col(V_FFN + 96 + 24 + f)).then_inc(ff_base[2 * q + 1], 1)
                        high(n + 3, h)
                        act.wait_ge(ff_conv[2 * q], turn + 1 + 1)
                        nc.scalar.activation(scr[q][:, :], scr[q][:, :], ACT.Gelu_apprx_tanh).then_inc(ff_gelu[q], 1)
                        act.wait_ge(ff_v[q], turn + 1 + 1)
                        nc.scalar.copy(gu_hi[:, bass.ds(2 * fp + q, 1), :], scr[2 + q][:, :].unsqueeze(1)
                                       ).then_inc(ff_hi[q], 1)

            with act.Fori(0, GROUPS - 1) as g:
                ff_up(g, 12 * g)
                with act.Fori(0, 2) as dp:
                    for b in range(4):
                        act.wait_ge(block_done, read(N_FF + 16 + b, 12 * g + 2 * dp))
                        high(N_FF + 16 + b + 2, 12 * g + 2 * dp)
            g = GROUPS - 1
            ff_up(g, 12 * g)
            for q in range(2):
                act.wait_ge(ff_lo[q], 4 * GROUPS + 1)
            with act.Fori(0, 2) as dp:
                for b in range(4):
                    act.wait_ge(block_done, read(N_FF + 16 + b, 12 * g + 2 * dp))
                    high(N_FF + 16 + b + 2, 12 * g + 2 * dp)
                    act.wait_ge(dn_done[b], 2 * g + dp + 1 + 1)
                    act.wait_ge(acc_done, 9 + 4 * dp + b + 1)
                    nc.scalar.activation(scr[2 + b % 2][:, :].unsqueeze(1), xs[:, bass.ds(4 * dp + b, 1), :],
                                         ACT.Square).then_inc(sq_done, 1)
            norm_root(2)
            highs(lambda c: xs[:, c, :], lambda c: (v_done, 16 + c + 1))

            for t in range(NT):
                act.wait_ge(tok_t, t + 1)
                if t >= 2:
                    act.wait_ge(res_parked[t % 2], 16 * (t // 2))
                nc.scalar.mul(scr[t % 2][:, :], ps[2 + t % 2][:, :], ALPHA).then_inc(tok_copied, 1)
                act.wait_ge(tok_copied, t + 1)
                act.dma_start(res_park[t], scr[t % 2][:, :]).then_inc(res_parked[t % 2], 16)
            for i in range(Q_TILES + KV_TILES):
                act.wait_ge(block_done, read(N_IN2 + i))
                high(N_IN2 + i + 2)
                act.wait_ge(lat_done, i + 1)
                if i >= 1:
                    act.wait_ge(acc_q_done if i <= Q_TILES else acc_kv_done,
                                i + 1 if i <= Q_TILES else i - Q_TILES + 1)
                nc.scalar.activation(square2[:, :], lat[:, i, :], ACT.Square).then_inc(sq2_done, 1)
                if i == 2:
                    act.wait_ge(red_done, 2)
                    act.wait_ge(sign_done, 4)
                    nc.scalar.activation(sin_t[:, :], sin_t[:, :], ACT.Sin, scale=sign[:, 0:1]).then_inc(trig_done, 1)
                    nc.scalar.activation(cos_t[:, :], cos_t[:, :], ACT.Sin).then_inc(trig_done, 1)
            act.wait_ge(pw_in, 16)
            act.wait_ge(acc_kv_done, KV_TILES + 1)
            for g in range(len(WINDOWS)):
                act.wait_ge(block_done, read(N_POOL + 2 * g))
                high(N_POOL + 2 * g + 2)
                if g >= 1:
                    act.wait_ge(pool_mm, g)
                nc.scalar.copy(pw_hi[:, :], pw_raw[:, g, :]).then_inc(pw_hi_done, 1)
                act.wait_ge(pl_done, g + 1)
                nc.scalar.copy(pooled_hi[:, :], scr[3][:, :]).then_inc(pl_hi, 1)
                act.wait_ge(block_done, read(N_POOL + 2 * g + 1))
                if g >= 1:
                    act.wait_ge(y_parked, 16 * g)
                nc.scalar.activation(square2[:, :], ps[1][:, :], ACT.Tanh, scale=0.5).then_inc(th_done, 1)
                high(N_POOL + 2 * g + 3)
                act.wait_ge(yb_done, g + 1)
                act.dma_start(y_park[4 + g], square2[:, :]).then_inc(y_parked, 16)
            act.wait_ge(ms2_done, 1)
            nc.scalar.activation(stat[:, 0:16], ps[3][:, 0:16], ACT.Sqrt, bias=eps[:, 0:1]).then_inc(root2_done, 1)
            for h in range(HEADS):
                act.wait_ge(block_done, read(N_GATE + h))
                if h >= 2:
                    act.wait_ge(gate_parked[h % 2], 16 * (h // 2))
                nc.scalar.activation(scr[h % 2][:, :], ps[h % 2][:, :], ACT.Tanh, scale=0.5).then_inc(ga_th, 1)
                high(N_GATE + h + 2)
                act.wait_ge(ga_done, h + 1)
                act.dma_start(gate_park[h], scr[h % 2][:, :]).then_inc(gate_parked[h % 2], 16)
            for q in range(2):
                act.wait_ge(gate_parked[q], 16 * HEADS // 2)

            def swap_halves(r, src):
                if r >= 1:
                    act.wait_ge(rope_v, r)
                for q in range(4):
                    p = q ^ 1
                    nc.scalar.copy(scr[1][32 * q:32 * q + 32, :], src[32 * p:32 * p + 32, :]).then_inc(rope_sw, 1)

            def rope_high(r, dst):
                act.wait_ge(rope_v, r + 1)
                nc.scalar.copy(dst, scr[2][:, :]).then_inc(rope_hi, 1)

            act.wait_ge(block_done, read(N_KR))
            for i, (hi, lo) in enumerate(latents()):
                act.wait_ge(latn_done, i + 1)
                nc.scalar.copy(hi, lat_tile(i)).then_inc(latn_hi, 1)
                if i == 1:
                    high(N_KR + 2)
            swap_halves(0, ps[0])
            rope_high(0, kr_hi[:, :])

            def nope_highs(dsts):
                for s, dst in dsts:
                    nc.scalar.copy(dst, ps[s][:, :]).then_inc(nope_hi, 1)

            act.wait_ge(block_done, read(N_UKV))
            high(N_UKV + 2)
            nope_highs([(h, kn_hi[:, h, :]) for h in range(HEADS)])
            act.wait_ge(block_done, read(N_UKV + 1))
            high(N_UKV + 3)
            act.wait_ge(latn_lo_d, 3)
            act.wait_ge(latn_lo_p, 3)
            for s in range(4):
                nc.scalar.copy(v_hi[:, 2 * s:2 * s + 2, :], ps[s][:, :].rearrange("p (t d) -> p t d", t=2)
                               ).then_inc(nope_hi, 1)
            for b in range(2):
                act.wait_ge(block_done, read(N_UQ + b))
                high(N_UQ + b + 2)
                nope_highs([(2 * b + e, qh_hi[:, 2 * b + e, :]) for e in range(2)])
            act.wait_ge(block_done, read(N_UQ + 2))
            act.wait_ge(y_parked, 16 * 4)
            for r in range(2):
                if r == 0:
                    act.wait_ge(rope_lo, 1)
                swap_halves(r + 1, ps[r])
                rope_high(r + 1, qr_hi[:, r, :])

            for u in range(UNITS + 2):
                if u < UNITS:
                    act.wait_ge(nmax_done, u + 1)
                    nc.scalar.activation(prob[u % 3][:, :], prob[u % 3][:, :], ACT.Exp,
                                         bias=stat[:, 3 + u % 3:4 + u % 3], scale=SCALE,
                                         accum_out=stat[:, 6 + u % 3:7 + u % 3]).then_inc(exp_done, 1)
                if u >= 2:
                    w = u - 2
                    act.wait_ge(pt_done, w + 1)
                    q = (w % 4) * P
                    nc.scalar.copy(pt_hi[:, :, q:q + P], ps[2][:, :].rearrange("p (k q) -> p k q", k=NT)
                                   ).then_inc(pt_hi_done, 1)
            act.wait_ge(pv_done, 2 * HEADS)
            for i in range(16):
                act.wait_ge(z_loaded[i % 4], 16 * (i // 4 + 1))
                k = (i // 2 + 4) % 8
                nc.scalar.copy((wo_hi if i % 2 == 0 else z_hi)[:, k, :], zin[i % 4][:, :]).then_inc(z_hi_done, 1)
            for t in range(NT):
                q = t % 2
                act.wait_ge(ln_mean, t + 1)
                if t >= 1:
                    act.wait_ge(ln_ssq, t)
                nc.scalar.activation(ln_sq[:, :], ln_v[q][:, :], ACT.Square, bias=stat[:, 2 + q:3 + q],
                                     accum_out=stat[:, 4 + q:5 + q]).then_inc(ln_ssq, 1)
                act.wait_ge(ln_ssq, t + 1)
                nc.scalar.activation(stat[:, 6 + q:7 + q], stat[:, 4 + q:5 + q], ACT.Sqrt, scale=1.0 / D,
                                     bias=eps[:, 1:2]).then_inc(ln_root, 1)

        @block.vector
        def _(dve):
            step = Steps(dve, dve_step)
            V = nc.vector
            for free in (x1_done, *ff_conv, *ff_v, *dn_done):
                nc.vector.sem_inc(free, 1)

            def col(c):
                return vec[:, c:c + 1] if isinstance(c, int) else vec[:, bass.ds(c, 1)]

            def norm(i, v0, gain, dst, rb, lo_before):
                def value(c):
                    if c >= 2 and dst(c) is not None and lo_before:
                        if c % 2:
                            dve.wait_ge(lo_pool, 4 * i + (c - 2) // 2 + 1)
                        else:
                            dve.wait_ge(lo_dve, 4 * i + (c - 2) // 2 + 1)
                    if v0 == 0:
                        dve.wait_ge(xt_copied, c + 1)
                    V.scalar_tensor_tensor(out=dst(c), in0=xs[:, c, :], scalar=col(gain + c), in1=rb,
                                           op0=ALU.mult, op1=ALU.mult).then_inc(v_done, 1)

                value(0)
                for c in range(KT):
                    if c + 1 < KT:
                        value(c + 1)
                    if c % 2 == 0:
                        low(i, c, dst(c))

            def low(i, c, src):
                dve.wait_ge(hi_done, 8 * i + c + 1)
                V.tensor_tensor(h_lo[:, c, :], src, h_hi[:, c, :].bitcast(f32), ALU.subtract).then_inc(lo_dve, 1)

            def tap(acc, src, shift, c):
                return V.scalar_tensor_tensor(out=acc[:, shift:SEQ], in0=src[:, 0:SEQ - shift], scalar=col(c),
                                              in1=acc[:, shift:SEQ], op0=ALU.mult, op1=ALU.add)

            for q in range(4):
                V.memset(sign[32 * q:32 * q + 32, :], -1.0 if q % 2 == 0 else 1.0).then_inc(sign_done, 1)
            dve.wait_ge(rows_in, 16 * 15)
            V.tensor_copy(pos_rows[0:NT, :], pos_rows_i[0:NT, :]).then_inc(pos_f_done, 1)
            for n in range(4):
                dve.wait_ge(x_in[n], 16)
            for n in range(5):
                if n >= 1:
                    dve.wait_ge(sumsq_dve, n)
                V.tensor_tensor_reduce(out=square_dve[:, :], in0=x_tok[:, n, :], in1=x_tok[:, n, :], scale=1.0,
                                       scalar=0.0, op0=ALU.mult, op1=ALU.add, accum_out=small[:, n:n + 1]
                                       ).then_inc(sumsq_dve, 1)
            dve.wait_ge(root_done, 1)
            V.reciprocal(rstd[:, :], small[:, 8:16]).then_inc(rstd_done, 1)
            dve.wait_ge(vec_done, 1)
            step(V.scalar_tensor_tensor(out=small[:, 16:24], in0=vec[:, V_LAM:V_LAM + 8], scalar=-1.0,
                                        in1=vec[:, V_LAM:V_LAM + 8], op0=ALU.mult, op1=ALU.min))
            V.tensor_scalar(half_ba[:, :], vec[:, V_BA:V_BA + 8], 0.5, None, ALU.mult).then_inc(lam_abs, 1)
            step(V.tensor_scalar(half_bx[:, :], vec[:, V_BX:V_BX + 8], 0.5, None, ALU.mult))
            step(V.tensor_scalar(half_ps[:, :], vec[:, V_POOL:V_POOL + 4], 0.5, None, ALU.mult))
            dve.wait_ge(rb_done, 1)
            norm(0, 0, V_NORM1, lambda c: scr[c % 2][:, :], ps[3][:, :], True)
            dve.wait_ge(lam_exp, 1)
            e, z, z2, pl = small[:, 24:32], small[:, 32:40], small[:, 40:48], small[:, 16:24]
            step(V.tensor_scalar(z, e, 2.0, None, ALU.add))
            step(V.reciprocal(z2, z))
            step(V.tensor_tensor(z, e, z2, ALU.mult))
            step(V.tensor_tensor(z2, z, z, ALU.mult))
            step(V.tensor_scalar(pl, z2, 1.0 / 15, None, ALU.mult))
            for k in (13, 11, 9, 7, 5, 3):
                step(V.scalar_tensor_tensor(out=pl, in0=pl, scalar=1.0 / k, in1=z2, op0=ALU.add, op1=ALU.mult))
            step(V.scalar_tensor_tensor(out=pl, in0=pl, scalar=1.0, in1=z, op0=ALU.add, op1=ALU.mult))
            step(V.tensor_scalar(z, vec[:, V_LAM:V_LAM + 8], -2.0, 0.0, ALU.mult, ALU.max))
            step(V.scalar_tensor_tensor(out=kh[:, :], in0=pl, scalar=4.0, in1=z, op0=ALU.mult, op1=ALU.add))
            V.tensor_scalar(kx[:, :], kh[:, :], -2.0, None, ALU.mult).then_inc(params_done, 1)

            for j in range(SC_TILES):
                dve.wait_ge(block_done, read(3 * j + 1))
                dve.wait_ge(sc_c, j + 1)
                V.tensor_tensor(scr[1][:, :], ps[(3 * j + 1) % 4][:, :], scr[0][:, :], ALU.mult).then_inc(sc_p, 1)
                dve.wait_ge(sc_base, j + 1)
                step(tap(scr[2], scr[1], 1, V_SCW + 4 + j))
                step(tap(scr[2], scr[1], 2, V_SCW + j))
                dve.wait_ge(block_done, read(3 * j + 2))
                if j >= 1:
                    dve.wait_ge(sc_lo, j)
                V.tensor_tensor(scr[3][:, :], ps[(3 * j + 2) % 4][:, :], scr[2][:, :], ALU.mult).then_inc(sc_y, 1)

            def convolve(c, one):
                xc = xs[:, one, :].rearrange("p o t -> p (o t)")
                dve.wait_ge(conv_base, c + 1)
                step(tap(xc, ps[0], 1, V_CONVW + 16 + c))
                step(tap(xc, ps[0], 2, V_CONVW + 8 + c))
                tap(xc, ps[0], 3, V_CONVW + c).then_inc(conv_done, 1)

            def recur(c, one):
                xc = xs[:, one, :].rearrange("p o t -> p (o t)")
                dve.wait_ge(ex_done, c + 1)
                step(V.tensor_scalar(scr[3][:, :], scr[3][:, :], 0.5, 0.5, ALU.mult, ALU.add))
                step(V.scalar_tensor_tensor(out=scr[1][:, :], in0=scr[4][:, :], scalar=1.0, in1=scr[3][:, :],
                                            op0=ALU.add, op1=ALU.mult))
                step(V.scalar_tensor_tensor(out=scr[1][:, :], in0=scr[1][:, :], scalar=-2.0, in1=scr[3][:, :],
                                            op0=ALU.add, op1=ALU.mult))
                step(V.tensor_scalar(scr[3][:, :], scr[1][:, :], -2.0, -1.0, ALU.mult, ALU.add))
                dve.wait_ge(it_done, c + 1)
                step(V.scalar_tensor_tensor(out=scr[2][:, :], in0=scr[2][:, :], scalar=1.0, in1=xc,
                                            op0=ALU.add, op1=ALU.mult))
                dve.wait_ge(root_s, c + 1)
                step(V.tensor_tensor(root[:, :], scr[1][:, :], root[:, :], ALU.mult))
                step(V.tensor_tensor(root[:, :], root[:, :], scr[2][:, :], ALU.mult))
                step(V.tensor_tensor_scan(xc, scr[3][:, :], root[:, :], 0.0, ALU.mult, ALU.subtract))
                dve.wait_ge(gelu_done, c + 1)
                V.tensor_tensor(xc, xc, gelu_gate[:, :], ALU.mult).then_inc(y_done, 1)

            def second_parts(c, one):
                dve.wait_ge(bd_hi_done, c + 1)
                step(V.tensor_tensor(bd_lo[:, :, :], bd_raw[:, :, one, :].rearrange("p w o n -> p w (o n)"),
                                     bd_hi[:, :, :].bitcast(f32), ALU.subtract))
                dve.wait_ge(xc_hi_done, c + 1)
                V.tensor_tensor(xc_lo[:, :].unsqueeze(1), xs[:, one, :], xc_hi[:, :].bitcast(f32).unsqueeze(1),
                                ALU.subtract).then_inc(xc_lo_done, 1)

            first, last = slice(0, 1), slice(LRU_TILES - 1, LRU_TILES)
            convolve(0, first)
            second_parts(0, first)
            with step.of(11).loop(LRU_TILES - 1) as i:
                c = i + 1
                convolve(c, bass.ds(c, 1))
                recur(i, bass.ds(i, 1))
                second_parts(c, bass.ds(c, 1))
            recur(LRU_TILES - 1, last)

            for c in range(0, KT, 2):
                low(1, c, xs[:, c, :])
            dve.wait_ge(hi_done, 16)
            dve.wait_ge(lo_pool, 8)
            with dve.Fori(0, 2) as r:
                for q in range(4):
                    dve.wait_ge(block_done, read(N_OUT + 2 + q, 3 * r))
                    dve.wait_ge(x_back[q % 2], 32 * r + 16 * (q // 2 + 1))
                    V.tensor_tensor(xs[:, bass.ds(4 * r + q, 1), :], ps[q][:, :].unsqueeze(1), scr[q % 2][:, :].unsqueeze(1),
                                    ALU.add).then_inc(x1_done, 1)

            def norm_scale(i):
                dve.wait_ge(root_done, i + 1)
                V.reciprocal(rstd[:, :], small[:, 8:16]).then_inc(rstd_done, 1)
                dve.wait_ge(rb_done, i + 1)

            norm_scale(1)
            norm(2, 1, V_NORM2, lambda c: scr[c % 2][:, :], ps[3][:, :], True)

            def ff_group(g, h0):
                with step.of(4).loop(FF_GROUP // 2) as fp:
                    for q in range(2):
                        f, turn = 8 * g + 2 * fp + q, 4 * g + fp
                        for part in range(2):
                            s, dst = 2 * q + part, scr[q + 2 * part]
                            dve.wait_ge(ff_base[s], turn + 1)
                            step(tap(dst, ps[s], 1, V_FFN + 48 + 24 * part + f))
                            tap(dst, ps[s], 2, V_FFN + 24 * part + f).then_inc(ff_conv[s], 1)
                        dve.wait_ge(ff_gelu[q], turn + 1)
                        dve.wait_ge(ff_conv[2 * q + 1], turn + 1 + 1)
                        V.tensor_tensor(scr[2 + q][:, :], scr[q][:, :], scr[2 + q][:, :], ALU.mult).then_inc(ff_v[q], 1)
                with dve.Fori(0, 2) as dp:
                    for b in range(4):
                        dve.wait_ge(block_done, read(N_FF + 16 + b, h0 + 2 * dp))
                        d = bass.ds(4 * dp + b, 1)
                        V.tensor_tensor(xs[:, d, :], ps[b][:, :].unsqueeze(1), xs[:, d, :], ALU.add).then_inc(dn_done[b], 1)

            with step.of(16).loop(GROUPS) as g:
                ff_group(g, 12 * g)

            norm_scale(2)
            norm(3, 2, V_FINAL, lambda c: xs[:, c, :], ps[3][:, :], False)

            dve.wait_ge(block_done, N_IN2)
            for i in range(Q_TILES + KV_TILES):
                dve.wait_ge(block_done, read(N_IN2 + i))
                V.tensor_copy(lat[:, i, :], ps[i % 2][:, :]).then_inc(lat_done, 1)
                if i == 0:
                    dve.wait_ge(pos_in, 16)
                    dve.wait_ge(freq_in, 16)
                    step(V.tensor_copy(pos_f[:, :], pos_i[:, :]))
                    step(V.tensor_scalar(scr[2][:, :], pos_f[:, :], freq[:, 0:1], None, ALU.mult))
                if i in (0, 1):
                    t = (sin_t, cos_t)[i]
                    step(V.tensor_scalar(scr[3][:, :], scr[2][:, :], float(1 / (2 * np.pi)), 0.25 * i,
                                         ALU.mult, ALU.add))
                    step(V.tensor_scalar(scr[3][:, :], scr[3][:, :], ROUND, None, ALU.add))
                    step(V.tensor_scalar(scr[3][:, :], scr[3][:, :], ROUND, None, ALU.subtract))
                    src = scr[2]
                    for part in (TWO_PI_A, TWO_PI_B, TWO_PI_C):
                        step(V.scalar_tensor_tensor(out=t[:, :], in0=scr[3][:, :], scalar=-part, in1=src[:, :],
                                                    op0=ALU.mult, op1=ALU.add))
                        src = t
                    step(V.tensor_scalar(t[:, :], t[:, :], float(np.pi / 2) * i, 3.1415925, ALU.add, ALU.min))
                    V.tensor_scalar(t[:, :], t[:, :], -3.1415925, None, ALU.max).then_inc(red_done, 1)

            for q in range(2):
                dve.wait_ge(res_parked[q], 16 * NT // 2)
            for g, w in enumerate(WINDOWS):
                dve.wait_ge(block_done, read(N_POOL + 2 * g))
                V.tensor_copy(scr[0][:, :], ps[0][:, :]).then_inc(u_done, 1)
                dve.wait_ge(u_done, g + 1)
                src, shift, k = scr[0], 1, 0
                while shift < w:
                    dst = scr[1 + k % 2]
                    step(V.tensor_tensor(dst[:, shift:SEQ], src[:, shift:SEQ], src[:, 0:SEQ - shift], ALU.add))
                    step(V.tensor_copy(dst[:, 0:shift], src[:, 0:shift]))
                    src, shift, k = dst, 2 * shift, k + 1
                if g >= 1:
                    dve.wait_ge(pl_lo, g)
                step(V.scalar_tensor_tensor(out=scr[3][:, :], in0=src[:, :], scalar=1.0 / w, in1=scr[0][:, :],
                                            op0=ALU.mult, op1=ALU.subtract))
                if g == 0:
                    dve.wait_ge(const_done, 21)
                step(V.tensor_tensor(small[:, 16:16 + w - 1], src[:, 0:w - 1], rc[:, 0:w - 1], ALU.mult))
                V.tensor_tensor(scr[3][:, 0:w - 1], small[:, 16:16 + w - 1], scr[0][:, 0:w - 1],
                                ALU.subtract).then_inc(pl_done, 1)
                dve.wait_ge(pw_hi_done, g + 1)
                step(V.tensor_tensor(pw_lo[:, :], pw_raw[:, g, :], pw_hi[:, :].bitcast(f32), ALU.subtract))
                dve.wait_ge(th_done, g + 1)
                V.scalar_tensor_tensor(out=square2[:, :], in0=square2[:, :], scalar=1.0, in1=ps[1][:, :],
                                       op0=ALU.add, op1=ALU.mult).then_inc(gb_done, 1)
                dve.wait_ge(gb_done, g + 1)
                dve.wait_ge(pool_mm, g + 1)
                V.scalar_tensor_tensor(out=square2[:, :], in0=ps[2][:, :], scalar=half_ps[:, g:g + 1],
                                       in1=square2[:, :], op0=ALU.mult, op1=ALU.mult).then_inc(yb_done, 1)
            dve.wait_ge(root2_done, 1)
            V.reciprocal(stat[:, 0:16], stat[:, 0:16]).then_inc(rstd2_done, 1)

            def gate(h):
                dve.wait_ge(ga_th, h + 1)
                V.scalar_tensor_tensor(out=scr[h % 2][:, :], in0=scr[h % 2][:, :], scalar=1.0, in1=ps[h % 2][:, :],
                                       op0=ALU.add, op1=ALU.mult).then_inc(ga_done, 1)

            gate(0)
            dve.wait_ge(rb2_done, 1)
            for i in range(KV_TILES + Q_TILES):
                kv = i < KV_TILES
                V.scalar_tensor_tensor(out=lat_tile(i), in0=lat_tile(i),
                                       scalar=col(V_KVN + i if kv else V_QN + i - KV_TILES),
                                       in1=ps[3 if kv else 2][:, :], op0=ALU.mult, op1=ALU.mult).then_inc(latn_done, 1)
                if i == 2:
                    gate(1)
            gate(2)
            gate(3)

            def latent_low(i):
                hi, lo = latents()[i]
                dve.wait_ge(latn_hi, i + 1)
                V.tensor_tensor(lo, lat_tile(i), hi.bitcast(f32), ALU.subtract).then_inc(latn_lo_d, 1)

            def rotate(r, src, hi, lo):
                dve.wait_ge(rope_sw, 4 * r + 4)
                V.tensor_tensor(scr[0][:, :], src[:, :], cos_t[:, :], ALU.mult).then_inc(rope_a, 1)
                step(V.tensor_tensor(scr[1][:, :], scr[1][:, :], sin_t[:, :], ALU.mult))
                dve.wait_ge(rope_a, r + 1)
                V.tensor_tensor(scr[2][:, :], scr[0][:, :], scr[1][:, :], ALU.add).then_inc(rope_v, 1)
                dve.wait_ge(rope_hi, r + 1)
                V.tensor_tensor(lo, scr[2][:, :], hi.bitcast(f32), ALU.subtract).then_inc(rope_lo, 1)

            def nope_lows(first, items):
                for i, (s, hi, lo) in enumerate(items):
                    dve.wait_ge(nope_hi, first + i + 1)
                    V.tensor_tensor(lo, s, hi.bitcast(f32), ALU.subtract).then_inc(nope_lo, 1)

            dve.wait_ge(trig_done, 2)
            for i in (0, 2, 4):
                latent_low(i)
            rotate(0, ps[0], kr_hi[:, :], kr_lo[:, :])
            nope_lows(0, [(ps[h][:, :], kn_hi[:, h, :], kn_lo[:, h, :]) for h in range(HEADS)])
            nope_lows(4, [(ps[s][:, :].rearrange("p (t d) -> p t d", t=2), v_hi[:, 2 * s:2 * s + 2, :],
                           v_lo[:, 2 * s:2 * s + 2, :]) for s in range(4)])
            nope_lows(8, [(ps[h][:, :], qh_hi[:, h, :], qh_lo[:, h, :]) for h in range(HEADS)])
            for r in range(2):
                rotate(r + 1, ps[r], qr_hi[:, r, :], qr_lo[:, r, :])

            def masks(u):
                if u < UNITS:
                    if u >= 2:
                        dve.wait_ge(smax_done, u - 1)
                    V.tensor_scalar(mask[u % 2][:, :], pos_f[:, :], col(V_POS + u % NT), MASKED, ALU.is_gt,
                                    ALU.mult).then_inc(mask_done, 1)

            masks(0)
            for u in range(UNITS + 3):
                masks(u + 1)
                if u < UNITS:
                    s = u % 3
                    dve.wait_ge(score_done, u + 1)
                    dve.wait_ge(mask_done, u + 1)
                    if u >= 3:
                        dve.wait_ge(pt_done, u - 2)
                    V.tensor_tensor_reduce(out=prob[s][:, :], in0=ps[u % 2][:, :], in1=mask[u % 2][:, :],
                                           scale=1.0, scalar=-3.0e38, op0=ALU.add, op1=ALU.max,
                                           accum_out=stat[:, s:s + 1]).then_inc(smax_done, 1)
                    dve.wait_ge(smax_done, u + 1)
                    V.tensor_scalar(stat[:, 3 + s:4 + s], stat[:, s:s + 1], -SCALE, None, ALU.mult
                                    ).then_inc(nmax_done, 1)
                if 1 <= u <= UNITS:
                    s = (u - 1) % 3
                    dve.wait_ge(exp_done, u)
                    step(V.reciprocal(stat[:, 9 + s:10 + s], stat[:, 6 + s:7 + s]))
                    V.tensor_scalar(prob[s][:, :], prob[s][:, :], stat[:, 9 + s:10 + s], None, ALU.mult
                                    ).then_inc(p_done, 1)
                if 2 <= u <= UNITS + 1:
                    w = u - 2
                    q = (w % 4) * P
                    dve.wait_ge(pt_hi_done, w + 1)
                    V.tensor_tensor(pt_lo[:, :, q:q + P], ps[2][:, :].rearrange("p (k q) -> p k q", k=NT),
                                    pt_hi[:, :, q:q + P].bitcast(f32), ALU.subtract).then_inc(pt_lo_done, 1)
                if u >= 6 and (u - 2) % 4 == 0:
                    i = (u - 2) // 4 - 1
                    dve.wait_ge(pv_done, i + 1)
                    dve.wait_ge(gate_back[i % 2], 16 * (i // 2 + 1))
                    if i >= 2:
                        dve.wait_ge(ya_parked[i % 2], 16 * (i // 2))
                    V.scalar_tensor_tensor(out=ya_out[i % 2][:, :], in0=ps[3][:, (i % 2) * HALF:(i % 2 + 1) * HALF],
                                           scalar=0.5, in1=gate_in[i % 2][:, :], op0=ALU.mult, op1=ALU.mult
                                           ).then_inc(ya_done, 1)
            for i in range(0, 16, 2):
                dve.wait_ge(z_hi_done, i + 1)
                k = (i // 2 + 4) % 8
                V.tensor_tensor(wo_lo[:, k, :], zin[i % 4][:, :], wo_hi[:, k, :].bitcast(f32),
                                ALU.subtract).then_inc(z_lo_done, 1)
            dve.wait_ge(res_back, 16)
            dve.wait_ge(ln_in, 32)

            def ln_first(t):
                q = t % 2
                dve.wait_ge(mix_done, t + 1)
                if t >= 2:
                    dve.wait_ge(stored[q], 16 * (t // 2))
                V.scalar_tensor_tensor(out=ln_v[q][:, :], in0=ps[t % 4][:, :], scalar=1.0, in1=resid[:, t, :],
                                       op0=ALU.mult, op1=ALU.add, accum_out=stat[:, q:q + 1]).then_inc(ln_sum, 1)
                dve.wait_ge(ln_sum, t + 1)
                V.tensor_scalar(stat[:, 2 + q:3 + q], stat[:, q:q + 1], -1.0 / D, None, ALU.mult).then_inc(ln_mean, 1)

            ln_first(0)
            for t in range(NT):
                q = t % 2
                if t + 1 < NT:
                    ln_first(t + 1)
                dve.wait_ge(ln_root, t + 1)
                step(V.reciprocal(stat[:, 8 + q:9 + q], stat[:, 6 + q:7 + q]))
                step(V.tensor_scalar(ln_v[q][:, :], ln_v[q][:, :], stat[:, 2 + q:3 + q], stat[:, 8 + q:9 + q],
                                     ALU.add, ALU.mult))
                step(V.tensor_tensor(ln_v[q][:, :], ln_v[q][:, :], ln_g[:, :], ALU.mult))
                V.tensor_tensor(ln_v[q][:, :], ln_v[q][:, :], ln_b[:, :], ALU.add).then_inc(ln_out, 1)

        @block.tensor
        def _(pe):
            def blocked(n):
                return [w[n % 2][:, :].rearrange("p (k n) -> p k n", n=P) for w in (w_hi, w_lo)]

            def project(n, h, dst, x_h, x_l):
                pe.wait_ge(w_lo_done, n + 1 + 2 * h)
                wh, wl = blocked(n)
                for k in range(8):
                    mm = matmul3(pe, dst, wh[:, k, :], wl[:, k, :], x_h[:, k, :], x_l[:, k, :], k == 0, k == 7)
                mm.then_inc(block_done, 1)

            def mean_squares(acc, dst, which):
                for t in range(NT):
                    mm = nc.tensor.matmul(dst[:, t:t + 1], acc[:, t * P:(t + 1) * P], meanw[:, which:which + 1],
                                          start=True, stop=True)
                return mm

            def spread(scale, dst):
                for t in range(NT):
                    mm = nc.tensor.matmul(dst[:, t * P:(t + 1) * P], scale[:, t:t + 1].to_broadcast([P, P]),
                                          ident[:, :], start=True, stop=True)
                return mm

            pe.wait_ge(ident_done, 1)
            for c in range(KT):
                if c % 2 == 0:
                    pe.wait_ge(x_in[c // 2], 16)
                if c >= 3:
                    pe.wait_ge(xt_copied, c - 2)
                for t in range(NT):
                    mm = nc.tensor.transpose(ps[c % 3][:, t * P:(t + 1) * P], x_tok[:, t, c * P:(c + 1) * P], ident[:, :])
                mm.then_inc(xt_done, 1)
            pe.wait_ge(rows_in, 16 * 15)
            pe.wait_ge(pos_f_done, 1)
            for src, n, c in ((rows0, V_ROWS, 0), (rows1, 72, V_FFN), (rows2, 72, V_FFN + 72), (pos_rows, NT, V_POS)):
                mm = nc.tensor.transpose(ps[3][:, c:c + n], src[0:n, 0:P], ident[0:n, 0:n])
            mm.then_inc(vec_t, 1)
            pe.wait_ge(rstd_done, 1)
            pe.wait_ge(vec_done, 1)
            spread(rstd, ps[3]).then_inc(rb_done, 1)

            def input_ready(i):
                pe.wait_ge(lo_dve, 4 * (i + 1))
                pe.wait_ge(lo_pool, 4 * (i + 1))

            def first_two(n, dsts, i):
                for k in range(8 + 3):
                    for b, j in ((0, k), (1, k - 3)):
                        if not 0 <= j < 8:
                            continue
                        if j == 0:
                            pe.wait_ge(w_lo_done, n + b + 1)
                        if b == 0:
                            pe.wait_ge(lo_dve if j % 2 == 0 else lo_pool, 4 * i + j // 2 + 1)
                        wh, wl = blocked(n + b)
                        mm = matmul3(pe, dsts[b], wh[:, j, :], wl[:, j, :], h_hi[:, j, :], h_lo[:, j, :], j == 0, j == 7)
                        if j == 7:
                            mm.then_inc(block_done, 1)

            pe.wait_ge(xt_copied, KT)
            first_two(0, (ps[0], ps[1]), 0)
            readers = (sc_c, sc_p, sc_y)
            for n in range(2, 3 * SC_TILES):
                if n == 3:
                    pe.wait_ge(v_done, 8)
                if n >= 4:
                    m = n - 4
                    pe.wait_ge(readers[m % 3], m // 3 + 1)
                project(n, 0, ps[n % 4], h_hi, h_lo)
            def gates():
                matmul3(pe, ps[2], bd_hi[:, 0, :], bd_lo[:, 0, :], xc_hi, xc_lo, True, True).then_inc(ri_done, 1)
                matmul3(pe, ps[3], bd_hi[:, 1, :], bd_lo[:, 1, :], xc_hi, xc_lo, True, True).then_inc(ri_done, 1)

            pe.wait_ge(sc_y, 3)
            project(N_LRU, 0, ps[0], h_hi, h_lo)
            pe.wait_ge(sc_c, 4)
            project(N_LRU + 1, 0, ps[1], h_hi, h_lo)
            pe.wait_ge(sc_y, 4)
            with pe.Fori(1, LRU_TILES) as c:
                pe.wait_ge(conv_done, c)
                project(N_LRU, c, ps[0], h_hi, h_lo)
                pe.wait_ge(xc_lo_done, c)
                gates()
                pe.wait_ge(gelu_done, c)
                project(N_LRU + 1, c, ps[1], h_hi, h_lo)
            pe.wait_ge(xc_lo_done, LRU_TILES)
            gates()
            pe.wait_ge(conv_done, LRU_TILES)
            pe.wait_ge(gelu_done, LRU_TILES)
            pe.wait_ge(sc_lo, SC_TILES)
            with pe.Fori(0, 2) as r:
                for b in range(6):
                    n = N_OUT + b
                    if b < 2:
                        if b == 1:
                            pe.wait_ge(it_done, LRU_TILES)
                        pe.wait_ge(x1_done, 2 * (b + 1) * r + 1)
                        pe.wait_ge(w_lo_done, n + 1 + 6 * r)
                        wh, wl = [w[n % 2][:, :].rearrange("p (k e n) -> p k e n", k=4, e=2) for w in (w_hi, w_lo)]
                        for e in range(2):
                            for k in range(4):
                                mm = matmul3(pe, ps[2 * b + e], wh[:, k, e, :], wl[:, k, e, :], ysc_hi[:, k, :],
                                             ysc_lo[:, k, :], k == 0, False)
                        mm.then_inc(block_done, 1)
                    else:
                        if b == 2:
                            input_ready(1)
                        pe.wait_ge(w_lo_done, n + 1 + 6 * r)
                        wh, wl = blocked(n)
                        for k in range(8):
                            mm = matmul3(pe, ps[b - 2], wh[:, k, :], wl[:, k, :], h_hi[:, k, :], h_lo[:, k, :],
                                         False, k == 7)
                        mm.then_inc(block_done, 1)

            def norm(i, acc_value):
                pe.wait_ge(acc_done, acc_value)
                mean_squares(scr[4], ps[2], 0).then_inc(ms_done, 1)
                pe.wait_ge(rstd_done, i + 1)
                spread(rstd, ps[3]).then_inc(rb_done, 1)

            norm(1, 10)
            def ff_up(g, fp, blocks):
                for b in blocks:
                    pe.wait_ge(ff_conv[b], 4 * g + fp + 1)
                    pe.wait_ge(dn_done[b], 2 * g + 1)
                    project(N_FF + b, 12 * g + 2 * fp, ps[b], h_hi, h_lo)

            def ff_down(g):
                with pe.Fori(0, 2) as dp:
                    for pair in range(2):
                        d0, d1 = 2 * pair, 2 * pair + 1
                        for b, ks in ((d0, range(7)), (d1, range(4)), (d0, range(7, 8)), (d1, range(4, 8))):
                            n = N_FF + 2 * FF_GROUP + b
                            if ks[0] == 0:
                                pe.wait_ge(ff_conv[b], 4 * g + 4 + 1)
                                pe.wait_ge(dn_done[b], 2 * g + dp + 1)
                                pe.wait_ge(w_lo_done, n + 1 + 24 * g + 4 * dp)
                                pe.wait_ge(ff_lo[0], 4 * g + 4 + 1)
                                pe.wait_ge(ff_lo[1], 4 * g + 3 + 1)
                            elif ks[0] == 7:
                                pe.wait_ge(ff_lo[1], 4 * g + 4 + 1)
                            wh, wl = blocked(n)
                            for k in ks:
                                mm = matmul3(pe, ps[b], wh[:, k, :], wl[:, k, :], gu_hi[:, k, :], gu_lo[:, k, :],
                                             k == 0, k == 7)
                            if ks[-1] == 7:
                                mm.then_inc(block_done, 1)

            first_two(N_FF, (ps[0], ps[1]), 2)
            pe.wait_ge(v_done, 16)
            ff_up(0, 0, (2, 3))
            with pe.Fori(1, FF_GROUP // 2) as fp:
                ff_up(0, fp, range(4))
            ff_down(0)
            with pe.Fori(1, GROUPS) as g:
                with pe.Fori(0, FF_GROUP // 2) as fp:
                    ff_up(g, fp, range(4))
                ff_down(g)
            norm(2, 19)
            pe.wait_ge(v_done, 24)
            for t in range(NT):
                if t >= 2:
                    pe.wait_ge(tok_copied, t - 1)
                for k in range(KT):
                    mm = nc.tensor.transpose(ps[2 + t % 2][:, k * P:(k + 1) * P], xs[:, k, t * P:(t + 1) * P], ident[:, :])
                mm.then_inc(tok_t, 1)
            input_ready(3)
            for i in range(Q_TILES + KV_TILES):
                if i >= 2:
                    pe.wait_ge(lat_done, i - 1)
                project(N_IN2 + i, 0, ps[i % 2], h_hi, h_lo)
            pe.wait_ge(tok_copied, NT)
            with pe.Fori(0, len(WINDOWS)) as g:
                pe.wait_ge(lat_done, 5)
                pe.wait_ge(u_done, g)
                project(N_POOL, g, ps[0], h_hi, h_lo)
                pe.wait_ge(lat_done, 6)
                pe.wait_ge(gb_done, g)
                project(N_POOL + 1, g, ps[1], h_hi, h_lo)
                pe.wait_ge(yb_done, g)
                pe.wait_ge(pl_lo, g + 1)
                pe.wait_ge(gb_done, g + 1)
                matmul3(pe, ps[2], pw_hi[:, :], pw_lo[:, :], pooled_hi, pooled_lo, True, True).then_inc(pool_mm, 1)
            pe.wait_ge(acc_q_done, Q_TILES + 1)
            pe.wait_ge(acc_kv_done, KV_TILES + 1)
            mean_squares(acc_q, ps[3][:, 0:8], 1)
            mean_squares(acc_kv, ps[3][:, 8:16], 2).then_inc(ms2_done, 1)
            for h in range(HEADS):
                if h < 2:
                    pe.wait_ge((u_done, gb_done)[h], 4)
                else:
                    pe.wait_ge(ga_done, h - 1)
                project(N_GATE + h, 0, ps[h % 2], h_hi, h_lo)
                if h == 0:
                    pe.wait_ge(rstd2_done, 1)
                    pe.wait_ge(yb_done, 4)
                    spread(stat[:, 0:8], ps[2])
                    spread(stat[:, 8:16], ps[3]).then_inc(rb2_done, 1)
            pe.wait_ge(ga_done, 3)
            project(N_KR, 0, ps[0], h_hi, h_lo)
            n = N_UKV
            pe.wait_ge(w_lo_done, n + 1)
            pe.wait_ge(latn_lo_d, 1)
            pe.wait_ge(latn_lo_p, 1)
            pe.wait_ge(latn_done, KV_TILES + Q_TILES)
            pe.wait_ge(ga_done, 4)
            wh, wl = [w[n % 2][:, :].rearrange("p (k h n) -> p k h n", k=2, h=HEADS) for w in (w_hi, w_lo)]
            for h in (1, 2, 3, 0):
                if h == 0:
                    pe.wait_ge(rope_a, 1)
                for k in range(2):
                    mm = matmul3(pe, ps[h], wh[:, k, h, :], wl[:, k, h, :], kvn_hi[:, k, :], kvn_lo[:, k, :],
                                 k == 0, k == 1)
            mm.then_inc(block_done, 1)
            n = N_UKV + 1
            pe.wait_ge(w_lo_done, n + 1)
            wh, wl = [w[n % 2][:, :].rearrange("p (k n) -> p k n", k=2) for w in (w_hi, w_lo)]
            for t in range(NT):
                if t % 2 == 0:
                    pe.wait_ge(nope_lo, t // 2 + 1)
                dst = ps[t // 2][:, (t % 2) * HALF:(t % 2 + 1) * HALF]
                cols_t = slice(t * P, (t + 1) * P)
                for k in range(2):
                    for a, b, first, last in ((kvn_hi, wh, k == 0, False), (kvn_hi, wl, False, False),
                                              (kvn_lo, wh, False, k == 1)):
                        mm = nc.tensor.matmul(dst, a[:, k, cols_t], b[:, k, :], start=first, stop=last)
            mm.then_inc(block_done, 1)
            pe.wait_ge(latn_lo_d, 3)
            pe.wait_ge(latn_lo_p, 3)
            for b in range(3):
                n = N_UQ + b
                pe.wait_ge(w_lo_done, n + 1)
                if b < 2:
                    pe.wait_ge(nope_lo, 4 + 2 * b + 2)
                else:
                    pe.wait_ge(nope_lo, 10)
                wh, wl = [w[n % 2][:, :].rearrange("p (k e n) -> p k e n", k=4, e=2) for w in (w_hi, w_lo)]
                for e in range(2):
                    for k in range(4):
                        mm = matmul3(pe, ps[(2 * b + e) % 4], wh[:, k, e, :], wl[:, k, e, :], qn_hi[:, k, :],
                                     qn_lo[:, k, :], k == 0, k == 3)
                mm.then_inc(block_done, 1)

            def scores(u):
                h, t = u // NT, slice((u % NT) * P, (u % NT + 1) * P)
                r = slice(64 * (h % 2), 64 * (h % 2) + 64)
                for half in range(2):
                    keys = slice(half * HALF, (half + 1) * HALF)
                    dst = ps[u % 2][:, keys]
                    for i, (q, k) in enumerate(((qh_hi, kn_hi), (qh_hi, kn_lo), (qh_lo, kn_hi))):
                        nc.tensor.matmul(dst, q[:, h, t], k[:, h, keys], start=i == 0, stop=False)
                    for i, (q, k) in enumerate(((qr_hi, kr_hi), (qr_hi, kr_lo), (qr_lo, kr_hi))):
                        mm = nc.tensor.matmul(dst, q[r, h // 2, t], k[r, keys], start=False, stop=i == 2)
                mm.then_inc(score_done, 1)

            def weigh(i):
                h = i // 2
                dst = ps[3][:, (i % 2) * HALF:(i % 2 + 1) * HALF]
                d = slice(h * VDIM, (h + 1) * VDIM)
                for k in range(NT):
                    for a, b, first, last in ((v_hi, pt_hi, k == 0, False), (v_hi, pt_lo, False, False),
                                              (v_lo, pt_hi, False, k == NT - 1)):
                        mm = nc.tensor.matmul(dst, a[:, k, d], b[:, k, :], start=first, stop=last)
                mm.then_inc(pv_done, 1)

            pe.wait_ge(nope_lo, 12)
            pe.wait_ge(rope_lo, 3)
            for u in range(UNITS + 3):
                if u < UNITS:
                    if u >= 2:
                        pe.wait_ge(smax_done, u - 1)
                    scores(u)
                if u >= 6 and (u - 2) % 4 == 0:
                    i = (u - 2) // 4 - 1
                    pe.wait_ge(pt_lo_done, 4 * (i + 1))
                    if i >= 2:
                        pe.wait_ge(ya_done, i - 1)
                    weigh(i)
                if 2 <= u <= UNITS + 1:
                    w = u - 2
                    pe.wait_ge(p_done, w + 1)
                    if w >= 1:
                        pe.wait_ge(pt_lo_done, w)
                    for k in range(NT):
                        mm = nc.tensor.transpose(ps[2][:, k * P:(k + 1) * P], prob[w % 3][:, k * P:(k + 1) * P], ident[:, :])
                    mm.then_inc(pt_done, 1)
            for t in range(NT):
                cols_t = slice(t * P, (t + 1) * P)
                if t == 3:
                    pe.wait_ge(ya_done, 2 * HEADS)
                if t >= 4:
                    pe.wait_ge(ln_sum, t - 3)
                for j in range(KT):
                    k = (j + 4) % 8
                    if t == 0:
                        pe.wait_ge(z_lo_done, j + 1)
                        pe.wait_ge(zp_lo_done, j + 1)
                    for a, b, first, last in ((z_hi, wo_hi, j == 0, False), (z_hi, wo_lo, False, False),
                                              (z_lo, wo_hi, False, j == KT - 1)):
                        for half in range(2):
                            c = slice(half * HALF, (half + 1) * HALF)
                            mm = nc.tensor.matmul(ps[t % 4][:, c], a[:, k, cols_t], b[:, k, c], start=first, stop=last)
                mm.then_inc(mix_done, 1)


_INS = ["x", "norm1_g", "w_in", "lru_conv_w", "lru_conv_b", "lru_wa", "lru_ba", "lru_wx", "lru_bx", "lru_lambda",
        "sc_conv_w", "w_out", "norm2_g", "w_up", "ffn_conv_w", "w_down", "final_g", "positions_2", "w_in_2",
        "q_norm_g_2", "w_uq_2", "kv_norm_g_2", "w_ukv_2", "pool_w_2", "pool_scale_2", "w_out_2", "ln_g_2", "ln_b_2"]


def kernel(**inputs):
    import numpy as _np
    import concourse.bacc as _bacc
    from concourse import mybir as _mybir
    from concourse.bass_utils import run_bass_kernel_spmd as _run

    nc = _bacc.Bacc("TRN2", target_bir_lowering=False, num_devices=1)
    arrays = {name: _np.ascontiguousarray(inputs[name]) for name in _INS}
    half = ROPE // 2
    one = _np.float32(10000.0) ** (-_np.arange(half, dtype=_np.float32) / _np.float32(half))
    arrays["rope_freq"] = _np.tile(one.astype(_np.float32), P // half).reshape(P, 1)
    args = [nc.dram_tensor(f"in_{name}", a.shape, _mybir.dt.from_np(a.dtype), kind="ExternalInput").ap()
            for name, a in arrays.items()]
    out = nc.dram_tensor("out", (1, SEQ, D), _mybir.dt.float32, kind="ExternalOutput").ap()
    program(nc, *args, out)
    r = _run(nc, [{f"in_{name}": a for name, a in arrays.items()}], core_ids=[0])
    return r.results[0]["out"]
```

```python
from contextlib import ExitStack, contextmanager

import numpy as np
import concourse.bass as bass
from concourse import mybir

P = 128
SEQ = 1024
D = 1024
KT = D // P
NT = SEQ // P
LRU_TILES = 8
SC_TILES = 4
FF_TILES = 24
FF_GROUP = 8
GROUPS = FF_TILES // FF_GROUP
HEADS = 4
NOPE, ROPE, VDIM = 128, 64, 128
QK = NOPE + ROPE
Q_TILES, KV_TILES = 4, 2
HALF = 512
EPS = 1e-6
LN_EPS = 1e-5
ALPHA = 2.0 ** 0.25
SCALE = float(QK) ** -0.5
MASKED = -1.0e30
WINDOWS = (2, 4, 8, 16)
TILE = SEQ * 4

V_NORM1, V_CONVW, V_CONVB, V_BA, V_BX, V_LAM = 0, 8, 40, 48, 56, 64
V_SCW, V_NORM2, V_FINAL, V_QN, V_KVN, V_POOL = 72, 84, 92, 100, 104, 106
V_ROWS = 110
FFN_ROWS = 144
V_FFN = V_ROWS
V_POS = V_FFN + FFN_ROWS
V_COLS = V_POS + NT

N_SC = 0
N_LRU = N_SC + 3 * SC_TILES
N_OUT = N_LRU + 2 * LRU_TILES
N_FF = N_OUT + 12
GROUP_BLOCKS = 2 * FF_GROUP + KT
N_IN2 = N_FF + GROUPS * GROUP_BLOCKS
N_POOL = N_IN2 + Q_TILES + KV_TILES
N_GATE = N_POOL + 2 * len(WINDOWS)
N_KR = N_GATE + HEADS
N_UQ = N_KR + 1
N_UKV = N_UQ + 3
N_BLOCKS = N_UKV + 2

UNITS = HEADS * NT

TWO_PI_A = 6.28125
TWO_PI_B = float(np.float32(np.floor((2 * np.pi - 6.28125) * 2 ** 20) / 2 ** 20))
TWO_PI_C = float(np.float32(2 * np.pi - 6.28125 - TWO_PI_B))
ROUND = 12582912.0


class Steps:

    def __init__(self, eng, sem):
        self.eng, self.sem, self.n, self.run = eng, sem, 0, 0

    def __call__(self, instruction):
        instruction.then_inc(self.sem, 1)
        self.n += 1
        self.eng.wait_ge(self.sem, self.n + self.run)

    @contextmanager
    def loop(self, count):
        start, outer, per = self.n, self.run, self.per
        with self.eng.Fori(0, count) as i:
            self.run = outer + i * per
            yield i
        assert self.n == start + per, (self.n - start, per)
        self.n, self.run = start + per * count, outer

    def of(self, per):
        self.per = per
        return self


def program(nc, x, norm1_g, w_in, lru_conv_w, lru_conv_b, lru_wa, lru_ba, lru_wx, lru_bx, lru_lambda,
            sc_conv_w, w_out, norm2_g, w_up, ffn_conv_w, w_down, final_g, positions_2, w_in_2,
            q_norm_g_2, w_uq_2, kv_norm_g_2, w_ukv_2, pool_w_2, pool_scale_2, w_out_2, ln_g_2,
            ln_b_2, rope_freq, out):
    f32, f32r, i32 = mybir.dt.float32, mybir.dt.float32r, mybir.dt.int32
    ALU, ACT = mybir.AluOpType, mybir.ActivationFunctionType
    ctx = ExitStack()
    with ctx:
        base = (nc.sbuf_base + 31) // 32 * 32
        W0, H0 = base, base + 6 * TILE
        X0 = H0 + 16 * TILE
        G0 = X0 + 8 * TILE
        S0 = G0 + 16 * TILE
        C0 = S0 + 5 * TILE

        def at(name, offset, shape, dt=f32):
            return nc.alloc_sbuf_tensor_at(name, [P] + list(shape), dt, offset=offset)

        def tile(name, offset, n, dt=f32, count=None):
            return at(name, offset + n * TILE, [SEQ] if count is None else [count, SEQ], dt)

        w_raw = [tile(f"w_raw{s}", W0, s) for s in range(2)]
        w_hi = [tile(f"w_hi{s}", W0, 2 + s, f32r) for s in range(2)]
        w_lo = [tile(f"w_lo{s}", W0, 4 + s, f32r) for s in range(2)]
        h_hi = tile("h_hi", H0, 0, f32r, 8)
        h_lo = tile("h_lo", H0, 8, f32r, 8)
        xs = tile("xs", X0, 0, f32, 8)
        x_tok = tile("x_tok", G0, 0, f32, 8)
        ysc_hi = tile("ysc_hi", G0, 0, f32r, 4)
        ysc_lo = tile("ysc_lo", G0, 4, f32r, 4)
        bd_raw = at("bd_raw", G0 + 8 * TILE, [2, LRU_TILES, P])
        bd_hi = at("bd_hi", G0 + 10 * TILE, [2, P], f32r)
        bd_lo = at("bd_lo", G0 + 11 * TILE, [2, P], f32r)
        xc_hi = tile("xc_hi", G0, 12, f32r)
        xc_lo = tile("xc_lo", G0, 13, f32r)
        root = tile("root", G0, 14)
        gelu_gate = tile("gelu_gate", G0, 15)
        square_dve = tile("square_dve", G0, 15)
        gu_hi = tile("gu_hi", G0, 0, f32r, 8)
        gu_lo = tile("gu_lo", G0, 8, f32r, 8)
        lat = tile("lat", G0, 0, f32, 6)
        qn_hi = tile("qn_hi", X0, 4, f32r, 4)
        qn_lo = tile("qn_lo", G0, 0, f32r, 4)
        kvn_lo = tile("kvn_lo", G0, 4, f32r, 2)
        kvn_hi = tile("kvn_hi", G0, 6, f32r, 2)
        acc_q = tile("acc_q", G0, 8)
        acc_kv = tile("acc_kv", G0, 9)
        pw_raw = at("pw_raw", G0 + 10 * TILE, [4, P])
        pw_hi = at("pw_hi", G0 + 10 * TILE + 2048, [P], f32r)
        pw_lo = at("pw_lo", G0 + 10 * TILE + 2560, [P], f32r)
        pooled_hi = tile("pooled_hi", G0, 11, f32r)
        pooled_lo = tile("pooled_lo", G0, 12, f32r)
        square2 = tile("square2", G0, 13)
        y_pool = tile("y_pool", X0, 0, f32, 4)
        sin_t = tile("sin_t", G0, 14)
        cos_t = tile("cos_t", G0, 15)
        pt_hi = at("pt_hi", G0, [NT, HALF], f32r)
        pt_lo = at("pt_lo", G0 + 4 * TILE, [NT, HALF], f32r)
        kr_hi = tile("kr_hi", G0, 8, f32r)
        kr_lo = tile("kr_lo", G0, 9, f32r)
        qr_hi = tile("qr_hi", G0, 10, f32r, 2)
        qr_lo = tile("qr_lo", G0, 12, f32r, 2)
        kn_hi = tile("kn_hi", X0, 0, f32r, 4)
        kn_lo = tile("kn_lo", X0, 4, f32r, 4)
        v_hi = at("v_hi", H0, [NT, HEADS * VDIM], f32r)
        v_lo = at("v_lo", H0 + 4 * TILE, [NT, HEADS * VDIM], f32r)
        qh_hi = tile("qh_hi", H0, 8, f32r, 4)
        qh_lo = tile("qh_lo", H0, 12, f32r, 4)
        prob = [tile(f"prob{s}", W0, s) for s in range(3)]
        mask = [tile(f"mask{s}", W0, 3 + s) for s in range(2)]
        gate_in = [at(f"gate_in{s}", S0 + s * 2048, [HALF]) for s in range(2)]
        ya_out = [at(f"ya_out{s}", S0 + TILE + s * 2048, [HALF]) for s in range(2)]
        z_hi, z_lo, wo_hi, wo_lo = ([tile(f"{name}{e}", place, 8 * e + part, f32r, 4) for e in range(2)]
                                    for name, place, part in (("z_hi", H0, 0), ("z_lo", H0, 4),
                                                              ("wo_hi", G0, 0), ("wo_lo", G0, 4)))
        zin = tile("zin", X0, 0, f32, 8)
        resid = tile("resid", W0, 0, f32, 6)
        resid_last = tile("resid_last", X0, 0, f32, 2)
        ln_g = tile("ln_g", S0, 0)
        ln_b = tile("ln_b", S0, 1)
        ln_sq = tile("ln_sq", S0, 2)
        ln_v = [tile(f"ln_v{s}", S0, 3 + s) for s in range(2)]
        scr = [tile(f"scr{s}", S0, s) for s in range(5)]
        pos_f = tile("pos_f", S0, 4)
        pos_i = at("pos_i", S0 + 4 * TILE, [SEQ], i32)
        at_c = [C0]

        def const(name, cols, dt=f32):
            t = at(name, at_c[0], [cols], dt)
            at_c[0] += (cols * 4 + 31) // 32 * 32
            return t

        vec = const("vec", V_COLS)
        ident = const("ident", P)
        meanw = const("meanw", 3)
        rc = const("rc", 16)
        eps = const("eps", 2)
        half_ba = const("half_ba", 8)
        half_bx = const("half_bx", 8)
        half_ps = const("half_ps", 4)
        kh = const("kh", 8)
        kx = const("kx", 8)
        small = const("small", 48)
        rstd = const("rstd", 8)
        freq = const("freq", 1)
        sign = const("sign", 1)
        stat = const("stat", 16)
        assert at_c[0] <= nc.sbuf_usable_end, at_c[0]

        ps = [ctx.enter_context(nc.psum_tensor(f"ps{s}", [P, SEQ], f32)) for s in range(4)]

        x_park = nc.dram_tensor("x_park", (KT, P, SEQ), f32, kind="Internal").ap()
        res_park = nc.dram_tensor("res_park", (NT, P, D), f32, kind="Internal").ap()
        gate_park = nc.dram_tensor("gate_park", (HEADS, P, SEQ), f32, kind="Internal").ap()
        y_park = nc.dram_tensor("y_park", (KT, P, SEQ), f32, kind="Internal").ap()

        def sem(name):
            return ctx.enter_context(nc.semaphore(name))

        rows_in, x_in = sem("rows_in"), [sem(f"x_in{n}") for n in range(4)]
        bd_in, pw_in, pos_in = sem("bd_in"), sem("pw_in"), sem("pos_in")
        w_in_sem = [sem(f"w_loaded{s}") for s in range(2)]
        x_parked, x_back = sem("x_parked"), [sem(f"x_back{s}") for s in range(2)]
        res_parked = [sem(f"res_parked{q}") for q in range(2)]
        gate_parked = [sem(f"gate_parked{q}") for q in range(2)]
        ya_parked = [sem(f"ya_parked{q}") for q in range(2)]
        y_parked = sem("y_parked")
        gate_back = [sem(f"gate_back{s}") for s in range(2)]
        z_loaded = [sem(f"z_loaded{s}") for s in range(4)]
        last_in = sem("last_in")
        stored = [sem(f"stored{q}") for q in range(2)]
        w_hi_done, w_lo_done, block_done = sem("w_hi_done"), sem("w_lo_done"), sem("block_done")
        dve_step, pool_step = sem("dve_step"), sem("pool_step")
        ident_done, bd_zeroed, const_done = sem("ident_done"), sem("bd_zeroed"), sem("const_done")
        sign_done = sem("sign_done")
        pos_f_done, vec_t, vec_done = sem("pos_f_done"), sem("vec_t"), sem("vec_done")
        lam_abs, lam_exp, params_done = sem("lam_abs"), sem("lam_exp"), sem("params_done")
        sumsq_dve = sem("sumsq_dve")
        sumsq, ms_done, root_done, rstd_done, rb_done = (sem("sumsq"), sem("ms_done"),
            sem("root_done"), sem("rstd_done"), sem("rb_done"))
        sq_done, acc_done = sem("sq_done"), sem("acc_done")
        xt_done, xt_copied = sem("xt_done"), sem("xt_copied")
        v_done, hi_done = sem("normed"), sem("normed_hi")
        lo_dve, lo_pool = sem("normed_lo_dve"), sem("normed_lo_pool")
        sc_c, sc_p, sc_base, sc_y, sc_hi, sc_lo = (sem("sc_c"), sem("sc_p"), sem("sc_base"),
            sem("sc_y"), sem("sc_hi"), sem("sc_lo"))
        conv_base, conv_done, xc_hi_done, xc_lo_done = (sem("conv_base"), sem("conv_done"),
            sem("xc_hi_done"), sem("xc_lo_done"))
        bd_hi_done, ri_done, rt_done, it_done = (sem("bd_hi_done"), sem("ri_done"), sem("rt_done"),
            sem("it_done"))
        gelu_done, ex_done, s_done, root_s, y_done = (sem("gelu_done"), sem("ex_done"),
            sem("s_done"), sem("root_s"), sem("y_done"))
        x1_done = sem("x1_done")
        ff_base = [sem(f"ff_base{s}") for s in range(4)]
        ff_conv = [sem(f"ff_conv{s}") for s in range(4)]
        ff_gelu = [sem(f"ff_gelu{q}") for q in range(2)]
        ff_v = [sem(f"ff_v{q}") for q in range(2)]
        ff_hi = [sem(f"ff_hi{q}") for q in range(2)]
        ff_lo = [sem(f"ff_lo{q}") for q in range(2)]
        dn_done = [sem(f"dn_done{s}") for s in range(4)]
        tok_t, tok_copied = sem("tok_t"), sem("tok_copied")
        lat_done, acc_q_done, acc_kv_done = sem("lat_done"), sem("acc_q_done"), sem("acc_kv_done")
        sq2_done = sem("sq2_done")
        red_done, trig_done = sem("red_done"), sem("trig_done")
        u_done, pl_done, pl_hi, pl_lo, pw_hi_done, pool_mm = (sem("u_done"), sem("pl_done"),
            sem("pl_hi"), sem("pl_lo"), sem("pw_hi_done"), sem("pool_mm"))
        gb_done = sem("gb_done")
        th_done, yb_done = sem("th_done"), sem("yb_done")
        ga_th, ga_done = sem("ga_th"), sem("ga_done")
        ms2_done, root2_done, rstd2_done, rb2_done = (sem("ms2_done"), sem("root2_done"),
            sem("rstd2_done"), sem("rb2_done"))
        latn_done, latn_hi, latn_lo_d, latn_lo_p = (sem("latn_done"), sem("latn_hi"),
            sem("latn_lo_d"), sem("latn_lo_p"))
        rope_sw, rope_a, rope_v, rope_hi, rope_lo = (sem("rope_sw"),
            sem("rope_a"), sem("rope_v"), sem("rope_hi"), sem("rope_lo"))
        up_done, nope_hi, nope_lo = sem("up_done"), sem("nope_hi"), sem("nope_lo")
        mask_done, score_done, smax_done, nmax_done, exp_done, inv_done, p_done = (sem("mask_done"),
            sem("score_done"), sem("smax_done"), sem("nmax_done"), sem("exp_done"),
            sem("inv_done"), sem("p_done"))
        pt_done, pt_hi_done, pt_lo_done, pv_done, ya_done = (sem("pt_done"), sem("pt_hi_done"),
            sem("pt_lo_done"), sem("pv_done"), sem("ya_done"))
        z_hi_done, z_lo_done, zp_lo_done, mix_done = (sem("z_hi_done"), sem("z_lo_done"),
            sem("zp_lo_done"), sem("mix_done"))
        ln_sum, ln_mean, ln_ssq, ln_root, ln_out = (sem("ln_sum"), sem("ln_mean"),
            sem("ln_ssq"), sem("ln_root"), sem("ln_out"))

        block = ctx.enter_context(nc.Block())
        rows0, rows1, rows2 = scr[0], scr[1], scr[2]
        pos_rows_i = at("pos_rows_i", S0 + 3 * TILE, [P], i32)
        pos_rows = at("pos_rows", S0 + 3 * TILE + 512, [P])

        @block.sync
        def _(sp):
            x_v = x.rearrange("o (n p) d -> p (o n) d", p=P)
            for n in range(4):
                sp.dma_start(x_tok[:, :, 256 * n:256 * n + 256], x_v[:, :, 256 * n:256 * n + 256]).then_inc(x_in[n], 16)

            def load(n, h, *views):
                if n >= 2:
                    sp.wait_ge(w_lo_done, n - 1 + 2 * h)
                for dst, src in views:
                    sp.dma_start(dst, src).then_inc(w_in_sem[n % 2], 16)

            def cols(n, k, w):
                return w_raw[n % 2][:, 0:k * w].rearrange("p (k n) -> p k n", n=w)

            w_in_v = w_in.rearrange("o (k p) n -> p (o k) n", p=P)
            sc0 = 2 * LRU_TILES * P
            for j in range(SC_TILES):
                for b, part in enumerate((1, 2, 0)):
                    n = N_SC + 3 * j + b
                    load(n, 0, (cols(n, 8, P), w_in_v[:, :, sc0 + part * 512 + j * P:sc0 + part * 512 + (j + 1) * P]))
                if j == 0:
                    sp.wait_ge(bd_zeroed, 1)
                    for which, wg in enumerate((lru_wa, lru_wx)):
                        heads = wg.rearrange("o (c e) i j -> (o e) i c j", e=2)
                        for e in range(2):
                            sp.dma_start(bd_raw[64 * e:64 * e + 64, which, :, 64 * e:64 * e + 64],
                                         heads[e]).then_inc(bd_in, 16)
            sp.wait_ge(xt_copied, KT)
            sp.dma_start(x_park.rearrange("c p t -> p c t"), xs[:, :, :]).then_inc(x_parked, 16)
            with sp.Fori(0, LRU_TILES) as c:
                for b in range(2):
                    load(N_LRU + b, c, (cols(b, 8, P), w_in_v[:, :, bass.ds(b * D + c * P, P)]))
            w_lru = w_out[0, 0:D, :].rearrange("(k p) n -> p k n", p=P)
            w_sc = w_out[0, D:D + 512, :].rearrange("(k p) n -> p k n", p=P)
            sp.wait_ge(x_parked, 16)
            with sp.Fori(1, 3) as r1:
                r = r1 - 1
                for b in range(6):
                    src = w_sc[:, :, bass.ds(r1 * 512 - 512 + b * 256, 256)] if b < 2 else \
                        w_lru[:, :, bass.ds(r1 * 512 - 512 + (b - 2) * P, P)]
                    load(N_OUT + b, 3 * r, (cols(b, 4, 256) if b < 2 else cols(b, 8, P), src))
                    if b >= 2:
                        if b == 2:
                            sp.wait_ge(y_done, LRU_TILES)
                        s = b % 2
                        sp.wait_ge(x1_done, (3 * r if b == 2 else 4 * r + b - 3) + 1)
                        sp.dma_start(scr[s][:, :], x_park[bass.ds(4 * r + b - 2, 1)].rearrange("o p t -> p (o t)")
                                     ).then_inc(x_back[s], 16)
            w_up_v = w_up.rearrange("o (k p) n -> p (o k) n", p=P)
            w_dn_v = w_down.rearrange("o (k p) n -> p (o k) n", p=P)
            with sp.Fori(0, GROUPS) as g:
                with sp.Fori(0, FF_GROUP // 2) as fp:
                    for b in range(4):
                        col = (b % 2) * 3072 + g * (FF_GROUP * P) + fp * 256 + (b // 2) * P
                        load(N_FF + b, g * (GROUP_BLOCKS // 2) + fp * 2,
                             (cols(b, 8, P), w_up_v[:, :, bass.ds(col, P)]))
                with sp.Fori(0, 2) as dp:
                    for b in range(4):
                        load(N_FF + 2 * FF_GROUP + b, g * (GROUP_BLOCKS // 2) + dp * 2,
                             (cols(b, 8, P), w_dn_v[:, bass.ds(g * FF_GROUP, FF_GROUP), bass.ds(dp * 512 + b * P, P)]))
            w2_v = w_in_2.rearrange("(k p) n -> p k n", p=P)
            order = [i * P for i in range(Q_TILES + KV_TILES)]
            for g in range(4):
                order += [1344 + g * P, 1856 + g * P]
            order += [832 + h * P for h in range(HEADS)]
            for i, col in enumerate(order):
                n = N_IN2 + i
                load(n, 0, (cols(n, 8, P), w2_v[:, :, col:col + P]))
                if i == 2:
                    sp.wait_ge(block_done, N_IN2)
                    sp.dma_start(pw_raw[:, :, :], pool_w_2.rearrange("g c d -> c g d")).then_inc(pw_in, 16)
                    sp.wait_ge(ms_done, 2)
                    sp.dma_start(pos_i[:, :], positions_2.broadcast_to([P, SEQ])).then_inc(pos_in, 16)
            n = N_KR
            load(n, 0, (cols(n, 8, P)[:, :, 0:64], w2_v[:, :, 768:832]),
                 (cols(n, 8, P)[:, :, 64:128], w2_v[:, :, 768:832]))
            uq = w_uq_2.rearrange("(k p) (h n) -> p k h n", p=P, h=HEADS)
            n = N_UQ
            dst = w_raw[n % 2][:, :].rearrange("p (k h n) -> p k h n", k=4, h=HEADS)
            load(n, 0, *[(dst[:, :, h, :], uq[:, :, h, NOPE:QK]) for h in range(HEADS)])
            for b in range(2):
                n = N_UQ + 1 + b
                dst = w_raw[n % 2][:, :].rearrange("p (k h n) -> p k h n", k=4, h=2)
                load(n, 0, *[(dst[:, :, e, :], uq[:, :, 2 * b + e, 0:NOPE]) for e in range(2)])
            ukv = w_ukv_2.rearrange("(k p) (h e n) -> p k h e n", p=P, h=HEADS, e=2)
            for part in range(2):
                n = N_UKV + part
                dst = w_raw[n % 2][:, :].rearrange("p (k h n) -> p k h n", k=2, h=HEADS)
                load(n, 0, *[(dst[:, k], ukv[:, k, :, part, :]) for k in range(2)])
            for q in range(2):
                sp.wait_ge(gate_parked[q], 16 * HEADS // 2)
            for i in range(2 * HEADS):
                if i >= 2:
                    sp.wait_ge(ya_done, i - 1)
                if i == 0:
                    sp.wait_ge(rope_lo, 3)
                sp.dma_start(gate_in[i % 2][:, :], gate_park[i // 2][:, (i % 2) * HALF:(i % 2 + 1) * HALF]
                             ).then_inc(gate_back[i % 2], 16)
                if i >= 1:
                    j = i - 1
                    sp.wait_ge(ya_done, j + 1)
                    sp.dma_start(y_park[j // 2][:, (j % 2) * HALF:(j % 2 + 1) * HALF], ya_out[j % 2][:, :]
                                 ).then_inc(ya_parked[j % 2], 16)
            def z_load(i):
                k = (i // 2 * 2 + 4) % 8
                src = w_out_2.rearrange("(k p) n -> p k n", p=P) if i % 2 == 0 else y_park.rearrange("k p t -> p k t")
                s = i % 4
                sp.dma_start(zin[:, 2 * s:2 * s + 2, :], src[:, k:k + 2, :]).then_inc(z_loaded[s], 16)

            sp.wait_ge(score_done, UNITS)
            sp.wait_ge(y_parked, 16 * 4)
            for i in range(4):
                z_load(i)
            j = 2 * HEADS - 1
            sp.wait_ge(ya_done, j + 1)
            sp.dma_start(y_park[j // 2][:, (j % 2) * HALF:(j % 2 + 1) * HALF], ya_out[j % 2][:, :]
                         ).then_inc(ya_parked[j % 2], 16)
            for q in range(2):
                sp.wait_ge(res_parked[q], 16 * NT // 2)
            sp.wait_ge(pt_done, UNITS)
            sp.dma_start(resid[:, :, :], res_park[0:6].rearrange("n p d -> p n d")).then_inc(last_in, 16)
            for i in range(4, 8):
                sp.wait_ge(z_lo_done if i % 2 == 0 else zp_lo_done, i // 2 * 2 - 2)
                if i == 5:
                    for q in range(2):
                        sp.wait_ge(ya_parked[q], 16 * HEADS)
                z_load(i)
            sp.dma_start(ln_g[:, :], ln_g_2.broadcast_to([P, D])).then_inc(last_in, 16)
            sp.dma_start(ln_b[:, :], ln_b_2.broadcast_to([P, D])).then_inc(last_in, 16)
            sp.wait_ge(z_lo_done, 6)
            sp.dma_start(resid_last[:, :, :], res_park[6:8].rearrange("n p d -> p n d")).then_inc(last_in, 16)
            out_v = out.rearrange("o (n p) d -> (o n) p d", p=P)
            for t in range(NT):
                sp.wait_ge(ln_out, t + 1)
                sp.dma_start(out_v[t], ln_v[t % 2][:, :]).then_inc(stored[t % 2], 16)
            for q in range(2):
                sp.wait_ge(stored[q], 16 * NT // 2)

        def latents():
            return [(kvn_hi[:, i, :], kvn_lo[:, i, :]) for i in range(KV_TILES)] + \
                   [(qn_hi[:, i, :], qn_lo[:, i, :]) for i in range(Q_TILES)]

        def lat_tile(i):
            return lat[:, (i + Q_TILES) % (Q_TILES + KV_TILES), :]

        def z_tiles(n):
            j = n // 2
            k = (j + 4) % 8
            return k // 4, k % 4, zin[:, 2 * ((j // 2 * 2 + n % 2) % 4) + j % 2, :]

        UP_ENDS = (1, 3, 5, 9, 13)

        def up_ready(j):
            if j in UP_ENDS:
                return block_done, read(N_UQ + UP_ENDS.index(j))
            return up_done, j + 1 - sum(end < j for end in UP_ENDS)

        def raw_loads(n):
            parts = {N_KR: 2, N_UQ: 4, N_UQ + 1: 2, N_UQ + 2: 2, N_UKV: 2, N_UKV + 1: 2}
            return n // 2 + 1 + sum(k - 1 for m, k in parts.items() if m <= n and m % 2 == n % 2)

        def read(sem_n, h=0):
            return sem_n + 1 + 2 * h

        def matmul3(pe, out_ap, w_h, w_l, x_h, x_l, first, last):
            halves = [slice(0, HALF), slice(HALF, SEQ)]
            for w, x, a, b in ((w_h, x_h, first, False), (w_h, x_l, False, False),
                               (w_l, x_h, False, last)):
                for t in halves:
                    mm = nc.tensor.matmul(out_ap[:, t], w, x[:, t], start=a, stop=b)
            return mm

        @block.gpsimd
        def _(pool):
            step = Steps(pool, pool_step)
            for free in (acc_done, *ff_lo):
                nc.gpsimd.sem_inc(free, 1)
            step(nc.gpsimd.memset(ident[:, :], 0.0))
            nc.gpsimd.affine_select(out=ident[:, :], in_=ident[:, :], compare_op=ALU.not_equal, fill=1.0,
                                    base=0, pattern=[[-1, P]], channel_multiplier=1).then_inc(ident_done, 1)
            nc.gpsimd.memset(bd_raw[:, :, :, :], 0.0).then_inc(bd_zeroed, 1)
            for i, n in enumerate((D, Q_TILES * P, KV_TILES * P)):
                nc.gpsimd.memset(meanw[:, i:i + 1], 1.0 / n).then_inc(const_done, 1)
            nc.gpsimd.memset(eps[:, 0:1], EPS).then_inc(const_done, 1)
            nc.gpsimd.memset(eps[:, 1:2], LN_EPS).then_inc(const_done, 1)
            for t in range(16):
                nc.gpsimd.memset(rc[:, t:t + 1], 1.0 / (t + 1)).then_inc(const_done, 1)

            def low(n, h=0):
                if n >= N_BLOCKS:
                    return
                s = n % 2
                pool.wait_ge(w_hi_done, n + 1 + 2 * h)
                nc.gpsimd.tensor_tensor(w_lo[s][:, :], w_raw[s][:, :], w_hi[s][:, :].bitcast(f32),
                                        ALU.subtract).then_inc(w_lo_done, 1)

            def odd_lows(i, src):
                for c in range(1, KT, 2):
                    pool.wait_ge(hi_done, 8 * i + c + 1)
                    nc.gpsimd.tensor_tensor(h_lo[:, c, :], src(c), h_hi[:, c, :].bitcast(f32),
                                            ALU.subtract).then_inc(lo_pool, 1)

            low(0)
            low(1)
            odd_lows(0, lambda c: scr[c % 2][:, :])
            for j in range(SC_TILES):
                low(3 * j + 2)
                low(3 * j + 3)
                low(3 * j + 4)
                pool.wait_ge(sc_hi, j + 1)
                nc.gpsimd.tensor_tensor(ysc_lo[:, j, :], scr[3][:, :], ysc_hi[:, j, :].bitcast(f32),
                                        ALU.subtract).then_inc(sc_lo, 1)
            with pool.Fori(0, LRU_TILES) as c:
                low(N_LRU + 2, c)
                low(N_LRU + 3, c)
            pool.wait_ge(y_done, LRU_TILES)
            nc.gpsimd.memset(scr[4][:, :], 0.0).then_inc(acc_done, 1)
            odd_lows(1, lambda c: xs[:, c, :])
            with pool.Fori(0, 2) as r:
                for b in range(6):
                    low(N_OUT + b + 2, 3 * r)
                    if b >= 2:
                        pool.wait_ge(sq_done, 4 * r + b - 1)
                        pool.wait_ge(acc_done, 4 * r + b - 1 + 1)
                        nc.gpsimd.tensor_tensor(scr[4][:, :], scr[4][:, :], scr[2 + b % 2][:, :],
                                                ALU.add).then_inc(acc_done, 1)
            odd_lows(2, lambda c: scr[c % 2][:, :])

            def ff_up(g, h0):
                with pool.Fori(0, FF_GROUP // 2) as fp:
                    for q in range(2):
                        low(N_FF + 2 * q + 2, h0 + 2 * fp)
                        low(N_FF + 2 * q + 3, h0 + 2 * fp)
                        pool.wait_ge(ff_hi[q], 4 * g + fp + 1)
                        f = bass.ds(2 * fp + q, 1)
                        nc.gpsimd.tensor_tensor(gu_lo[:, f, :], scr[2 + q][:, :].unsqueeze(1), gu_hi[:, f, :].bitcast(f32),
                                                ALU.subtract).then_inc(ff_lo[q], 1)

            with pool.Fori(0, GROUPS - 1) as g:
                ff_up(g, 12 * g)
                with pool.Fori(0, 2) as dp:
                    for b in range(4):
                        low(N_FF + 16 + b + 2, 12 * g + 2 * dp)
            g = GROUPS - 1
            ff_up(g, 12 * g)
            pool.wait_ge(lo_dve, 12)
            nc.gpsimd.memset(scr[4][:, :], 0.0).then_inc(acc_done, 1)
            with pool.Fori(0, 2) as dp:
                for b in range(4):
                    low(N_FF + 16 + b + 2, 12 * g + 2 * dp)
                    pool.wait_ge(sq_done, 8 + 4 * dp + b + 1)
                    pool.wait_ge(acc_done, 10 + 4 * dp + b + 1)
                    nc.gpsimd.tensor_tensor(scr[4][:, :], scr[4][:, :], scr[2 + b % 2][:, :],
                                            ALU.add).then_inc(acc_done, 1)
            pool.wait_ge(block_done, N_IN2)
            odd_lows(3, lambda c: xs[:, c, :])
            nc.gpsimd.memset(acc_q[:, :], 0.0).then_inc(acc_q_done, 1)
            nc.gpsimd.memset(acc_kv[:, :], 0.0).then_inc(acc_kv_done, 1)
            for i in range(Q_TILES + KV_TILES):
                low(N_IN2 + i + 2)
                pool.wait_ge(sq2_done, i + 1)
                acc, done, k = (acc_q, acc_q_done, i) if i < Q_TILES else (acc_kv, acc_kv_done, i - Q_TILES)
                pool.wait_ge(done, k + 1)
                nc.gpsimd.tensor_tensor(acc[:, :], acc[:, :], square2[:, :], ALU.add).then_inc(done, 1)
            for g in range(len(WINDOWS)):
                low(N_POOL + 2 * g + 2)
                low(N_POOL + 2 * g + 3)
                pool.wait_ge(pl_hi, g + 1)
                nc.gpsimd.tensor_tensor(pooled_lo[:, :], scr[3][:, :], pooled_hi[:, :].bitcast(f32),
                                        ALU.subtract).then_inc(pl_lo, 1)
            for h in range(HEADS):
                low(N_GATE + h + 2)
                if h == 1:
                    for i, (hi, lo) in enumerate(latents()):
                        if i % 2 == 1:
                            pool.wait_ge(latn_hi, i + 1)
                            nc.gpsimd.tensor_tensor(lo, lat_tile(i), hi.bitcast(f32), ALU.subtract).then_inc(latn_lo_p, 1)
            for n in range(N_KR, N_BLOCKS):
                low(n + 2)
            for i in range(1, 16, 2):
                pool.wait_ge(z_hi_done, i + 1)
                e, k, raw = z_tiles(i)
                nc.gpsimd.tensor_tensor(z_lo[e][:, k, :], raw, z_hi[e][:, k, :].bitcast(f32),
                                        ALU.subtract).then_inc(zp_lo_done, 1)

        @block.scalar
        def _(act):
            def col(c):
                return vec[:, c:c + 1] if isinstance(c, int) else vec[:, bass.ds(c, 1)]

            def high(n, h=0):
                if n >= N_BLOCKS:
                    return
                s = n % 2
                act.wait_ge(w_in_sem[s], 16 * raw_loads(n) + 16 * h)
                if n >= 2:
                    act.wait_ge(block_done, n - 1 + 2 * h)
                nc.scalar.copy(w_hi[s][:, :], w_raw[s][:, :]).then_inc(w_hi_done, 1)

            def highs(src, waits):
                for c in range(KT):
                    act.wait_ge(*waits(c))
                    nc.scalar.copy(h_hi[:, c, :], src(c)).then_inc(hi_done, 1)

            row = 0
            for v in (norm1_g.rearrange("o (c p) -> (o c) p", p=P),
                      lru_conv_w.rearrange("o k (c p) -> (o k c) p", p=P),
                      lru_conv_b.rearrange("o (c p) -> (o c) p", p=P),
                      lru_ba.rearrange("o (c p) -> (o c) p", p=P),
                      lru_bx.rearrange("o (c p) -> (o c) p", p=P),
                      lru_lambda.rearrange("o (c p) -> (o c) p", p=P),
                      sc_conv_w.rearrange("o k (c p) -> (o k c) p", p=P),
                      norm2_g.rearrange("o (c p) -> (o c) p", p=P),
                      final_g.rearrange("(c p) -> c p", p=P),
                      q_norm_g_2.rearrange("(c p) -> c p", p=P),
                      kv_norm_g_2.rearrange("(c p) -> c p", p=P),
                      pool_scale_2.rearrange("(c p) -> c p", p=P)):
                n = v.shape[0]
                act.dma_start(rows0[row:row + n, 0:P], v).then_inc(rows_in, 16)
                row += n
            assert row == V_ROWS
            ffn_rows = ffn_conv_w.rearrange("o k (c p) -> (o k c) p", p=P)
            act.dma_start(rows1[0:72, 0:P], ffn_rows[0:72, :]).then_inc(rows_in, 16)
            act.dma_start(rows2[0:72, 0:P], ffn_rows[72:144, :]).then_inc(rows_in, 16)
            act.dma_start(pos_rows_i[0:NT, :], positions_2.rearrange("o (n p) -> (o n) p", p=P)
                         ).then_inc(rows_in, 16)
            act.dma_start(freq[:, :], rope_freq).then_inc(rows_in, 16)
            def xt_copy(c):
                act.wait_ge(xt_done, c + 1)
                nc.scalar.copy(xs[:, c, :], ps[c % 3][:, :]).then_inc(xt_copied, 1)

            for c in range(6):
                xt_copy(c)
            for n in range(4):
                act.wait_ge(x_in[n], 16)
            for n in range(5, NT):
                if n >= 6:
                    act.wait_ge(sumsq, n - 5)
                nc.scalar.activation(scr[4][:, :], x_tok[:, n, :], ACT.Square,
                                     accum_out=small[:, n:n + 1]).then_inc(sumsq, 1)
            act.wait_ge(sumsq, NT - 5)
            act.wait_ge(sumsq_dve, 5)
            act.wait_ge(const_done, 5)
            nc.scalar.activation(small[:, 8:16], small[:, 0:8], ACT.Sqrt, bias=eps[:, 0:1],
                                 scale=1.0 / D).then_inc(root_done, 1)
            xt_copy(6)
            xt_copy(7)
            act.wait_ge(vec_t, 1)
            nc.scalar.copy(vec[:, :], ps[3][:, 0:V_COLS]).then_inc(vec_done, 1)
            high(0)
            high(1)
            highs(lambda c: scr[c % 2][:, :], lambda c: (v_done, c + 1))
            act.wait_ge(lam_abs, 1)
            nc.scalar.activation(small[:, 24:32], small[:, 16:24], ACT.Exp).then_inc(lam_exp, 1)

            for j in range(SC_TILES):
                act.wait_ge(block_done, read(3 * j))
                if j >= 1:
                    act.wait_ge(sc_p, j)
                nc.scalar.copy(scr[0][:, :], ps[(3 * j) % 4][:, :]).then_inc(sc_c, 1)
                high(3 * j + 2)
                high(3 * j + 3)
                act.wait_ge(sc_p, j + 1)
                if j >= 1:
                    act.wait_ge(sc_y, j)
                nc.scalar.activation(scr[2][:, :], scr[1][:, :], ACT.Identity,
                                     scale=col(V_SCW + 8 + j)).then_inc(sc_base, 1)
                high(3 * j + 4)
                act.wait_ge(sc_y, j + 1)
                nc.scalar.copy(ysc_hi[:, j, :], scr[3][:, :]).then_inc(sc_hi, 1)

            act.wait_ge(params_done, 1)
            act.wait_ge(bd_in, 64)
            act.wait_ge(sc_lo, SC_TILES)
            act.wait_ge(x_parked, 16)

            def conv_first(c, one):
                act.wait_ge(block_done, read(N_LRU, c))
                nc.scalar.activation(xs[:, one, :], ps[0][:, :].unsqueeze(1), ACT.Identity,
                                     scale=col(V_CONVW + 24 + c), bias=col(V_CONVB + c)).then_inc(conv_base, 1)
                high(N_LRU + 2, c)

            def gate_weights(c, one):
                nc.scalar.copy(bd_hi[:, :, :], bd_raw[:, :, one, :].rearrange("p w o n -> p w (o n)")
                               ).then_inc(bd_hi_done, 1)

            def gate_curves(c, one):
                act.wait_ge(ri_done, 2 * c + 1)
                nc.scalar.activation(scr[1][:, :], ps[2][:, :], ACT.Tanh, scale=0.5,
                                     bias=half_ba[:, one]).then_inc(rt_done, 1)
                act.wait_ge(ri_done, 2 * c + 2)
                nc.scalar.activation(scr[2][:, :], ps[3][:, :], ACT.Tanh, scale=0.5,
                                     bias=half_bx[:, one]).then_inc(it_done, 1)
                act.wait_ge(rt_done, c + 1)
                nc.scalar.activation(scr[4][:, :], scr[1][:, :], ACT.Tanh, scale=kh[:, one],
                                     bias=kh[:, one]).then_inc(s_done, 1)
                nc.scalar.activation(scr[3][:, :], scr[1][:, :], ACT.Exp, scale=kx[:, one],
                                     bias=kx[:, one]).then_inc(ex_done, 1)
                act.wait_ge(s_done, c + 1)
                nc.scalar.activation(root[:, :], scr[4][:, :], ACT.Sqrt).then_inc(root_s, 1)

            def gate_gelu(c, one):
                act.wait_ge(conv_done, c + 1)
                act.wait_ge(block_done, read(N_LRU + 1, c))
                high(N_LRU + 3, c)
                nc.scalar.copy(xc_hi[:, :].unsqueeze(1), xs[:, one, :]).then_inc(xc_hi_done, 1)
                if not isinstance(c, int):
                    act.wait_ge(y_done, c)
                nc.scalar.activation(gelu_gate[:, :], ps[1][:, :], ACT.Gelu_apprx_tanh).then_inc(gelu_done, 1)

            first = slice(0, 1)
            conv_first(0, first)
            gate_weights(0, first)
            gate_gelu(0, first)
            with act.Fori(1, LRU_TILES) as c:
                conv_first(c, bass.ds(c, 1))
                gate_curves(c - 1, bass.ds(c - 1, 1))
                gate_weights(c, bass.ds(c, 1))
                gate_gelu(c, bass.ds(c, 1))
            gate_curves(LRU_TILES - 1, slice(LRU_TILES - 1, LRU_TILES))

            act.wait_ge(block_done, N_OUT)
            highs(lambda c: xs[:, c, :], lambda c: (y_done, c + 1))
            with act.Fori(0, 2) as r:
                for b in range(6):
                    act.wait_ge(block_done, read(N_OUT + b, 3 * r))
                    high(N_OUT + b + 2, 3 * r)
                    if b >= 2:
                        act.wait_ge(x1_done, 4 * r + b - 1 + 1)
                        act.wait_ge(acc_done, 4 * r + b - 2 + 1)
                        nc.scalar.activation(scr[2 + b % 2][:, :].unsqueeze(1), xs[:, bass.ds(4 * r + b - 2, 1), :],
                                             ACT.Square).then_inc(sq_done, 1)

            def norm_root(i):
                act.wait_ge(ms_done, i)
                nc.scalar.activation(small[:, 8:16], ps[2][:, 0:NT], ACT.Sqrt, bias=eps[:, 0:1]
                                     ).then_inc(root_done, 1)

            norm_root(1)
            highs(lambda c: scr[c % 2][:, :], lambda c: (v_done, 8 + c + 1))
            act.wait_ge(lo_dve, 12)
            act.wait_ge(lo_pool, 12)

            def ff_up(g, h0):
                with act.Fori(0, FF_GROUP // 2) as fp:
                    for q in range(2):
                        n, h, turn = N_FF + 2 * q, h0 + 2 * fp, 4 * g + fp
                        f = 8 * g + 2 * fp + q
                        act.wait_ge(block_done, read(n, h))
                        act.wait_ge(ff_v[q], turn + 1)
                        nc.scalar.activation(scr[q][:, :], ps[2 * q][:, :], ACT.Identity,
                                             scale=col(V_FFN + 96 + f)).then_inc(ff_base[2 * q], 1)
                        high(n + 2, h)
                        act.wait_ge(block_done, read(n + 1, h))
                        act.wait_ge(ff_lo[q], turn + 1)
                        nc.scalar.activation(scr[2 + q][:, :], ps[2 * q + 1][:, :], ACT.Identity,
                                             scale=col(V_FFN + 96 + 24 + f)).then_inc(ff_base[2 * q + 1], 1)
                        high(n + 3, h)
                        act.wait_ge(ff_conv[2 * q], turn + 1 + 1)
                        nc.scalar.activation(scr[q][:, :], scr[q][:, :], ACT.Gelu_apprx_tanh).then_inc(ff_gelu[q], 1)
                        act.wait_ge(ff_v[q], turn + 1 + 1)
                        nc.scalar.copy(gu_hi[:, bass.ds(2 * fp + q, 1), :], scr[2 + q][:, :].unsqueeze(1)
                                       ).then_inc(ff_hi[q], 1)

            with act.Fori(0, GROUPS - 1) as g:
                ff_up(g, 12 * g)
                with act.Fori(0, 2) as dp:
                    for b in range(4):
                        act.wait_ge(block_done, read(N_FF + 16 + b, 12 * g + 2 * dp))
                        high(N_FF + 16 + b + 2, 12 * g + 2 * dp)
            g = GROUPS - 1
            ff_up(g, 12 * g)
            for q in range(2):
                act.wait_ge(ff_lo[q], 4 * GROUPS + 1)
            with act.Fori(0, 2) as dp:
                for b in range(4):
                    act.wait_ge(block_done, read(N_FF + 16 + b, 12 * g + 2 * dp))
                    high(N_FF + 16 + b + 2, 12 * g + 2 * dp)
                    act.wait_ge(dn_done[b], 2 * g + dp + 1 + 1)
                    act.wait_ge(acc_done, 9 + 4 * dp + b + 1)
                    nc.scalar.activation(scr[2 + b % 2][:, :].unsqueeze(1), xs[:, bass.ds(4 * dp + b, 1), :],
                                         ACT.Square).then_inc(sq_done, 1)
            norm_root(2)
            highs(lambda c: xs[:, c, :], lambda c: (v_done, 16 + c + 1))

            def park_residual(t):
                act.wait_ge(tok_t, t + 1)
                if t >= 2:
                    act.wait_ge(res_parked[t % 2], 16 * (t // 2))
                nc.scalar.mul(scr[t % 2][:, :], ps[2 + t % 2][:, :], ALPHA).then_inc(tok_copied, 1)
                act.wait_ge(tok_copied, t + 1)
                act.dma_start(res_park[t], scr[t % 2][:, :]).then_inc(res_parked[t % 2], 16)

            for i in range(Q_TILES + KV_TILES):
                act.wait_ge(block_done, read(N_IN2 + i))
                high(N_IN2 + i + 2)
                act.wait_ge(lat_done, i + 1)
                if i >= 1:
                    act.wait_ge(acc_q_done if i <= Q_TILES else acc_kv_done,
                                i + 1 if i <= Q_TILES else i - Q_TILES + 1)
                nc.scalar.activation(square2[:, :], lat[:, i, :], ACT.Square).then_inc(sq2_done, 1)
                if 1 <= i <= NT // 2:
                    park_residual(2 * i - 2)
                    park_residual(2 * i - 1)
                if i == 2:
                    act.wait_ge(red_done, 2)
                    act.wait_ge(sign_done, 4)
                    nc.scalar.activation(sin_t[:, :], sin_t[:, :], ACT.Sin, scale=sign[:, 0:1]).then_inc(trig_done, 1)
                    nc.scalar.activation(cos_t[:, :], cos_t[:, :], ACT.Sin).then_inc(trig_done, 1)
            act.wait_ge(pw_in, 16)
            act.wait_ge(acc_kv_done, KV_TILES + 1)

            def park_pooled(g):
                act.wait_ge(yb_done, g + 1)
                act.dma_start(y_park[4 + g], y_pool[:, g, :]).then_inc(y_parked, 16)

            for g in range(len(WINDOWS)):
                act.wait_ge(block_done, read(N_POOL + 2 * g))
                high(N_POOL + 2 * g + 2)
                if g >= 1:
                    act.wait_ge(pool_mm, g)
                nc.scalar.copy(pw_hi[:, :], pw_raw[:, g, :]).then_inc(pw_hi_done, 1)
                act.wait_ge(pl_done, g + 1)
                nc.scalar.copy(pooled_hi[:, :], scr[3][:, :]).then_inc(pl_hi, 1)
                if g == 0:
                    act.wait_ge(ms2_done, 1)
                    nc.scalar.activation(stat[:, 0:16], ps[3][:, 0:16], ACT.Sqrt, bias=eps[:, 0:1]).then_inc(root2_done, 1)
                act.wait_ge(block_done, read(N_POOL + 2 * g + 1))
                nc.scalar.activation(y_pool[:, g, :], ps[1][:, :], ACT.Tanh, scale=0.5).then_inc(th_done, 1)
                high(N_POOL + 2 * g + 3)
                if g >= 1:
                    park_pooled(g - 1)

            def gate(h):
                act.wait_ge(block_done, read(N_GATE + h))
                if h >= 2:
                    act.wait_ge(gate_parked[h % 2], 16 * (h // 2))
                nc.scalar.activation(scr[h % 2][:, :], ps[h % 2][:, :], ACT.Tanh, scale=0.5).then_inc(ga_th, 1)
                high(N_GATE + h + 2)
                act.wait_ge(ga_done, h + 1)
                act.dma_start(gate_park[h], scr[h % 2][:, :]).then_inc(gate_parked[h % 2], 16)

            gate(0)
            park_pooled(3)
            gate(1)
            for i, (hi, lo) in enumerate(latents()):
                act.wait_ge(latn_done, i + 1)
                nc.scalar.copy(hi, lat_tile(i)).then_inc(latn_hi, 1)
            gate(2)
            gate(3)
            for q in range(2):
                act.wait_ge(gate_parked[q], 16 * HEADS // 2)

            def rope(r, src, dst):
                for q in range(4):
                    p = q ^ 1
                    nc.scalar.copy(scr[1][32 * q:32 * q + 32, :], src[32 * p:32 * p + 32, :]).then_inc(rope_sw, 1)
                act.wait_ge(rope_v, r + 1)
                nc.scalar.copy(dst, scr[2][:, :]).then_inc(rope_hi, 1)

            def up_high(j, dst, **split):
                act.wait_ge(*up_ready(j))
                src = ps[(j + 1) % 4][:, :]
                nc.scalar.copy(dst, src.rearrange("p (t d) -> p t d", t=2) if split else src).then_inc(nope_hi, 1)

            act.wait_ge(block_done, read(N_KR))
            high(N_KR + 2)
            act.wait_ge(acc_q_done, Q_TILES + 1)
            rope(0, ps[0], kr_hi[:, :])
            act.wait_ge(*up_ready(0))
            rope(1, ps[1], qr_hi[:, 0, :])
            act.wait_ge(block_done, read(N_UQ))
            high(N_UQ + 2)
            rope(2, ps[2], qr_hi[:, 1, :])
            for h in range(HEADS):
                up_high(2 + h, qh_hi[:, h, :])
                if h % 2 == 1:
                    act.wait_ge(block_done, read(N_UQ + 1 + h // 2))
                    high(N_UQ + 1 + h // 2 + 2)
            act.wait_ge(y_parked, 16 * 4)
            for h in range(HEADS):
                up_high(6 + h, kn_hi[:, h, :])
            for i in range(4):
                up_high(10 + i, v_hi[:, 2 * i:2 * i + 2, :], token_pairs=True)

            def z_high(n):
                i = n // 4 * 2 + n % 2
                act.wait_ge(z_loaded[i % 4], 16 * (i // 4 + 1))
                e, k, raw = z_tiles(n)
                nc.scalar.copy((wo_hi if n % 2 == 0 else z_hi)[e][:, k, :], raw).then_inc(z_hi_done, 1)

            for u in range(UNITS + 2):
                if 1 <= u <= UNITS:
                    s = (u - 1) % 3
                    act.wait_ge(inv_done, u)
                    nc.scalar.activation(prob[s][:, :], prob[s][:, :], ACT.Identity, scale=stat[:, 9 + s:10 + s]
                                         ).then_inc(p_done, 1)
                if u >= 2:
                    w = u - 2
                    act.wait_ge(pt_done, w + 1)
                    q = (w % 4) * P
                    nc.scalar.copy(pt_hi[:, :, q:q + P], ps[2][:, :].rearrange("p (k q) -> p k q", k=NT)
                                   ).then_inc(pt_hi_done, 1)
                if u < UNITS:
                    act.wait_ge(nmax_done, u + 1)
                    nc.scalar.activation(prob[u % 3][:, :], prob[u % 3][:, :], ACT.Exp,
                                         bias=stat[:, 3 + u % 3:4 + u % 3], scale=SCALE,
                                         accum_out=stat[:, 6 + u % 3:7 + u % 3]).then_inc(exp_done, 1)
                if u == UNITS:
                    z_high(0)
                    z_high(1)
            for n in range(2, 16):
                if n == 8:
                    act.wait_ge(pv_done, 2 * HEADS)
                z_high(n)
            for t in range(NT):
                q = t % 2
                act.wait_ge(ln_mean, t + 1)
                if t >= 1:
                    act.wait_ge(ln_ssq, t)
                nc.scalar.activation(ln_sq[:, :], ln_v[q][:, :], ACT.Square, bias=stat[:, 2 + q:3 + q],
                                     accum_out=stat[:, 4 + q:5 + q]).then_inc(ln_ssq, 1)
                act.wait_ge(ln_ssq, t + 1)
                nc.scalar.activation(stat[:, 6 + q:7 + q], stat[:, 4 + q:5 + q], ACT.Sqrt, scale=1.0 / D,
                                     bias=eps[:, 1:2]).then_inc(ln_root, 1)

        @block.vector
        def _(dve):
            step = Steps(dve, dve_step)
            V = nc.vector
            for free in (x1_done, *ff_conv, *ff_v, *dn_done):
                nc.vector.sem_inc(free, 1)

            def col(c):
                return vec[:, c:c + 1] if isinstance(c, int) else vec[:, bass.ds(c, 1)]

            def norm(i, v0, gain, dst, rb, lo_before):
                def value(c):
                    if c >= 2 and dst(c) is not None and lo_before:
                        if c % 2:
                            dve.wait_ge(lo_pool, 4 * i + (c - 2) // 2 + 1)
                        else:
                            dve.wait_ge(lo_dve, 4 * i + (c - 2) // 2 + 1)
                    if v0 == 0:
                        dve.wait_ge(xt_copied, c + 1)
                    V.scalar_tensor_tensor(out=dst(c), in0=xs[:, c, :], scalar=col(gain + c), in1=rb,
                                           op0=ALU.mult, op1=ALU.mult).then_inc(v_done, 1)

                value(0)
                for c in range(KT):
                    if c + 1 < KT:
                        value(c + 1)
                    if c % 2 == 0:
                        low(i, c, dst(c))

            def low(i, c, src):
                dve.wait_ge(hi_done, 8 * i + c + 1)
                V.tensor_tensor(h_lo[:, c, :], src, h_hi[:, c, :].bitcast(f32), ALU.subtract).then_inc(lo_dve, 1)

            def tap(acc, src, shift, c):
                return V.scalar_tensor_tensor(out=acc[:, shift:SEQ], in0=src[:, 0:SEQ - shift], scalar=col(c),
                                              in1=acc[:, shift:SEQ], op0=ALU.mult, op1=ALU.add)

            for q in range(4):
                V.memset(sign[32 * q:32 * q + 32, :], -1.0 if q % 2 == 0 else 1.0).then_inc(sign_done, 1)
            dve.wait_ge(rows_in, 16 * 16)
            V.tensor_copy(pos_rows[0:NT, :], pos_rows_i[0:NT, :]).then_inc(pos_f_done, 1)
            for n in range(4):
                dve.wait_ge(x_in[n], 16)
            for n in range(5):
                if n >= 1:
                    dve.wait_ge(sumsq_dve, n)
                V.tensor_tensor_reduce(out=square_dve[:, :], in0=x_tok[:, n, :], in1=x_tok[:, n, :], scale=1.0,
                                       scalar=0.0, op0=ALU.mult, op1=ALU.add, accum_out=small[:, n:n + 1]
                                       ).then_inc(sumsq_dve, 1)
            dve.wait_ge(root_done, 1)
            V.reciprocal(rstd[:, :], small[:, 8:16]).then_inc(rstd_done, 1)
            dve.wait_ge(vec_done, 1)
            step(V.scalar_tensor_tensor(out=small[:, 16:24], in0=vec[:, V_LAM:V_LAM + 8], scalar=-1.0,
                                        in1=vec[:, V_LAM:V_LAM + 8], op0=ALU.mult, op1=ALU.min))
            V.tensor_scalar(half_ba[:, :], vec[:, V_BA:V_BA + 8], 0.5, None, ALU.mult).then_inc(lam_abs, 1)
            step(V.tensor_scalar(half_bx[:, :], vec[:, V_BX:V_BX + 8], 0.5, None, ALU.mult))
            step(V.tensor_scalar(half_ps[:, :], vec[:, V_POOL:V_POOL + 4], 0.5, None, ALU.mult))
            dve.wait_ge(rb_done, 1)
            norm(0, 0, V_NORM1, lambda c: scr[c % 2][:, :], ps[3][:, :], True)
            dve.wait_ge(lam_exp, 1)
            e, z, z2, pl = small[:, 24:32], small[:, 32:40], small[:, 40:48], small[:, 16:24]
            step(V.tensor_scalar(z, e, 2.0, None, ALU.add))
            step(V.reciprocal(z2, z))
            step(V.tensor_tensor(z, e, z2, ALU.mult))
            step(V.tensor_tensor(z2, z, z, ALU.mult))
            step(V.tensor_scalar(pl, z2, 1.0 / 15, None, ALU.mult))
            for k in (13, 11, 9, 7, 5, 3):
                step(V.scalar_tensor_tensor(out=pl, in0=pl, scalar=1.0 / k, in1=z2, op0=ALU.add, op1=ALU.mult))
            step(V.scalar_tensor_tensor(out=pl, in0=pl, scalar=1.0, in1=z, op0=ALU.add, op1=ALU.mult))
            step(V.tensor_scalar(z, vec[:, V_LAM:V_LAM + 8], -2.0, 0.0, ALU.mult, ALU.max))
            step(V.scalar_tensor_tensor(out=kh[:, :], in0=pl, scalar=4.0, in1=z, op0=ALU.mult, op1=ALU.add))
            V.tensor_scalar(kx[:, :], kh[:, :], -2.0, None, ALU.mult).then_inc(params_done, 1)

            for j in range(SC_TILES):
                dve.wait_ge(block_done, read(3 * j + 1))
                dve.wait_ge(sc_c, j + 1)
                V.tensor_tensor(scr[1][:, :], ps[(3 * j + 1) % 4][:, :], scr[0][:, :], ALU.mult).then_inc(sc_p, 1)
                dve.wait_ge(sc_base, j + 1)
                step(tap(scr[2], scr[1], 1, V_SCW + 4 + j))
                step(tap(scr[2], scr[1], 2, V_SCW + j))
                dve.wait_ge(block_done, read(3 * j + 2))
                if j >= 1:
                    dve.wait_ge(sc_lo, j)
                V.tensor_tensor(scr[3][:, :], ps[(3 * j + 2) % 4][:, :], scr[2][:, :], ALU.mult).then_inc(sc_y, 1)

            def convolve(c, one):
                xc = xs[:, one, :].rearrange("p o t -> p (o t)")
                dve.wait_ge(conv_base, c + 1)
                step(tap(xc, ps[0], 1, V_CONVW + 16 + c))
                step(tap(xc, ps[0], 2, V_CONVW + 8 + c))
                tap(xc, ps[0], 3, V_CONVW + c).then_inc(conv_done, 1)

            def recur(c, one):
                xc = xs[:, one, :].rearrange("p o t -> p (o t)")
                dve.wait_ge(ex_done, c + 1)
                step(V.tensor_scalar(scr[3][:, :], scr[3][:, :], 0.5, 0.5, ALU.mult, ALU.add))
                step(V.scalar_tensor_tensor(out=scr[1][:, :], in0=scr[4][:, :], scalar=1.0, in1=scr[3][:, :],
                                            op0=ALU.add, op1=ALU.mult))
                step(V.scalar_tensor_tensor(out=scr[1][:, :], in0=scr[1][:, :], scalar=-2.0, in1=scr[3][:, :],
                                            op0=ALU.add, op1=ALU.mult))
                step(V.tensor_scalar(scr[3][:, :], scr[1][:, :], -2.0, -1.0, ALU.mult, ALU.add))
                dve.wait_ge(it_done, c + 1)
                step(V.scalar_tensor_tensor(out=scr[2][:, :], in0=scr[2][:, :], scalar=1.0, in1=xc,
                                            op0=ALU.add, op1=ALU.mult))
                dve.wait_ge(root_s, c + 1)
                step(V.tensor_tensor(root[:, :], scr[1][:, :], root[:, :], ALU.mult))
                step(V.tensor_tensor(root[:, :], root[:, :], scr[2][:, :], ALU.mult))
                step(V.tensor_tensor_scan(xc, scr[3][:, :], root[:, :], 0.0, ALU.mult, ALU.subtract))
                dve.wait_ge(gelu_done, c + 1)
                V.tensor_tensor(xc, xc, gelu_gate[:, :], ALU.mult).then_inc(y_done, 1)

            def second_parts(c, one):
                dve.wait_ge(bd_hi_done, c + 1)
                step(V.tensor_tensor(bd_lo[:, :, :], bd_raw[:, :, one, :].rearrange("p w o n -> p w (o n)"),
                                     bd_hi[:, :, :].bitcast(f32), ALU.subtract))
                dve.wait_ge(xc_hi_done, c + 1)
                V.tensor_tensor(xc_lo[:, :].unsqueeze(1), xs[:, one, :], xc_hi[:, :].bitcast(f32).unsqueeze(1),
                                ALU.subtract).then_inc(xc_lo_done, 1)

            first, last = slice(0, 1), slice(LRU_TILES - 1, LRU_TILES)
            convolve(0, first)
            second_parts(0, first)
            with step.of(11).loop(LRU_TILES - 1) as i:
                c = i + 1
                convolve(c, bass.ds(c, 1))
                recur(i, bass.ds(i, 1))
                second_parts(c, bass.ds(c, 1))
            recur(LRU_TILES - 1, last)

            for c in range(0, KT, 2):
                low(1, c, xs[:, c, :])
            dve.wait_ge(hi_done, 16)
            dve.wait_ge(lo_pool, 8)
            with dve.Fori(0, 2) as r:
                for q in range(4):
                    dve.wait_ge(block_done, read(N_OUT + 2 + q, 3 * r))
                    dve.wait_ge(x_back[q % 2], 32 * r + 16 * (q // 2 + 1))
                    V.tensor_tensor(xs[:, bass.ds(4 * r + q, 1), :], ps[q][:, :].unsqueeze(1), scr[q % 2][:, :].unsqueeze(1),
                                    ALU.add).then_inc(x1_done, 1)

            def norm_scale(i):
                dve.wait_ge(root_done, i + 1)
                V.reciprocal(rstd[:, :], small[:, 8:16]).then_inc(rstd_done, 1)
                dve.wait_ge(rb_done, i + 1)

            norm_scale(1)
            norm(2, 1, V_NORM2, lambda c: scr[c % 2][:, :], ps[3][:, :], True)

            def ff_group(g, h0):
                with step.of(4).loop(FF_GROUP // 2) as fp:
                    for q in range(2):
                        f, turn = 8 * g + 2 * fp + q, 4 * g + fp
                        for part in range(2):
                            s, dst = 2 * q + part, scr[q + 2 * part]
                            dve.wait_ge(ff_base[s], turn + 1)
                            step(tap(dst, ps[s], 1, V_FFN + 48 + 24 * part + f))
                            tap(dst, ps[s], 2, V_FFN + 24 * part + f).then_inc(ff_conv[s], 1)
                        dve.wait_ge(ff_gelu[q], turn + 1)
                        dve.wait_ge(ff_conv[2 * q + 1], turn + 1 + 1)
                        V.tensor_tensor(scr[2 + q][:, :], scr[q][:, :], scr[2 + q][:, :], ALU.mult).then_inc(ff_v[q], 1)
                with dve.Fori(0, 2) as dp:
                    for b in range(4):
                        dve.wait_ge(block_done, read(N_FF + 16 + b, h0 + 2 * dp))
                        d = bass.ds(4 * dp + b, 1)
                        V.tensor_tensor(xs[:, d, :], ps[b][:, :].unsqueeze(1), xs[:, d, :], ALU.add).then_inc(dn_done[b], 1)

            with step.of(16).loop(GROUPS) as g:
                ff_group(g, 12 * g)

            norm_scale(2)
            norm(3, 2, V_FINAL, lambda c: xs[:, c, :], ps[3][:, :], False)

            dve.wait_ge(block_done, N_IN2)
            for i in range(Q_TILES + KV_TILES):
                dve.wait_ge(block_done, read(N_IN2 + i))
                V.tensor_copy(lat[:, i, :], ps[i % 2][:, :]).then_inc(lat_done, 1)
                if i == 0:
                    dve.wait_ge(pos_in, 16)
                    step(V.tensor_copy(pos_f[:, :], pos_i[:, :]))
                    step(V.tensor_scalar(scr[2][:, :], pos_f[:, :], freq[:, 0:1], None, ALU.mult))
                if i in (0, 1):
                    t = (sin_t, cos_t)[i]
                    step(V.tensor_scalar(scr[3][:, :], scr[2][:, :], float(1 / (2 * np.pi)), 0.25 * i,
                                         ALU.mult, ALU.add))
                    step(V.tensor_scalar(scr[3][:, :], scr[3][:, :], ROUND, None, ALU.add))
                    step(V.tensor_scalar(scr[3][:, :], scr[3][:, :], ROUND, None, ALU.subtract))
                    src = scr[2]
                    for part in (TWO_PI_A, TWO_PI_B, TWO_PI_C):
                        step(V.scalar_tensor_tensor(out=t[:, :], in0=scr[3][:, :], scalar=-part, in1=src[:, :],
                                                    op0=ALU.mult, op1=ALU.add))
                        src = t
                    step(V.tensor_scalar(t[:, :], t[:, :], float(np.pi / 2) * i, 3.1415925, ALU.add, ALU.min))
                    V.tensor_scalar(t[:, :], t[:, :], -3.1415925, None, ALU.max).then_inc(red_done, 1)

            for q in range(2):
                dve.wait_ge(res_parked[q], 16 * NT // 2)
            def pooled_gate(g):
                dve.wait_ge(pool_mm, g + 1)
                dve.wait_ge(gb_done, g + 1)
                V.scalar_tensor_tensor(out=y_pool[:, g, :], in0=ps[2][:, :], scalar=half_ps[:, g:g + 1],
                                       in1=y_pool[:, g, :], op0=ALU.mult, op1=ALU.mult).then_inc(yb_done, 1)

            for g, w in enumerate(WINDOWS):
                dve.wait_ge(block_done, read(N_POOL + 2 * g))
                V.tensor_copy(scr[0][:, :], ps[0][:, :]).then_inc(u_done, 1)
                dve.wait_ge(u_done, g + 1)
                src, shift, k = scr[0], 1, 0
                while shift < w:
                    dst = scr[1 + k % 2]
                    step(V.tensor_tensor(dst[:, shift:SEQ], src[:, shift:SEQ], src[:, 0:SEQ - shift], ALU.add))
                    step(V.tensor_copy(dst[:, 0:shift], src[:, 0:shift]))
                    src, shift, k = dst, 2 * shift, k + 1
                if g >= 1:
                    pooled_gate(g - 1)
                    dve.wait_ge(pl_lo, g)
                step(V.scalar_tensor_tensor(out=scr[3][:, :], in0=src[:, :], scalar=1.0 / w, in1=scr[0][:, :],
                                            op0=ALU.mult, op1=ALU.subtract))
                if g == 0:
                    dve.wait_ge(const_done, 21)
                step(V.tensor_tensor(small[:, 16:16 + w - 1], src[:, 0:w - 1], rc[:, 0:w - 1], ALU.mult))
                V.tensor_tensor(scr[3][:, 0:w - 1], small[:, 16:16 + w - 1], scr[0][:, 0:w - 1],
                                ALU.subtract).then_inc(pl_done, 1)
                dve.wait_ge(pw_hi_done, g + 1)
                step(V.tensor_tensor(pw_lo[:, :], pw_raw[:, g, :], pw_hi[:, :].bitcast(f32), ALU.subtract))
                if g == 0:
                    dve.wait_ge(root2_done, 1)
                    V.reciprocal(stat[:, 0:16], stat[:, 0:16]).then_inc(rstd2_done, 1)
                dve.wait_ge(th_done, g + 1)
                V.scalar_tensor_tensor(out=y_pool[:, g, :], in0=y_pool[:, g, :], scalar=1.0, in1=ps[1][:, :],
                                       op0=ALU.add, op1=ALU.mult).then_inc(gb_done, 1)

            def gate(h):
                dve.wait_ge(ga_th, h + 1)
                V.scalar_tensor_tensor(out=scr[h % 2][:, :], in0=scr[h % 2][:, :], scalar=1.0, in1=ps[h % 2][:, :],
                                       op0=ALU.add, op1=ALU.mult).then_inc(ga_done, 1)

            gate(0)
            pooled_gate(3)
            gate(1)
            dve.wait_ge(rb2_done, 1)
            for i in range(KV_TILES + Q_TILES):
                kv = i < KV_TILES
                V.scalar_tensor_tensor(out=lat_tile(i), in0=lat_tile(i),
                                       scalar=col(V_KVN + i if kv else V_QN + i - KV_TILES),
                                       in1=ps[3 if kv else 2][:, :], op0=ALU.mult, op1=ALU.mult).then_inc(latn_done, 1)
            for i in range(0, KV_TILES + Q_TILES, 2):
                hi, lo = latents()[i]
                dve.wait_ge(latn_hi, i + 1)
                V.tensor_tensor(lo, lat_tile(i), hi.bitcast(f32), ALU.subtract).then_inc(latn_lo_d, 1)
            gate(2)
            gate(3)

            def rotate(r, src, hi, lo):
                if r == 0:
                    for q in range(2):
                        dve.wait_ge(gate_parked[q], 16 * HEADS // 2)
                dve.wait_ge(rope_sw, 4 * r + 4)
                V.tensor_tensor(scr[0][:, :], src[:, :], cos_t[:, :], ALU.mult).then_inc(rope_a, 1)
                step(V.tensor_tensor(scr[1][:, :], scr[1][:, :], sin_t[:, :], ALU.mult))
                dve.wait_ge(rope_a, r + 1)
                V.tensor_tensor(scr[2][:, :], scr[0][:, :], scr[1][:, :], ALU.add).then_inc(rope_v, 1)
                dve.wait_ge(rope_hi, r + 1)
                V.tensor_tensor(lo, scr[2][:, :], hi.bitcast(f32), ALU.subtract).then_inc(rope_lo, 1)

            def up_low(j, hi, lo, **split):
                src = ps[(j + 1) % 4][:, :]
                dve.wait_ge(nope_hi, j - 2 + 1)
                V.tensor_tensor(lo, src.rearrange("p (t d) -> p t d", t=2) if split else src, hi.bitcast(f32),
                                ALU.subtract).then_inc(nope_lo, 1)

            dve.wait_ge(trig_done, 2)
            dve.wait_ge(block_done, read(N_KR))
            rotate(0, ps[0], kr_hi[:, :], kr_lo[:, :])
            for r in range(2):
                dve.wait_ge(*up_ready(r))
                rotate(r + 1, ps[r + 1], qr_hi[:, r, :], qr_lo[:, r, :])
            for h in range(HEADS):
                up_low(2 + h, qh_hi[:, h, :], qh_lo[:, h, :])
            for h in range(HEADS):
                up_low(6 + h, kn_hi[:, h, :], kn_lo[:, h, :])
            for i in range(4):
                up_low(10 + i, v_hi[:, 2 * i:2 * i + 2, :], v_lo[:, 2 * i:2 * i + 2, :], token_pairs=True)

            def masks(u):
                if u < UNITS:
                    if u >= 2:
                        dve.wait_ge(smax_done, u - 1)
                    V.tensor_scalar(mask[u % 2][:, :], pos_f[:, :], col(V_POS + u % NT), MASKED, ALU.is_gt,
                                    ALU.mult).then_inc(mask_done, 1)

            def z_low(n):
                dve.wait_ge(z_hi_done, n + 1)
                e, k, raw = z_tiles(n)
                V.tensor_tensor(wo_lo[e][:, k, :], raw, wo_hi[e][:, k, :].bitcast(f32),
                                ALU.subtract).then_inc(z_lo_done, 1)

            masks(0)
            for u in range(UNITS + 3):
                if u < UNITS:
                    s = u % 3
                    dve.wait_ge(score_done, u + 1)
                    dve.wait_ge(mask_done, u + 1)
                    if u >= 3:
                        dve.wait_ge(pt_done, u - 2)
                    V.tensor_tensor_reduce(out=prob[s][:, :], in0=ps[u % 2][:, :], in1=mask[u % 2][:, :],
                                           scale=1.0, scalar=-3.0e38, op0=ALU.add, op1=ALU.max,
                                           accum_out=stat[:, s:s + 1]).then_inc(smax_done, 1)
                    dve.wait_ge(smax_done, u + 1)
                    V.tensor_scalar(stat[:, 3 + s:4 + s], stat[:, s:s + 1], -SCALE, None, ALU.mult
                                    ).then_inc(nmax_done, 1)
                masks(u + 1)
                if 2 <= u <= UNITS + 1:
                    w = u - 2
                    q = (w % 4) * P
                    dve.wait_ge(pt_hi_done, w + 1)
                    V.tensor_tensor(pt_lo[:, :, q:q + P], ps[2][:, :].rearrange("p (k q) -> p k q", k=NT),
                                    pt_hi[:, :, q:q + P].bitcast(f32), ALU.subtract).then_inc(pt_lo_done, 1)
                if u < UNITS:
                    dve.wait_ge(exp_done, u + 1)
                    V.reciprocal(stat[:, 9 + s:10 + s], stat[:, 6 + s:7 + s]).then_inc(inv_done, 1)
                if u == UNITS + 1:
                    for n in range(0, 8, 2):
                        z_low(n)
                if u >= 6 and (u - 2) % 4 == 0:
                    i = (u - 2) // 4 - 1
                    dve.wait_ge(pv_done, i + 1)
                    dve.wait_ge(gate_back[i % 2], 16 * (i // 2 + 1))
                    if i >= 2:
                        dve.wait_ge(ya_parked[i % 2], 16 * (i // 2))
                    V.scalar_tensor_tensor(out=ya_out[i % 2][:, :], in0=ps[3][:, (i % 2) * HALF:(i % 2 + 1) * HALF],
                                           scalar=0.5, in1=gate_in[i % 2][:, :], op0=ALU.mult, op1=ALU.mult
                                           ).then_inc(ya_done, 1)
            for n in range(8, 16, 2):
                z_low(n)
            dve.wait_ge(last_in, 16 * 4)

            def ln_first(t):
                q = t % 2
                dve.wait_ge(mix_done, t + 1)
                if t >= 2:
                    dve.wait_ge(stored[q], 16 * (t // 2))
                V.scalar_tensor_tensor(out=ln_v[q][:, :], in0=ps[t % 4][:, :], scalar=1.0,
                                       in1=resid[:, t, :] if t < 6 else resid_last[:, t - 6, :],
                                       op0=ALU.mult, op1=ALU.add, accum_out=stat[:, q:q + 1]).then_inc(ln_sum, 1)
                dve.wait_ge(ln_sum, t + 1)
                V.tensor_scalar(stat[:, 2 + q:3 + q], stat[:, q:q + 1], -1.0 / D, None, ALU.mult).then_inc(ln_mean, 1)

            ln_first(0)
            for t in range(NT):
                q = t % 2
                if t + 1 < NT:
                    ln_first(t + 1)
                dve.wait_ge(ln_root, t + 1)
                step(V.reciprocal(stat[:, 8 + q:9 + q], stat[:, 6 + q:7 + q]))
                step(V.tensor_scalar(ln_v[q][:, :], ln_v[q][:, :], stat[:, 2 + q:3 + q], stat[:, 8 + q:9 + q],
                                     ALU.add, ALU.mult))
                step(V.tensor_tensor(ln_v[q][:, :], ln_v[q][:, :], ln_g[:, :], ALU.mult))
                V.tensor_tensor(ln_v[q][:, :], ln_v[q][:, :], ln_b[:, :], ALU.add).then_inc(ln_out, 1)

        @block.tensor
        def _(pe):
            def blocked(n):
                return [w[n % 2][:, :].rearrange("p (k n) -> p k n", n=P) for w in (w_hi, w_lo)]

            def project(n, h, dst, x_h, x_l):
                pe.wait_ge(w_lo_done, n + 1 + 2 * h)
                wh, wl = blocked(n)
                for k in range(8):
                    mm = matmul3(pe, dst, wh[:, k, :], wl[:, k, :], x_h[:, k, :], x_l[:, k, :], k == 0, k == 7)
                mm.then_inc(block_done, 1)

            def mean_squares(acc, dst, which):
                for t in range(NT):
                    mm = nc.tensor.matmul(dst[:, t:t + 1], acc[:, t * P:(t + 1) * P], meanw[:, which:which + 1],
                                          start=True, stop=True)
                return mm

            def spread(scale, dst):
                for t in range(NT):
                    mm = nc.tensor.matmul(dst[:, t * P:(t + 1) * P], scale[:, t:t + 1].to_broadcast([P, P]),
                                          ident[:, :], start=True, stop=True)
                return mm

            pe.wait_ge(ident_done, 1)
            for c in range(KT):
                if c % 2 == 0:
                    pe.wait_ge(x_in[c // 2], 16)
                if c >= 3:
                    pe.wait_ge(xt_copied, c - 2)
                for t in range(NT):
                    mm = nc.tensor.transpose(ps[c % 3][:, t * P:(t + 1) * P], x_tok[:, t, c * P:(c + 1) * P], ident[:, :])
                mm.then_inc(xt_done, 1)
            pe.wait_ge(rows_in, 16 * 16)
            pe.wait_ge(pos_f_done, 1)
            for src, n, c in ((rows0, V_ROWS, 0), (rows1, 72, V_FFN), (rows2, 72, V_FFN + 72), (pos_rows, NT, V_POS)):
                mm = nc.tensor.transpose(ps[3][:, c:c + n], src[0:n, 0:P], ident[0:n, 0:n])
            mm.then_inc(vec_t, 1)
            pe.wait_ge(rstd_done, 1)
            pe.wait_ge(vec_done, 1)
            spread(rstd, ps[3]).then_inc(rb_done, 1)

            def input_ready(i):
                pe.wait_ge(lo_dve, 4 * (i + 1))
                pe.wait_ge(lo_pool, 4 * (i + 1))

            def first_two(n, dsts, i):
                for k in range(8 + 3):
                    for b, j in ((0, k), (1, k - 3)):
                        if not 0 <= j < 8:
                            continue
                        if j == 0:
                            pe.wait_ge(w_lo_done, n + b + 1)
                        if b == 0:
                            pe.wait_ge(lo_dve if j % 2 == 0 else lo_pool, 4 * i + j // 2 + 1)
                        wh, wl = blocked(n + b)
                        mm = matmul3(pe, dsts[b], wh[:, j, :], wl[:, j, :], h_hi[:, j, :], h_lo[:, j, :], j == 0, j == 7)
                        if j == 7:
                            mm.then_inc(block_done, 1)

            pe.wait_ge(xt_copied, KT)
            first_two(0, (ps[0], ps[1]), 0)
            readers = (sc_c, sc_p, sc_y)
            for n in range(2, 3 * SC_TILES):
                if n == 3:
                    pe.wait_ge(v_done, 8)
                if n >= 4:
                    m = n - 4
                    pe.wait_ge(readers[m % 3], m // 3 + 1)
                project(n, 0, ps[n % 4], h_hi, h_lo)
            def gates():
                matmul3(pe, ps[2], bd_hi[:, 0, :], bd_lo[:, 0, :], xc_hi, xc_lo, True, True).then_inc(ri_done, 1)
                matmul3(pe, ps[3], bd_hi[:, 1, :], bd_lo[:, 1, :], xc_hi, xc_lo, True, True).then_inc(ri_done, 1)

            pe.wait_ge(sc_y, 3)
            project(N_LRU, 0, ps[0], h_hi, h_lo)
            pe.wait_ge(sc_c, 4)
            project(N_LRU + 1, 0, ps[1], h_hi, h_lo)
            pe.wait_ge(sc_y, 4)
            with pe.Fori(1, LRU_TILES) as c:
                pe.wait_ge(conv_done, c)
                project(N_LRU, c, ps[0], h_hi, h_lo)
                pe.wait_ge(xc_lo_done, c)
                gates()
                pe.wait_ge(gelu_done, c)
                project(N_LRU + 1, c, ps[1], h_hi, h_lo)
            pe.wait_ge(xc_lo_done, LRU_TILES)
            gates()
            pe.wait_ge(conv_done, LRU_TILES)
            pe.wait_ge(gelu_done, LRU_TILES)
            pe.wait_ge(sc_lo, SC_TILES)
            with pe.Fori(0, 2) as r:
                for b in range(6):
                    n = N_OUT + b
                    if b < 2:
                        if b == 1:
                            pe.wait_ge(it_done, LRU_TILES)
                        pe.wait_ge(x1_done, 2 * (b + 1) * r + 1)
                        pe.wait_ge(w_lo_done, n + 1 + 6 * r)
                        wh, wl = [w[n % 2][:, :].rearrange("p (k e n) -> p k e n", k=4, e=2) for w in (w_hi, w_lo)]
                        for e in range(2):
                            for k in range(4):
                                mm = matmul3(pe, ps[2 * b + e], wh[:, k, e, :], wl[:, k, e, :], ysc_hi[:, k, :],
                                             ysc_lo[:, k, :], k == 0, False)
                        mm.then_inc(block_done, 1)
                    else:
                        if b == 2:
                            input_ready(1)
                        pe.wait_ge(w_lo_done, n + 1 + 6 * r)
                        wh, wl = blocked(n)
                        for k in range(8):
                            mm = matmul3(pe, ps[b - 2], wh[:, k, :], wl[:, k, :], h_hi[:, k, :], h_lo[:, k, :],
                                         False, k == 7)
                        mm.then_inc(block_done, 1)

            def norm(i, acc_value):
                pe.wait_ge(acc_done, acc_value)
                mean_squares(scr[4], ps[2], 0).then_inc(ms_done, 1)
                pe.wait_ge(rstd_done, i + 1)
                spread(rstd, ps[3]).then_inc(rb_done, 1)

            norm(1, 10)
            def ff_up(g, fp, blocks):
                for b in blocks:
                    pe.wait_ge(ff_conv[b], 4 * g + fp + 1)
                    pe.wait_ge(dn_done[b], 2 * g + 1)
                    project(N_FF + b, 12 * g + 2 * fp, ps[b], h_hi, h_lo)

            def ff_down(g):
                with pe.Fori(0, 2) as dp:
                    for pair in range(2):
                        d0, d1 = 2 * pair, 2 * pair + 1
                        for b, ks in ((d0, range(7)), (d1, range(4)), (d0, range(7, 8)), (d1, range(4, 8))):
                            n = N_FF + 2 * FF_GROUP + b
                            if ks[0] == 0:
                                pe.wait_ge(ff_conv[b], 4 * g + 4 + 1)
                                pe.wait_ge(dn_done[b], 2 * g + dp + 1)
                                pe.wait_ge(w_lo_done, n + 1 + 24 * g + 4 * dp)
                                pe.wait_ge(ff_lo[0], 4 * g + 4 + 1)
                                pe.wait_ge(ff_lo[1], 4 * g + 3 + 1)
                            elif ks[0] == 7:
                                pe.wait_ge(ff_lo[1], 4 * g + 4 + 1)
                            wh, wl = blocked(n)
                            for k in ks:
                                mm = matmul3(pe, ps[b], wh[:, k, :], wl[:, k, :], gu_hi[:, k, :], gu_lo[:, k, :],
                                             k == 0, k == 7)
                            if ks[-1] == 7:
                                mm.then_inc(block_done, 1)

            first_two(N_FF, (ps[0], ps[1]), 2)
            pe.wait_ge(v_done, 16)
            ff_up(0, 0, (2, 3))
            with pe.Fori(1, FF_GROUP // 2) as fp:
                ff_up(0, fp, range(4))
            ff_down(0)
            with pe.Fori(1, GROUPS) as g:
                with pe.Fori(0, FF_GROUP // 2) as fp:
                    ff_up(g, fp, range(4))
                ff_down(g)
            norm(2, 19)
            def by_token(t):
                if t >= 2:
                    pe.wait_ge(tok_copied, t - 1)
                for k in range(KT):
                    mm = nc.tensor.transpose(ps[2 + t % 2][:, k * P:(k + 1) * P], xs[:, k, t * P:(t + 1) * P], ident[:, :])
                mm.then_inc(tok_t, 1)

            first_two(N_IN2, (ps[0], ps[1]), 3)
            pe.wait_ge(v_done, 24)
            for i in range(2, Q_TILES + KV_TILES):
                by_token(2 * i - 4)
                by_token(2 * i - 3)
                pe.wait_ge(lat_done, i - 1)
                project(N_IN2 + i, 0, ps[i % 2], h_hi, h_lo)
            def pool_product():
                matmul3(pe, ps[2], pw_hi[:, :], pw_lo[:, :], pooled_hi, pooled_lo, True, True).then_inc(pool_mm, 1)

            pe.wait_ge(tok_copied, NT)
            pe.wait_ge(lat_done, 5)
            project(N_POOL, 0, ps[0], h_hi, h_lo)
            pe.wait_ge(acc_q_done, Q_TILES + 1)
            pe.wait_ge(acc_kv_done, KV_TILES + 1)
            mean_squares(acc_q, ps[3][:, 0:8], 1)
            mean_squares(acc_kv, ps[3][:, 8:16], 2).then_inc(ms2_done, 1)
            pe.wait_ge(lat_done, 6)
            project(N_POOL + 1, 0, ps[1], h_hi, h_lo)
            with pe.Fori(1, len(WINDOWS)) as g:
                pe.wait_ge(u_done, g)
                project(N_POOL, g, ps[0], h_hi, h_lo)
                pe.wait_ge(gb_done, g)
                pe.wait_ge(pl_lo, g)
                pool_product()
                project(N_POOL + 1, g, ps[1], h_hi, h_lo)
            for h in range(HEADS):
                if h == 0:
                    pe.wait_ge(u_done, 4)
                elif h == 1:
                    pe.wait_ge(pl_lo, 4)
                    pe.wait_ge(gb_done, 4)
                    pool_product()
                    pe.wait_ge(rstd2_done, 1)
                    spread(stat[:, 8:16], ps[3])
                else:
                    pe.wait_ge(ga_done, h - 1)
                project(N_GATE + h, 0, ps[h % 2], h_hi, h_lo)
                if h == 1:
                    pe.wait_ge(yb_done, 4)
                    spread(stat[:, 0:8], ps[2]).then_inc(rb2_done, 1)
            pe.wait_ge(ga_done, 3)
            project(N_KR, 0, ps[0], h_hi, h_lo)
            def free_slot(j):
                if j == 0:
                    pe.wait_ge(ga_done, 4)
                elif j == 1:
                    pe.wait_ge(latn_done, KV_TILES + Q_TILES)
                elif 3 <= j <= 5:
                    pe.wait_ge(rope_a, j - 2)
                elif j >= 6:
                    pe.wait_ge(nope_lo, j - 5)

            pe.wait_ge(latn_lo_d, 3)
            pe.wait_ge(latn_lo_p, 3)
            for b in range(3):
                n = N_UQ + b
                pe.wait_ge(w_lo_done, n + 1)
                wh, wl = [w[n % 2][:, :].rearrange("p (k e n) -> p k e n", k=4, e=2) for w in (w_hi, w_lo)]
                for e in range(2):
                    j = 2 * b + e
                    free_slot(j)
                    for k in range(4):
                        mm = matmul3(pe, ps[(j + 1) % 4], wh[:, k, e, :], wl[:, k, e, :], qn_hi[:, k, :],
                                     qn_lo[:, k, :], k == 0, k == 3)
                    mm.then_inc(up_ready(j)[0], 1)
            n = N_UKV
            pe.wait_ge(w_lo_done, n + 1)
            wh, wl = [w[n % 2][:, :].rearrange("p (k h n) -> p k h n", k=2, h=HEADS) for w in (w_hi, w_lo)]
            for h in range(HEADS):
                free_slot(6 + h)
                for k in range(2):
                    mm = matmul3(pe, ps[(7 + h) % 4], wh[:, k, h, :], wl[:, k, h, :], kvn_hi[:, k, :],
                                 kvn_lo[:, k, :], k == 0, k == 1)
                mm.then_inc(up_ready(6 + h)[0], 1)
            n = N_UKV + 1
            pe.wait_ge(w_lo_done, n + 1)
            wh, wl = [w[n % 2][:, :].rearrange("p (k n) -> p k n", k=2) for w in (w_hi, w_lo)]
            for t in range(NT):
                j = 10 + t // 2
                if t % 2 == 0:
                    free_slot(j)
                dst = ps[(j + 1) % 4][:, (t % 2) * HALF:(t % 2 + 1) * HALF]
                cols_t = slice(t * P, (t + 1) * P)
                for k in range(2):
                    for a, b, first, last in ((kvn_hi, wh, k == 0, False), (kvn_hi, wl, False, False),
                                              (kvn_lo, wh, False, k == 1)):
                        mm = nc.tensor.matmul(dst, a[:, k, cols_t], b[:, k, :], start=first, stop=last)
                if t % 2 == 1:
                    mm.then_inc(up_ready(j)[0], 1)

            def scores(u):
                h, t = u // NT, slice((u % NT) * P, (u % NT + 1) * P)
                r = slice(64 * (h % 2), 64 * (h % 2) + 64)
                for half in range(2):
                    keys = slice(half * HALF, (half + 1) * HALF)
                    dst = ps[u % 2][:, keys]
                    for i, (q, k) in enumerate(((qh_hi, kn_hi), (qh_hi, kn_lo), (qh_lo, kn_hi))):
                        nc.tensor.matmul(dst, q[:, h, t], k[:, h, keys], start=i == 0, stop=False)
                    for i, (q, k) in enumerate(((qr_hi, kr_hi), (qr_hi, kr_lo), (qr_lo, kr_hi))):
                        mm = nc.tensor.matmul(dst, q[r, h // 2, t], k[r, keys], start=False, stop=i == 2)
                mm.then_inc(score_done, 1)

            def weigh(i):
                h = i // 2
                dst = ps[3][:, (i % 2) * HALF:(i % 2 + 1) * HALF]
                d = slice(h * VDIM, (h + 1) * VDIM)
                for k in range(NT):
                    for a, b, first, last in ((v_hi, pt_hi, k == 0, False), (v_hi, pt_lo, False, False),
                                              (v_lo, pt_hi, False, k == NT - 1)):
                        mm = nc.tensor.matmul(dst, a[:, k, d], b[:, k, :], start=first, stop=last)
                mm.then_inc(pv_done, 1)

            pe.wait_ge(rope_lo, 3)
            for u in range(UNITS + 3):
                if u < UNITS:
                    if u < 2:
                        pe.wait_ge(nope_lo, 10 + u)
                    else:
                        pe.wait_ge(smax_done, u - 1)
                    scores(u)
                if u >= 6 and (u - 2) % 4 == 0:
                    i = (u - 2) // 4 - 1
                    pe.wait_ge(pt_lo_done, 4 * (i + 1))
                    if i >= 2:
                        pe.wait_ge(ya_done, i - 1)
                    weigh(i)
                if 2 <= u <= UNITS + 1:
                    w = u - 2
                    pe.wait_ge(p_done, w + 1)
                    if w >= 1:
                        pe.wait_ge(pt_lo_done, w)
                    else:
                        pe.wait_ge(nope_lo, 12)
                    for k in range(NT):
                        mm = nc.tensor.transpose(ps[2][:, k * P:(k + 1) * P], prob[w % 3][:, k * P:(k + 1) * P], ident[:, :])
                    mm.then_inc(pt_done, 1)
            def mix(t, js):
                cols_t = slice(t * P, (t + 1) * P)
                for j in js:
                    e, k = 1 - j // 4, j % 4
                    if t == 0:
                        pe.wait_ge(z_lo_done, j + 1)
                        pe.wait_ge(zp_lo_done, j + 1)
                    for a, b, first, last in ((z_hi, wo_hi, j == 0, False), (z_hi, wo_lo, False, False),
                                              (z_lo, wo_hi, False, j == KT - 1)):
                        for half in range(2):
                            c = slice(half * HALF, (half + 1) * HALF)
                            mm = nc.tensor.matmul(ps[t % 4][:, c], a[e][:, k, cols_t], b[e][:, k, c], start=first, stop=last)
                if js[-1] == KT - 1:
                    mm.then_inc(mix_done, 1)

            for t in range(4):
                if t == 2:
                    pe.wait_ge(pt_lo_done, UNITS)
                if t == 3:
                    pe.wait_ge(ya_done, 2 * HEADS)
                mix(t, range(4))
            for t in range(4):
                mix(t, range(4, 8))
            for t in range(4, NT):
                pe.wait_ge(ln_sum, t - 3)
                mix(t, range(8))

_INS = ["x", "norm1_g", "w_in", "lru_conv_w", "lru_conv_b", "lru_wa", "lru_ba", "lru_wx", "lru_bx", "lru_lambda",
        "sc_conv_w", "w_out", "norm2_g", "w_up", "ffn_conv_w", "w_down", "final_g", "positions_2", "w_in_2",
        "q_norm_g_2", "w_uq_2", "kv_norm_g_2", "w_ukv_2", "pool_w_2", "pool_scale_2", "w_out_2", "ln_g_2", "ln_b_2"]


def kernel(**inputs):
    import numpy as _np
    import concourse.bacc as _bacc
    from concourse import mybir as _mybir
    from concourse.bass_utils import run_bass_kernel_spmd as _run

    nc = _bacc.Bacc("TRN2", target_bir_lowering=False, num_devices=1)
    arrays = {name: _np.ascontiguousarray(inputs[name]) for name in _INS}
    half = ROPE // 2
    one = _np.float32(10000.0) ** (-_np.arange(half, dtype=_np.float32) / _np.float32(half))
    arrays["rope_freq"] = _np.tile(one.astype(_np.float32), P // half).reshape(P, 1)
    args = [nc.dram_tensor(f"in_{name}", a.shape, _mybir.dt.from_np(a.dtype), kind="ExternalInput").ap()
            for name, a in arrays.items()]
    out = nc.dram_tensor("out", (1, SEQ, D), _mybir.dt.float32, kind="ExternalOutput").ap()
    program(nc, *args, out)
    r = _run(nc, [{f"in_{name}": a for name, a in arrays.items()}], core_ids=[0])
    return r.results[0]["out"]
```

```python
from contextlib import ExitStack, contextmanager

import numpy as np
import concourse.bass as bass
from concourse import mybir

P = 128
SEQ = 1024
D = 1024
KT = D // P
NT = SEQ // P
LRU_TILES = 8
SC_TILES = 4
FF_TILES = 24
FF_GROUP = 8
GROUPS = FF_TILES // FF_GROUP
HEADS = 4
NOPE, ROPE, VDIM = 128, 64, 128
QK = NOPE + ROPE
Q_TILES, KV_TILES = 4, 2
HALF = 512
EPS = 1e-6
LN_EPS = 1e-5
ALPHA = 2.0 ** 0.25
SCALE = float(QK) ** -0.5
MASKED = -1.0e30
WINDOWS = (2, 4, 8, 16)
TILE = SEQ * 4

V_NORM1, V_CONVW, V_CONVB, V_BA, V_BX, V_LAM = 0, 8, 40, 48, 56, 64
V_SCW, V_NORM2, V_FINAL, V_QN, V_KVN, V_POOL = 72, 84, 92, 100, 104, 106
V_ROWS = 110
FFN_ROWS = 144
V_FFN = V_ROWS
V_POS = V_FFN + FFN_ROWS
V_COLS = V_POS + NT

N_SC = 0
N_LRU = N_SC + 3 * SC_TILES
N_OUT = N_LRU + 2 * LRU_TILES
N_FF = N_OUT + 12
GROUP_BLOCKS = 2 * FF_GROUP + KT
N_IN2 = N_FF + GROUPS * GROUP_BLOCKS
N_POOL = N_IN2 + Q_TILES + KV_TILES
N_GATE = N_POOL + 2 * len(WINDOWS)
N_KR = N_GATE + HEADS
N_UQ = N_KR + 1
N_UKV = N_UQ + 3
N_BLOCKS = N_UKV + 2

UNITS = HEADS * NT

TWO_PI_A = 6.28125
TWO_PI_B = float(np.float32(np.floor((2 * np.pi - 6.28125) * 2 ** 20) / 2 ** 20))
TWO_PI_C = float(np.float32(2 * np.pi - 6.28125 - TWO_PI_B))
ROUND = 12582912.0


class Steps:

    def __init__(self, eng, sem):
        self.eng, self.sem, self.n, self.run = eng, sem, 0, 0

    def __call__(self, instruction):
        instruction.then_inc(self.sem, 1)
        self.n += 1
        self.eng.wait_ge(self.sem, self.n + self.run)

    @contextmanager
    def loop(self, count):
        start, outer, per = self.n, self.run, self.per
        with self.eng.Fori(0, count) as i:
            self.run = outer + i * per
            yield i
        assert self.n == start + per, (self.n - start, per)
        self.n, self.run = start + per * count, outer

    def of(self, per):
        self.per = per
        return self


def program(nc, x, norm1_g, w_in, lru_conv_w, lru_conv_b, lru_wa, lru_ba, lru_wx, lru_bx, lru_lambda,
            sc_conv_w, w_out, norm2_g, w_up, ffn_conv_w, w_down, final_g, positions_2, w_in_2,
            q_norm_g_2, w_uq_2, kv_norm_g_2, w_ukv_2, pool_w_2, pool_scale_2, w_out_2, ln_g_2,
            ln_b_2, rope_freq, out):
    f32, f32r, i32 = mybir.dt.float32, mybir.dt.float32r, mybir.dt.int32
    ALU, ACT = mybir.AluOpType, mybir.ActivationFunctionType
    ctx = ExitStack()
    with ctx:
        base = (nc.sbuf_base + 31) // 32 * 32
        W0, H0 = base, base + 6 * TILE
        X0 = H0 + 16 * TILE
        G0 = X0 + 8 * TILE
        S0 = G0 + 16 * TILE
        C0 = S0 + 5 * TILE

        def at(name, offset, shape, dt=f32):
            return nc.alloc_sbuf_tensor_at(name, [P] + list(shape), dt, offset=offset)

        def tile(name, offset, n, dt=f32, count=None):
            return at(name, offset + n * TILE, [SEQ] if count is None else [count, SEQ], dt)

        w_raw = [tile(f"w_raw{s}", W0, s) for s in range(2)]
        w_hi = [tile(f"w_hi{s}", W0, 2 + s, f32r) for s in range(2)]
        w_lo = [tile(f"w_lo{s}", W0, 4 + s, f32r) for s in range(2)]
        h_hi = tile("h_hi", H0, 0, f32r, 8)
        h_lo = tile("h_lo", H0, 8, f32r, 8)
        xs = tile("xs", X0, 0, f32, 8)
        x_tok = tile("x_tok", G0, 0, f32, 8)
        ysc_hi = tile("ysc_hi", G0, 0, f32r, 4)
        ysc_lo = tile("ysc_lo", G0, 4, f32r, 4)
        bd_raw = at("bd_raw", G0 + 8 * TILE, [2, LRU_TILES, P])
        bd_hi = at("bd_hi", G0 + 10 * TILE, [2, P], f32r)
        bd_lo = at("bd_lo", G0 + 11 * TILE, [2, P], f32r)
        xc_hi = tile("xc_hi", G0, 12, f32r)
        xc_lo = tile("xc_lo", G0, 13, f32r)
        root = tile("root", G0, 14)
        gelu_gate = tile("gelu_gate", G0, 15)
        gelu_last = tile("gelu_last", G0, 8)
        square_dve = tile("square_dve", G0, 15)
        gu_hi = tile("gu_hi", G0, 0, f32r, 8)
        gu_lo = tile("gu_lo", G0, 8, f32r, 8)
        lat = tile("lat", G0, 0, f32, 6)
        qn_hi = tile("qn_hi", X0, 4, f32r, 4)
        qn_lo = tile("qn_lo", G0, 0, f32r, 4)
        kvn_lo = tile("kvn_lo", G0, 4, f32r, 2)
        kvn_hi = tile("kvn_hi", G0, 6, f32r, 2)
        acc_q = tile("acc_q", G0, 8)
        acc_kv = tile("acc_kv", G0, 9)
        pw_raw = at("pw_raw", G0 + 10 * TILE, [4, P])
        pw_hi = at("pw_hi", G0 + 10 * TILE + 2048, [P], f32r)
        pw_lo = at("pw_lo", G0 + 10 * TILE + 2560, [P], f32r)
        pooled_hi = tile("pooled_hi", G0, 11, f32r)
        pooled_lo = tile("pooled_lo", G0, 12, f32r)
        square2 = tile("square2", G0, 13)
        y_pool = tile("y_pool", X0, 0, f32, 4)
        sin_t = tile("sin_t", G0, 14)
        cos_t = tile("cos_t", G0, 15)
        pt_hi = at("pt_hi", G0, [NT, HALF], f32r)
        pt_lo = at("pt_lo", G0 + 4 * TILE, [NT, HALF], f32r)
        kr_hi = tile("kr_hi", G0, 8, f32r)
        kr_lo = tile("kr_lo", G0, 9, f32r)
        qr = tile("qr", G0, 10, f32r, 4)
        kn_hi = tile("kn_hi", X0, 0, f32r, 4)
        kn_lo = tile("kn_lo", X0, 4, f32r, 4)
        v_hi = at("v_hi", H0, [NT, HEADS * VDIM], f32r)
        v_lo = at("v_lo", H0 + 4 * TILE, [NT, HEADS * VDIM], f32r)
        qh_hi = tile("qh_hi", H0, 8, f32r, 4)
        qh_lo = tile("qh_lo", H0, 12, f32r, 4)
        mask = [tile(f"mask{s}", W0, 2 + 2 * s) for s in range(2)]
        prob = [tile(f"prob{s}", W0, place) for s, place in enumerate((0, 1, 3))]
        gate_in = [at(f"gate_in{s}", S0 + s * 2048, [HALF]) for s in range(2)]
        ya_out = [at(f"ya_out{s}", S0 + TILE + s * 2048, [HALF]) for s in range(2)]
        z_hi = [tile("z_hi0", H0, 0, f32r, 4), tile("z_hi1", H0, 8, f32r, 4)]
        z_lo = [tile("z_lo0", H0, 4, f32r, 4), tile("z_lo1", H0, 12, f32r, 4)]
        wo_hi = [tile("wo_hi0", G0, 0, f32r, 4), tile("wo_hi1", X0, 0, f32r, 4)]
        wo_lo = [tile("wo_lo0", G0, 4, f32r, 4), tile("wo_lo1", X0, 4, f32r, 4)]
        zin = [tile(f"zin{i}", *place, f32, 2) for i, place in
               enumerate(((G0, 14), (S0, 2), (G0, 8), (G0, 10), (G0, 12), (G0, 8), (G0, 14), (S0, 2)))]
        resid = tile("resid", W0, 0, f32, 6)
        resid_last = tile("resid_last", G0, 10, f32, 2)
        ln_y = tile("ln_y", G0, 12)
        ln_g = tile("ln_g", S0, 0)
        ln_b = tile("ln_b", S0, 1)
        ln_sq = tile("ln_sq", S0, 2)
        ln_v = [tile(f"ln_v{s}", S0, 3 + s) for s in range(2)]
        scr = [tile(f"scr{s}", S0, s) for s in range(5)]
        pos_f = tile("pos_f", S0, 4)
        pos_i = at("pos_i", S0 + 4 * TILE, [SEQ], i32)
        at_c = [C0]

        def const(name, cols, dt=f32):
            t = at(name, at_c[0], [cols], dt)
            at_c[0] += (cols * 4 + 31) // 32 * 32
            return t

        vec = const("vec", V_COLS)
        ident = const("ident", P)
        meanw = const("meanw", 3)
        rc = const("rc", 16)
        eps = const("eps", 2)
        half_ba = const("half_ba", 8)
        half_bx = const("half_bx", 8)
        half_ps = const("half_ps", 4)
        kh = const("kh", 8)
        kx = const("kx", 8)
        small = const("small", 48)
        rstd = const("rstd", 8)
        freq = const("freq", 1)
        sign = const("sign", 1)
        stat = const("stat", 16)
        assert at_c[0] <= nc.sbuf_usable_end, at_c[0]

        ps = [ctx.enter_context(nc.psum_tensor(f"ps{s}", [P, SEQ], f32)) for s in range(4)]

        x_park = nc.dram_tensor("x_park", (KT, P, SEQ), f32, kind="Internal").ap()
        res_park = nc.dram_tensor("res_park", (NT, P, D), f32, kind="Internal").ap()
        gate_park = nc.dram_tensor("gate_park", (HEADS, P, SEQ), f32, kind="Internal").ap()
        y_park = nc.dram_tensor("y_park", (KT, P, SEQ), f32, kind="Internal").ap()

        def sem(name):
            return ctx.enter_context(nc.semaphore(name))

        rows_in, x_in = sem("rows_in"), [sem(f"x_in{n}") for n in range(4)]
        bd_in, pw_in, pos_in = sem("bd_in"), sem("pw_in"), sem("pos_in")
        w_in_sem = [sem(f"w_loaded{s}") for s in range(2)]
        x_parked, x_back = sem("x_parked"), [sem(f"x_back{s}") for s in range(2)]
        res_parked = [sem(f"res_parked{q}") for q in range(2)]
        gate_parked = [sem(f"gate_parked{q}") for q in range(2)]
        ya_parked = [sem(f"ya_parked{q}") for q in range(2)]
        y_parked = sem("y_parked")
        gate_back = [sem(f"gate_back{s}") for s in range(2)]
        z_loaded = [sem(f"z_loaded{s}") for s in range(4)]
        last_in = sem("last_in")
        stored = [sem(f"stored{q}") for q in range(2)]
        w_hi_done, w_lo_done, block_done = sem("w_hi_done"), sem("w_lo_done"), sem("block_done")
        dve_step, pool_step = sem("dve_step"), sem("pool_step")
        ident_done, bd_zeroed, const_done = sem("ident_done"), sem("bd_zeroed"), sem("const_done")
        sign_done = sem("sign_done")
        pos_f_done, vec_t, vec_done = sem("pos_f_done"), sem("vec_t"), sem("vec_done")
        lam_abs, lam_exp, params_done = sem("lam_abs"), sem("lam_exp"), sem("params_done")
        sumsq_dve = sem("sumsq_dve")
        sumsq, ms_done, root_done, rstd_done, rb_done = (sem("sumsq"), sem("ms_done"),
            sem("root_done"), sem("rstd_done"), sem("rb_done"))
        sq_done, acc_done = sem("sq_done"), sem("acc_done")
        xt_done, xt_copied = sem("xt_done"), sem("xt_copied")
        v_done, hi_done = sem("normed"), sem("normed_hi")
        lo_dve, lo_pool = sem("normed_lo_dve"), sem("normed_lo_pool")
        sc_c, sc_p, sc_base, sc_y, sc_hi, sc_lo = (sem("sc_c"), sem("sc_p"), sem("sc_base"),
            sem("sc_y"), sem("sc_hi"), sem("sc_lo"))
        conv_base, conv_done, xc_hi_done, xc_lo_done = (sem("conv_base"), sem("conv_done"),
            sem("xc_hi_done"), sem("xc_lo_done"))
        bd_hi_done, ri_done, rt_done, it_done = (sem("bd_hi_done"), sem("ri_done"), sem("rt_done"),
            sem("it_done"))
        gelu_done, ex_done, s_done, root_s, y_done = (sem("gelu_done"), sem("ex_done"),
            sem("s_done"), sem("root_s"), sem("y_done"))
        x1_done = sem("x1_done")
        ff_base = [sem(f"ff_base{s}") for s in range(4)]
        ff_conv = [sem(f"ff_conv{s}") for s in range(4)]
        ff_gelu = [sem(f"ff_gelu{q}") for q in range(2)]
        ff_v = [sem(f"ff_v{q}") for q in range(2)]
        ff_hi = [sem(f"ff_hi{q}") for q in range(2)]
        ff_lo = [sem(f"ff_lo{q}") for q in range(2)]
        dn_done = [sem(f"dn_done{s}") for s in range(4)]
        tok_t, tok_copied = sem("tok_t"), sem("tok_copied")
        lat_done, acc_q_done, acc_kv_done = sem("lat_done"), sem("acc_q_done"), sem("acc_kv_done")
        sq2_done = sem("sq2_done")
        red_done, trig_done = sem("red_done"), sem("trig_done")
        u_done, pl_done, pl_hi, pl_lo, pw_hi_done, pool_mm = (sem("u_done"), sem("pl_done"),
            sem("pl_hi"), sem("pl_lo"), sem("pw_hi_done"), sem("pool_mm"))
        gb_done = sem("gb_done")
        th_done, yb_done = sem("th_done"), sem("yb_done")
        ga_th, ga_done = sem("ga_th"), sem("ga_done")
        ms2_done, root2_done, rstd2_done = (sem("ms2_done"), sem("root2_done"),
            sem("rstd2_done"))
        latn_done, latn_hi, latn_lo_d, latn_lo_p = (sem("latn_done"), sem("latn_hi"),
            sem("latn_lo_d"), sem("latn_lo_p"))
        rope_sw, rope_a, rope_v, rope_hi, rope_lo, rope_moved = (sem("rope_sw"),
            sem("rope_a"), sem("rope_v"), sem("rope_hi"), sem("rope_lo"), sem("rope_moved"))
        up_done, nope_hi, nope_lo = sem("up_done"), sem("nope_hi"), sem("nope_lo")
        mask_done = [sem(f"mask_done{q}") for q in range(2)]
        score_done, smax_done, nmax_done, exp_done, inv_done, p_done = (
            sem("score_done"), sem("smax_done"), sem("nmax_done"), sem("exp_done"),
            sem("inv_done"), sem("p_done"))
        pt_done, pt_hi_done, pt_lo_done, pv_done, ya_done = (sem("pt_done"), sem("pt_hi_done"),
            sem("pt_lo_done"), sem("pv_done"), sem("ya_done"))
        z_hi_done, z_lo_done, zp_lo_done, mix_done = (sem("z_hi_done"), sem("z_lo_done"),
            sem("zp_lo_done"), sem("mix_done"))
        ln_sum, ln_mean, ln_ssq, ln_root, ln_out = (sem("ln_sum"), sem("ln_mean"),
            sem("ln_ssq"), sem("ln_root"), sem("ln_out"))

        block = ctx.enter_context(nc.Block())
        rows0, rows1, rows2 = scr[0], scr[1], scr[2]
        pos_rows_i = at("pos_rows_i", S0 + 3 * TILE, [P], i32)
        pos_rows = at("pos_rows", S0 + 3 * TILE + 512, [P])

        def out_parts(t):
            return (slice(0, D),) if t < NT - 1 else (slice(0, HALF), slice(HALF, D))

        @block.sync
        def _(sp):
            x_v = x.rearrange("o (n p) d -> p (o n) d", p=P)
            for n in range(4):
                sp.dma_start(x_tok[:, 2 * n:2 * n + 2, :], x_v[:, 2 * n:2 * n + 2, :]).then_inc(x_in[n], 16)
            row = 0
            for v in (norm1_g.rearrange("o (c p) -> (o c) p", p=P),
                      lru_conv_w.rearrange("o k (c p) -> (o k c) p", p=P),
                      lru_conv_b.rearrange("o (c p) -> (o c) p", p=P),
                      lru_ba.rearrange("o (c p) -> (o c) p", p=P),
                      lru_bx.rearrange("o (c p) -> (o c) p", p=P),
                      lru_lambda.rearrange("o (c p) -> (o c) p", p=P),
                      sc_conv_w.rearrange("o k (c p) -> (o k c) p", p=P),
                      norm2_g.rearrange("o (c p) -> (o c) p", p=P),
                      final_g.rearrange("(c p) -> c p", p=P),
                      q_norm_g_2.rearrange("(c p) -> c p", p=P),
                      kv_norm_g_2.rearrange("(c p) -> c p", p=P),
                      pool_scale_2.rearrange("(c p) -> c p", p=P)):
                n = v.shape[0]
                sp.dma_start(rows0[row:row + n, 0:P], v).then_inc(rows_in, 16)
                row += n
            assert row == V_ROWS
            ffn_rows = ffn_conv_w.rearrange("o k (c p) -> (o k c) p", p=P)
            sp.dma_start(rows1[0:72, 0:P], ffn_rows[0:72, :]).then_inc(rows_in, 16)
            sp.dma_start(rows2[0:72, 0:P], ffn_rows[72:144, :]).then_inc(rows_in, 16)
            sp.dma_start(pos_rows_i[0:NT, :], positions_2.rearrange("o (n p) -> (o n) p", p=P)
                         ).then_inc(rows_in, 16)
            sp.dma_start(freq[:, :], rope_freq).then_inc(rows_in, 16)

            def load(n, h, *views):
                if n >= 2:
                    sp.wait_ge(w_lo_done, n - 1 + 2 * h)
                for dst, src in views:
                    sp.dma_start(dst, src).then_inc(w_in_sem[n % 2], 16)

            def cols(n, k, w):
                return w_raw[n % 2][:, 0:k * w].rearrange("p (k n) -> p k n", n=w)

            w_in_v = w_in.rearrange("o (k p) n -> p (o k) n", p=P)
            sc0 = 2 * LRU_TILES * P
            for j in range(SC_TILES):
                for b, part in enumerate((1, 2, 0)):
                    n = N_SC + 3 * j + b
                    load(n, 0, (cols(n, 8, P), w_in_v[:, :, sc0 + part * 512 + j * P:sc0 + part * 512 + (j + 1) * P]))
                if j == 0:
                    sp.wait_ge(bd_zeroed, 1)
                    for which, wg in enumerate((lru_wa, lru_wx)):
                        heads = wg.rearrange("o (c e) i j -> (o e) i c j", e=2)
                        for e in range(2):
                            sp.dma_start(bd_raw[64 * e:64 * e + 64, which, :, 64 * e:64 * e + 64],
                                         heads[e]).then_inc(bd_in, 16)
            sp.wait_ge(xt_copied, NT)
            sp.dma_start(x_park.rearrange("c p t -> p c t"), xs[:, :, :]).then_inc(x_parked, 16)
            with sp.Fori(0, LRU_TILES) as c:
                for b in range(2):
                    load(N_LRU + b, c, (cols(b, 8, P), w_in_v[:, :, bass.ds(b * D + c * P, P)]))
            w_lru = w_out[0, 0:D, :].rearrange("(k p) n -> p k n", p=P)
            w_sc = w_out[0, D:D + 512, :].rearrange("(k p) n -> p k n", p=P)
            sp.wait_ge(x_parked, 16)
            with sp.Fori(1, 3) as r1:
                r = r1 - 1
                for b in range(6):
                    src = w_sc[:, :, bass.ds(r1 * 512 - 512 + b * 256, 256)] if b < 2 else \
                        w_lru[:, :, bass.ds(r1 * 512 - 512 + (b - 2) * P, P)]
                    load(N_OUT + b, 3 * r, (cols(b, 4, 256) if b < 2 else cols(b, 8, P), src))
                    if b >= 2:
                        if b == 2:
                            sp.wait_ge(y_done, LRU_TILES)
                        s = b % 2
                        sp.wait_ge(x1_done, (3 * r if b == 2 else 4 * r + b - 3) + 1)
                        sp.dma_start(scr[s][:, :], x_park[bass.ds(4 * r + b - 2, 1)].rearrange("o p t -> p (o t)")
                                     ).then_inc(x_back[s], 16)
            w_up_v = w_up.rearrange("o (k p) n -> p (o k) n", p=P)
            w_dn_v = w_down.rearrange("o (k p) n -> p (o k) n", p=P)
            with sp.Fori(0, GROUPS) as g:
                with sp.Fori(0, FF_GROUP // 2) as fp:
                    for b in range(4):
                        col = (b % 2) * 3072 + g * (FF_GROUP * P) + fp * 256 + (b // 2) * P
                        load(N_FF + b, g * (GROUP_BLOCKS // 2) + fp * 2,
                             (cols(b, 8, P), w_up_v[:, :, bass.ds(col, P)]))
                with sp.Fori(0, 2) as dp:
                    for b in range(4):
                        load(N_FF + 2 * FF_GROUP + b, g * (GROUP_BLOCKS // 2) + dp * 2,
                             (cols(b, 8, P), w_dn_v[:, bass.ds(g * FF_GROUP, FF_GROUP), bass.ds(dp * 512 + b * P, P)]))
            w2_v = w_in_2.rearrange("(k p) n -> p k n", p=P)
            order = [i * P for i in range(Q_TILES + KV_TILES)]
            for g in range(4):
                order += [1344 + g * P, 1856 + g * P]
            order += [832 + h * P for h in range(HEADS)]
            for i, col in enumerate(order):
                n = N_IN2 + i
                load(n, 0, (cols(n, 8, P), w2_v[:, :, col:col + P]))
                if i == 2:
                    sp.wait_ge(block_done, N_IN2)
                    sp.dma_start(pw_raw[:, :, :], pool_w_2.rearrange("g c d -> c g d")).then_inc(pw_in, 16)
                    sp.wait_ge(ms_done, 2)
                    sp.dma_start(pos_i[:, :], positions_2.broadcast_to([P, SEQ])).then_inc(pos_in, 16)
            n = N_KR
            load(n, 0, (cols(n, 8, P)[:, :, 0:64], w2_v[:, :, 768:832]),
                 (cols(n, 8, P)[:, :, 64:128], w2_v[:, :, 768:832]))
            uq = w_uq_2.rearrange("(k p) (h n) -> p k h n", p=P, h=HEADS)
            n = N_UQ
            dst = w_raw[n % 2][:, :].rearrange("p (k h n) -> p k h n", k=4, h=HEADS)
            load(n, 0, *[(dst[:, :, h, :], uq[:, :, h, NOPE:QK]) for h in range(HEADS)])
            for b in range(2):
                n = N_UQ + 1 + b
                dst = w_raw[n % 2][:, :].rearrange("p (k h n) -> p k h n", k=4, h=2)
                load(n, 0, *[(dst[:, :, e, :], uq[:, :, 2 * b + e, 0:NOPE]) for e in range(2)])
            ukv = w_ukv_2.rearrange("(k p) (h e n) -> p k h e n", p=P, h=HEADS, e=2)
            for part in range(2):
                n = N_UKV + part
                dst = w_raw[n % 2][:, :].rearrange("p (k h n) -> p k h n", k=2, h=HEADS)
                load(n, 0, *[(dst[:, k], ukv[:, k, :, part, :]) for k in range(2)])
            def z_load(i):
                k = (i // 2 * 2 + 4) % 8
                src = w_out_2.rearrange("(k p) n -> p k n", p=P) if i % 2 == 0 else y_park.rearrange("k p t -> p k t")
                sp.dma_start(zin[i][:, :, :], src[:, k:k + 2, :]).then_inc(z_loaded[i % 4], 16)

            for q in range(2):
                sp.wait_ge(gate_parked[q], 16 * HEADS // 2)
            sp.wait_ge(rope_moved, 4)
            sp.wait_ge(y_parked, 16 * 4)
            for i in range(2 * HEADS):
                if i >= 2:
                    sp.wait_ge(ya_done, i - 1)
                sp.dma_start(gate_in[i % 2][:, :], gate_park[i // 2][:, (i % 2) * HALF:(i % 2 + 1) * HALF]
                             ).then_inc(gate_back[i % 2], 16)
                if i >= 1:
                    j = i - 1
                    sp.wait_ge(ya_done, j + 1)
                    sp.dma_start(y_park[j // 2][:, (j % 2) * HALF:(j % 2 + 1) * HALF], ya_out[j % 2][:, :]
                                 ).then_inc(ya_parked[j % 2], 16)
                if i in (1, 2):
                    z_load(i - 1)
            sp.wait_ge(score_done, UNITS)
            for i in (2, 3, 4):
                z_load(i)
            j = 2 * HEADS - 1
            sp.wait_ge(ya_done, j + 1)
            sp.dma_start(y_park[j // 2][:, (j % 2) * HALF:(j % 2 + 1) * HALF], ya_out[j % 2][:, :]
                         ).then_inc(ya_parked[j % 2], 16)
            sp.wait_ge(z_lo_done, 4)
            for q in range(2):
                sp.wait_ge(ya_parked[q], 16 * 2)
            z_load(5)
            z_load(6)
            for q in range(2):
                sp.wait_ge(ya_parked[q], 16 * HEADS)
            sp.wait_ge(zp_lo_done, 2)
            z_load(7)
            for q in range(2):
                sp.wait_ge(res_parked[q], 16 * NT // 2)
            sp.wait_ge(pt_done, UNITS)
            sp.dma_start(resid[:, :, :], res_park[0:6].rearrange("n p d -> p n d")).then_inc(last_in, 16)
            sp.dma_start(ln_g[:, :], ln_g_2.broadcast_to([P, D])).then_inc(last_in, 16)
            sp.dma_start(ln_b[:, :], ln_b_2.broadcast_to([P, D])).then_inc(last_in, 16)
            sp.wait_ge(zp_lo_done, 4)
            sp.dma_start(resid_last[:, :, :], res_park[6:8].rearrange("n p d -> p n d")).then_inc(last_in, 16)
            out_v = out.rearrange("o (n p) d -> (o n) p d", p=P)
            for t in range(NT):
                for i, c in enumerate(out_parts(t)):
                    sp.wait_ge(ln_out, t + i + 1)
                    sp.dma_start(out_v[t][:, c], ln_v[t % 2][:, c]).then_inc(stored[t % 2], 16)
            sp.wait_ge(stored[0], 16 * NT // 2)
            sp.wait_ge(stored[1], 16 * (NT // 2 + 1))

        def latents():
            return [(kvn_hi[:, i, :], kvn_lo[:, i, :]) for i in range(KV_TILES)] + \
                   [(qn_hi[:, i, :], qn_lo[:, i, :]) for i in range(Q_TILES)]

        def lat_tile(i):
            return lat[:, (i + Q_TILES) % (Q_TILES + KV_TILES), :]

        def z_tiles(n):
            j = n // 2
            k = (j + 4) % 8
            return k // 4, k % 4, zin[j // 2 * 2 + n % 2][:, j % 2, :]

        UP_ENDS = (1, 3, 5, 9, 13)

        def up_ready(j):
            if j in UP_ENDS:
                return block_done, read(N_UQ + UP_ENDS.index(j))
            return up_done, j + 1 - sum(end < j for end in UP_ENDS)

        def raw_loads(n):
            parts = {N_KR: 2, N_UQ: 4, N_UQ + 1: 2, N_UQ + 2: 2, N_UKV: 2, N_UKV + 1: 2}
            return n // 2 + 1 + sum(k - 1 for m, k in parts.items() if m <= n and m % 2 == n % 2)

        def read(n, h=0):
            return n + 1 + 2 * h

        def matmul3(pe, out_ap, w_h, w_l, x_h, x_l, first, last):
            halves = [slice(0, HALF), slice(HALF, SEQ)]
            for w, x, a, b in ((w_h, x_h, first, False), (w_h, x_l, False, False),
                               (w_l, x_h, False, last)):
                for t in halves:
                    mm = nc.tensor.matmul(out_ap[:, t], w, x[:, t], start=a, stop=b)
            return mm

        @block.gpsimd
        def _(pool):
            step = Steps(pool, pool_step)
            for free in (acc_done, *ff_lo):
                nc.gpsimd.sem_inc(free, 1)
            step(nc.gpsimd.memset(ident[:, :], 0.0))
            nc.gpsimd.affine_select(out=ident[:, :], in_=ident[:, :], compare_op=ALU.not_equal, fill=1.0,
                                    base=0, pattern=[[-1, P]], channel_multiplier=1).then_inc(ident_done, 1)
            nc.gpsimd.memset(bd_raw[:, :, :, :], 0.0).then_inc(bd_zeroed, 1)
            for i, n in enumerate((D, Q_TILES * P, KV_TILES * P)):
                nc.gpsimd.memset(meanw[:, i:i + 1], 1.0 / n).then_inc(const_done, 1)
            nc.gpsimd.memset(eps[:, 0:1], EPS).then_inc(const_done, 1)
            nc.gpsimd.memset(eps[:, 1:2], LN_EPS).then_inc(const_done, 1)
            for t in range(16):
                nc.gpsimd.memset(rc[:, t:t + 1], 1.0 / (t + 1)).then_inc(const_done, 1)

            def low(n, h=0):
                if n >= N_BLOCKS:
                    return
                s = n % 2
                pool.wait_ge(w_hi_done, n + 1 + 2 * h)
                nc.gpsimd.tensor_tensor(w_lo[s][:, :], w_raw[s][:, :], w_hi[s][:, :].bitcast(f32),
                                        ALU.subtract).then_inc(w_lo_done, 1)

            def odd_lows(i, src):
                for c in range(1, KT, 2):
                    pool.wait_ge(hi_done, 8 * i + c + 1)
                    nc.gpsimd.tensor_tensor(h_lo[:, c, :], src(c), h_hi[:, c, :].bitcast(f32),
                                            ALU.subtract).then_inc(lo_pool, 1)

            low(0)
            low(1)
            odd_lows(0, lambda c: scr[c % 4][:, :])
            for j in range(SC_TILES):
                low(3 * j + 2)
                low(3 * j + 3)
                low(3 * j + 4)
                pool.wait_ge(sc_hi, j + 1)
                nc.gpsimd.tensor_tensor(ysc_lo[:, j, :], scr[3][:, :], ysc_hi[:, j, :].bitcast(f32),
                                        ALU.subtract).then_inc(sc_lo, 1)
            with pool.Fori(0, LRU_TILES) as c:
                low(N_LRU + 2, c)
                low(N_LRU + 3, c)
            def y_low(c):
                pool.wait_ge(hi_done, 8 + c + 1)
                nc.gpsimd.tensor_tensor(h_lo[:, c, :], xs[:, c, :], h_hi[:, c, :].bitcast(f32),
                                        ALU.subtract).then_inc(lo_pool, 1)

            for c in (1, 3, 5):
                y_low(c)
            low(N_OUT + 2)
            y_low(6)
            pool.wait_ge(y_done, LRU_TILES)
            for s in (3, 4):
                nc.gpsimd.memset(scr[s][:, :], 0.0).then_inc(acc_done, 1)
            for r in range(2):
                for b in range(6):
                    if (r, b) != (0, 0):
                        low(N_OUT + b + 2, 3 * r)
            odd_lows(2, lambda c: scr[c % 4][:, :])

            def ff_up(g, h0):
                with pool.Fori(0, FF_GROUP // 2) as fp:
                    for q in range(2):
                        low(N_FF + 2 * q + 2, h0 + 2 * fp)
                        low(N_FF + 2 * q + 3, h0 + 2 * fp)
                        pool.wait_ge(ff_hi[q], 4 * g + fp + 1)
                        f = bass.ds(2 * fp + q, 1)
                        nc.gpsimd.tensor_tensor(gu_lo[:, f, :], scr[2 + q][:, :].unsqueeze(1), gu_hi[:, f, :].bitcast(f32),
                                                ALU.subtract).then_inc(ff_lo[q], 1)

            with pool.Fori(0, GROUPS - 1) as g:
                ff_up(g, 12 * g)
                with pool.Fori(0, 2) as dp:
                    for b in range(4):
                        low(N_FF + 16 + b + 2, 12 * g + 2 * dp)
            g = GROUPS - 1
            ff_up(g, 12 * g)
            pool.wait_ge(lo_dve, 12)
            pool.wait_ge(ff_lo[1], 4 * GROUPS + 1)
            for tile_s in (3, 4):
                nc.gpsimd.memset(scr[tile_s][:, :], 0.0).then_inc(acc_done, 1)
            with pool.Fori(0, 2) as dp:
                for b in range(4):
                    low(N_FF + 16 + b + 2, 12 * g + 2 * dp)
            odd_lows(3, lambda c: xs[:, c, :])
            nc.gpsimd.memset(acc_q[:, :], 0.0).then_inc(acc_q_done, 1)
            nc.gpsimd.memset(acc_kv[:, :], 0.0).then_inc(acc_kv_done, 1)
            for i in range(Q_TILES + KV_TILES):
                low(N_IN2 + i + 2)
                pool.wait_ge(sq2_done, i + 1)
                acc, done, k = (acc_q, acc_q_done, i) if i < Q_TILES else (acc_kv, acc_kv_done, i - Q_TILES)
                pool.wait_ge(done, k + 1)
                nc.gpsimd.tensor_tensor(acc[:, :], acc[:, :], square2[:, :], ALU.add).then_inc(done, 1)
            for g in range(len(WINDOWS)):
                low(N_POOL + 2 * g + 2)
                low(N_POOL + 2 * g + 3)
                pool.wait_ge(pl_hi, g + 1)
                nc.gpsimd.tensor_tensor(pooled_lo[:, :], scr[3][:, :], pooled_hi[:, :].bitcast(f32),
                                        ALU.subtract).then_inc(pl_lo, 1)
            for h in range(HEADS):
                low(N_GATE + h + 2)
                if h == 1:
                    for i, (hi, lo) in enumerate(latents()):
                        if i % 2 == 1:
                            pool.wait_ge(latn_hi, i + 1)
                            nc.gpsimd.tensor_tensor(lo, lat_tile(i), hi.bitcast(f32), ALU.subtract).then_inc(latn_lo_p, 1)
            for n in range(N_KR, N_BLOCKS):
                low(n + 2)
            pool.wait_ge(block_done, N_BLOCKS - 1)
            def z_second(n):
                pool.wait_ge(z_hi_done, n + 1)
                e, k, raw = z_tiles(n)
                nc.gpsimd.tensor_tensor(z_lo[e][:, k, :], raw, z_hi[e][:, k, :].bitcast(f32),
                                        ALU.subtract).then_inc(zp_lo_done, 1)

            for u in range(1, UNITS, 2):
                if u >= 2:
                    pool.wait_ge(smax_done, u - 1)
                nc.gpsimd.tensor_scalar(mask[1][:, :], pos_f[:, :], vec[:, V_POS + u % NT:V_POS + u % NT + 1],
                                        MASKED, ALU.is_gt, ALU.mult).then_inc(mask_done[1], 1)
                if u in (19, 27):
                    z_second(1 if u == 19 else 3)
            for n in range(5, 16, 2):
                z_second(n)

        @block.scalar
        def _(act):
            def col(c):
                return vec[:, c:c + 1] if isinstance(c, int) else vec[:, bass.ds(c, 1)]

            def high(n, h=0):
                if n >= N_BLOCKS:
                    return
                s = n % 2
                act.wait_ge(w_in_sem[s], 16 * raw_loads(n) + 16 * h)
                if n >= 2:
                    act.wait_ge(block_done, n - 1 + 2 * h)
                nc.scalar.copy(w_hi[s][:, :], w_raw[s][:, :]).then_inc(w_hi_done, 1)

            def highs(src, waits):
                for c in range(KT):
                    act.wait_ge(*waits(c))
                    nc.scalar.copy(h_hi[:, c, :], src(c)).then_inc(hi_done, 1)

            nc.scalar.sem_inc(sq_done, 1)

            def xt_copy(t):
                act.wait_ge(xt_done, t + 1)
                nc.scalar.copy(xs[:, :, t * P:(t + 1) * P], ps[t % 3][:, :].rearrange("p (c q) -> p c q", c=KT)
                               ).then_inc(xt_copied, 1)

            for t in range(NT - 2):
                xt_copy(t)
            act.wait_ge(x_in[3], 16)
            nc.scalar.activation(scr[4][:, :], x_tok[:, NT - 1, :], ACT.Square,
                                 accum_out=small[:, NT - 1:NT]).then_inc(sumsq, 1)
            act.wait_ge(sumsq, 1)
            act.wait_ge(sumsq_dve, NT - 1)
            act.wait_ge(const_done, 5)
            nc.scalar.activation(small[:, 8:16], small[:, 0:8], ACT.Sqrt, bias=eps[:, 0:1],
                                 scale=1.0 / D).then_inc(root_done, 1)
            xt_copy(NT - 2)
            xt_copy(NT - 1)
            act.wait_ge(vec_t, 1)
            nc.scalar.copy(vec[:, :], ps[3][:, 0:V_COLS]).then_inc(vec_done, 1)
            high(0)
            high(1)
            highs(lambda c: scr[c % 4][:, :], lambda c: (v_done, c + 1))
            act.wait_ge(lam_abs, 1)
            nc.scalar.activation(small[:, 24:32], small[:, 16:24], ACT.Exp).then_inc(lam_exp, 1)

            for j in range(SC_TILES):
                act.wait_ge(block_done, read(3 * j))
                if j >= 1:
                    act.wait_ge(sc_p, j)
                nc.scalar.copy(scr[0][:, :], ps[(3 * j) % 4][:, :]).then_inc(sc_c, 1)
                high(3 * j + 2)
                high(3 * j + 3)
                act.wait_ge(sc_p, j + 1)
                if j >= 1:
                    act.wait_ge(sc_y, j)
                nc.scalar.activation(scr[2][:, :], scr[1][:, :], ACT.Identity,
                                     scale=col(V_SCW + 8 + j)).then_inc(sc_base, 1)
                high(3 * j + 4)
                act.wait_ge(sc_y, j + 1)
                nc.scalar.copy(ysc_hi[:, j, :], scr[3][:, :]).then_inc(sc_hi, 1)

            act.wait_ge(params_done, 1)
            act.wait_ge(bd_in, 64)
            act.wait_ge(sc_lo, SC_TILES)
            act.wait_ge(x_parked, 16)

            def conv_first(c, one):
                act.wait_ge(block_done, read(N_LRU, c))
                nc.scalar.activation(xs[:, one, :], ps[0][:, :].unsqueeze(1), ACT.Identity,
                                     scale=col(V_CONVW + 24 + c), bias=col(V_CONVB + c)).then_inc(conv_base, 1)
                high(N_LRU + 2, c)

            def gate_weights(c, one):
                nc.scalar.copy(bd_hi[:, :, :], bd_raw[:, :, one, :].rearrange("p w o n -> p w (o n)")
                               ).then_inc(bd_hi_done, 1)

            def gate_curves(c, one):
                act.wait_ge(ri_done, 2 * c + 1)
                nc.scalar.activation(scr[1][:, :], ps[2][:, :], ACT.Tanh, scale=0.5,
                                     bias=half_ba[:, one]).then_inc(rt_done, 1)
                act.wait_ge(ri_done, 2 * c + 2)
                nc.scalar.activation(scr[2][:, :], ps[3][:, :], ACT.Tanh, scale=0.5,
                                     bias=half_bx[:, one]).then_inc(it_done, 1)
                act.wait_ge(rt_done, c + 1)
                nc.scalar.activation(scr[4][:, :], scr[1][:, :], ACT.Tanh, scale=kh[:, one],
                                     bias=kh[:, one]).then_inc(s_done, 1)
                nc.scalar.activation(scr[3][:, :], scr[1][:, :], ACT.Exp, scale=kx[:, one],
                                     bias=kx[:, one]).then_inc(ex_done, 1)
                act.wait_ge(s_done, c + 1)
                nc.scalar.activation(root[:, :], scr[4][:, :], ACT.Sqrt).then_inc(root_s, 1)

            def conv_high(one):
                nc.scalar.copy(xc_hi[:, :].unsqueeze(1), xs[:, one, :]).then_inc(xc_hi_done, 1)

            def gate_gelu(c, one):
                act.wait_ge(conv_done, c + 1)
                if one is last:
                    conv_high(one)
                act.wait_ge(block_done, read(N_LRU + 1, c))
                high(N_LRU + 3, c)
                if one is not last:
                    conv_high(one)
                if one is last:
                    act.wait_ge(xc_lo_done, c + 1)
                elif one is not first:
                    act.wait_ge(y_done, c)
                gelu = gelu_last if one is last else gelu_gate
                nc.scalar.activation(gelu[:, :], ps[1][:, :], ACT.Gelu_apprx_tanh).then_inc(gelu_done, 1)

            first, last = slice(0, 1), slice(LRU_TILES - 1, LRU_TILES)
            conv_first(0, first)
            gate_weights(0, first)
            gate_gelu(0, first)
            with act.Fori(1, LRU_TILES - 1) as c:
                conv_first(c, bass.ds(c, 1))
                gate_curves(c - 1, bass.ds(c - 1, 1))
                gate_weights(c, bass.ds(c, 1))
                gate_gelu(c, bass.ds(c, 1))
            c = LRU_TILES - 1
            conv_first(c, last)
            gate_curves(c - 1, slice(c - 1, c))
            gate_weights(c, last)
            gate_gelu(c, last)

            def y_high(c):
                act.wait_ge(y_done, c + 1)
                nc.scalar.copy(h_hi[:, c, :], xs[:, c, :]).then_inc(hi_done, 1)

            act.wait_ge(block_done, N_OUT)
            for i in range(KT - 2):
                y_high(i)
            act.wait_ge(y_done, c)
            gate_curves(c, last)
            y_high(KT - 2)
            act.wait_ge(block_done, read(N_OUT))
            high(N_OUT + 2)
            y_high(KT - 1)

            for r in range(2):
                for b in range(6):
                    if (r, b) != (0, 0):
                        act.wait_ge(block_done, read(N_OUT + b, 3 * r))
                        high(N_OUT + b + 2, 3 * r)
                    if b >= 2:
                        act.wait_ge(x1_done, 4 * r + b - 1 + 1)
                        act.wait_ge(acc_done, 4 * r + b + 1)
                        nc.scalar.activation(scr[2 + b % 2][:, :].unsqueeze(1), xs[:, 4 * r + b - 2:4 * r + b - 1, :],
                                             ACT.Square).then_inc(sq_done, 1)

            def norm_root(i):
                act.wait_ge(ms_done, i)
                nc.scalar.activation(small[:, 8:16], ps[2][:, 0:NT], ACT.Sqrt, bias=eps[:, 0:1]
                                     ).then_inc(root_done, 1)

            norm_root(1)
            highs(lambda c: scr[c % 4][:, :], lambda c: (v_done, 8 + c + 1))
            act.wait_ge(lo_dve, 12)
            act.wait_ge(lo_pool, 12)

            def ff_up(g, h0):
                with act.Fori(0, FF_GROUP // 2) as fp:
                    for q in range(2):
                        n, h, turn = N_FF + 2 * q, h0 + 2 * fp, 4 * g + fp
                        f = 8 * g + 2 * fp + q
                        act.wait_ge(block_done, read(n, h))
                        act.wait_ge(ff_v[q], turn + 1)
                        nc.scalar.activation(scr[q][:, :], ps[2 * q][:, :], ACT.Identity,
                                             scale=col(V_FFN + 96 + f)).then_inc(ff_base[2 * q], 1)
                        high(n + 2, h)
                        act.wait_ge(block_done, read(n + 1, h))
                        act.wait_ge(ff_lo[q], turn + 1)
                        nc.scalar.activation(scr[2 + q][:, :], ps[2 * q + 1][:, :], ACT.Identity,
                                             scale=col(V_FFN + 96 + 24 + f)).then_inc(ff_base[2 * q + 1], 1)
                        high(n + 3, h)
                        act.wait_ge(ff_conv[2 * q], turn + 1 + 1)
                        nc.scalar.activation(scr[q][:, :], scr[q][:, :], ACT.Gelu_apprx_tanh).then_inc(ff_gelu[q], 1)
                        act.wait_ge(ff_v[q], turn + 1 + 1)
                        nc.scalar.copy(gu_hi[:, bass.ds(2 * fp + q, 1), :], scr[2 + q][:, :].unsqueeze(1)
                                       ).then_inc(ff_hi[q], 1)

            with act.Fori(0, GROUPS - 1) as g:
                ff_up(g, 12 * g)
                with act.Fori(0, 2) as dp:
                    for b in range(4):
                        act.wait_ge(block_done, read(N_FF + 16 + b, 12 * g + 2 * dp))
                        high(N_FF + 16 + b + 2, 12 * g + 2 * dp)
            g = GROUPS - 1
            ff_up(g, 12 * g)
            for q in range(2):
                act.wait_ge(ff_lo[q], 4 * GROUPS + 1)
            with act.Fori(0, 2) as dp:
                for b in range(4):
                    act.wait_ge(block_done, read(N_FF + 16 + b, 12 * g + 2 * dp))
                    high(N_FF + 16 + b + 2, 12 * g + 2 * dp)
                    act.wait_ge(dn_done[b], 2 * g + dp + 1 + 1)
                    act.wait_ge(acc_done, 14 + 4 * dp + b)
                    nc.scalar.activation(scr[2 + b % 2][:, :].unsqueeze(1), xs[:, bass.ds(4 * dp + b, 1), :],
                                         ACT.Square).then_inc(sq_done, 1)
            norm_root(2)
            highs(lambda c: xs[:, c, :], lambda c: (v_done, 16 + c + 1))

            def park_residual(t):
                act.wait_ge(tok_t, t + 1)
                if t >= 2:
                    act.wait_ge(res_parked[t % 2], 16 * (t // 2))
                nc.scalar.mul(scr[t % 2][:, :], ps[2 + t % 2][:, :], ALPHA).then_inc(tok_copied, 1)
                act.wait_ge(tok_copied, t + 1)
                act.dma_start(res_park[t], scr[t % 2][:, :]).then_inc(res_parked[t % 2], 16)

            for i in range(Q_TILES + KV_TILES):
                act.wait_ge(block_done, read(N_IN2 + i))
                high(N_IN2 + i + 2)
                act.wait_ge(lat_done, i + 1)
                if i >= 1:
                    act.wait_ge(acc_q_done if i <= Q_TILES else acc_kv_done,
                                i + 1 if i <= Q_TILES else i - Q_TILES + 1)
                nc.scalar.activation(square2[:, :], lat[:, i, :], ACT.Square).then_inc(sq2_done, 1)
                if 1 <= i <= NT // 2:
                    park_residual(2 * i - 2)
                    park_residual(2 * i - 1)
                if i == 2:
                    act.wait_ge(red_done, 2)
                    act.wait_ge(sign_done, 4)
                    nc.scalar.activation(sin_t[:, :], sin_t[:, :], ACT.Sin, scale=sign[:, 0:1]).then_inc(trig_done, 1)
                    nc.scalar.activation(cos_t[:, :], cos_t[:, :], ACT.Sin).then_inc(trig_done, 1)
            act.wait_ge(pw_in, 16)
            act.wait_ge(acc_kv_done, KV_TILES + 1)

            def park_pooled(g):
                act.wait_ge(yb_done, g + 1)
                act.dma_start(y_park[4 + g], y_pool[:, g, :]).then_inc(y_parked, 16)

            for g in range(len(WINDOWS)):
                act.wait_ge(block_done, read(N_POOL + 2 * g))
                high(N_POOL + 2 * g + 2)
                if g >= 1:
                    act.wait_ge(pool_mm, g)
                nc.scalar.copy(pw_hi[:, :], pw_raw[:, g, :]).then_inc(pw_hi_done, 1)
                act.wait_ge(pl_done, g + 1)
                nc.scalar.copy(pooled_hi[:, :], scr[3][:, :]).then_inc(pl_hi, 1)
                if g < 2:
                    act.wait_ge(ms2_done, g + 1)
                    nc.scalar.activation((acc_q, acc_kv)[g][:, :], ps[3][:, :], ACT.Sqrt, bias=eps[:, 0:1]
                                         ).then_inc(root2_done, 1)
                act.wait_ge(block_done, read(N_POOL + 2 * g + 1))
                nc.scalar.activation(y_pool[:, g, :], ps[1][:, :], ACT.Tanh, scale=0.5).then_inc(th_done, 1)
                high(N_POOL + 2 * g + 3)
                if g >= 1:
                    park_pooled(g - 1)

            def gate(h):
                act.wait_ge(block_done, read(N_GATE + h))
                if h >= 2:
                    act.wait_ge(gate_parked[h % 2], 16 * (h // 2))
                nc.scalar.activation(scr[h % 2][:, :], ps[h % 2][:, :], ACT.Tanh, scale=0.5).then_inc(ga_th, 1)
                high(N_GATE + h + 2)
                act.wait_ge(ga_done, h + 1)
                act.dma_start(gate_park[h], scr[h % 2][:, :]).then_inc(gate_parked[h % 2], 16)

            gate(0)
            park_pooled(3)
            gate(1)
            for i, (hi, lo) in enumerate(latents()):
                act.wait_ge(latn_done, i + 1)
                nc.scalar.copy(hi, lat_tile(i)).then_inc(latn_hi, 1)
            gate(2)
            gate(3)
            for q in range(2):
                act.wait_ge(gate_parked[q], 16 * HEADS // 2)

            swapped = (scr[1], scr[3], scr[1])

            def swap_halves(r, src):
                if r == 2:
                    act.wait_ge(rope_v, 1)
                for q in range(4):
                    p = q ^ 1
                    nc.scalar.copy(swapped[r][32 * q:32 * q + 32, :], src[32 * p:32 * p + 32, :]).then_inc(rope_sw, 1)

            def rotated_queries(r):
                heads = ((slice(0, 64), 2 * r - 2), (slice(64, P), 2 * r - 1))
                act.wait_ge(rope_v, r + 1)
                for half, h in heads:
                    nc.scalar.copy(qr[half, h, :], scr[2][half, :]).then_inc(rope_hi, 1)
                act.wait_ge(rope_lo, r + 1)
                for (half, h), (other, _) in zip(heads, heads[::-1]):
                    nc.scalar.copy(qr[other, h, :], swapped[r][half, :]).then_inc(rope_moved, 1)

            def up_high(j, dst, **split):
                act.wait_ge(*up_ready(j))
                src = ps[(j + 1) % 4][:, :]
                nc.scalar.copy(dst, src.rearrange("p (t d) -> p t d", t=2) if split else src).then_inc(nope_hi, 1)

            act.wait_ge(block_done, read(N_KR))
            high(N_KR + 2)
            swap_halves(0, ps[0])
            act.wait_ge(*up_ready(0))
            swap_halves(1, ps[1])
            act.wait_ge(rope_v, 1)
            nc.scalar.copy(kr_hi[:, :], scr[2][:, :]).then_inc(rope_hi, 1)
            act.wait_ge(block_done, read(N_UQ))
            high(N_UQ + 2)
            swap_halves(2, ps[2])
            rotated_queries(1)
            act.wait_ge(block_done, read(N_UQ + 1))
            high(N_UQ + 3)
            rotated_queries(2)
            for h in range(HEADS):
                up_high(2 + h, qh_hi[:, h, :])
                if h == 1:
                    act.wait_ge(block_done, read(N_UQ + 2))
                    high(N_UQ + 4)
            act.wait_ge(y_parked, 16 * 4)
            for h in range(HEADS):
                up_high(6 + h, kn_hi[:, h, :])
            for i in range(4):
                up_high(10 + i, v_hi[:, 2 * i:2 * i + 2, :], token_pairs=True)

            def z_high(n):
                i = n // 4 * 2 + n % 2
                act.wait_ge(z_loaded[i % 4], 16 * (i // 4 + 1))
                e, k, raw = z_tiles(n)
                nc.scalar.copy((wo_hi if n % 2 == 0 else z_hi)[e][:, k, :], raw).then_inc(z_hi_done, 1)

            for u in range(UNITS + 2):
                if 1 <= u <= UNITS:
                    s = (u - 1) % 3
                    act.wait_ge(inv_done, u)
                    nc.scalar.activation(prob[s][:, :], prob[s][:, :], ACT.Identity, scale=stat[:, 9 + s:10 + s]
                                         ).then_inc(p_done, 1)
                if u in (14, 18, 22, 26):
                    z_high((u - 14) // 4)
                if u >= 2:
                    w = u - 2
                    act.wait_ge(pt_done, w + 1)
                    q = (w % 4) * P
                    nc.scalar.copy(pt_hi[:, :, q:q + P], ps[2][:, :].rearrange("p (k q) -> p k q", k=NT)
                                   ).then_inc(pt_hi_done, 1)
                if u < UNITS:
                    act.wait_ge(nmax_done, u + 1)
                    nc.scalar.activation(prob[u % 3][:, :], prob[u % 3][:, :], ACT.Exp,
                                         bias=stat[:, 3 + u % 3:4 + u % 3], scale=SCALE,
                                         accum_out=stat[:, 6 + u % 3:7 + u % 3]).then_inc(exp_done, 1)
            for n in range(4, 16):
                if n == 8:
                    act.wait_ge(pv_done, 2 * HEADS)
                z_high(n)
            for t in range(NT):
                q = t % 2
                act.wait_ge(ln_mean, t + 1)
                if t >= 1:
                    act.wait_ge(ln_ssq, t)
                nc.scalar.activation(ln_sq[:, :], ln_v[q][:, :], ACT.Square, bias=stat[:, 2 + q:3 + q],
                                     accum_out=stat[:, 4 + q:5 + q]).then_inc(ln_ssq, 1)
                act.wait_ge(ln_ssq, t + 1)
                nc.scalar.activation(stat[:, 6 + q:7 + q], stat[:, 4 + q:5 + q], ACT.Sqrt, scale=1.0 / D,
                                     bias=eps[:, 1:2]).then_inc(ln_root, 1)

        @block.vector
        def _(dve):
            step = Steps(dve, dve_step)
            V = nc.vector
            for free in (x1_done, *ff_conv, *ff_v, *dn_done):
                nc.vector.sem_inc(free, 1)

            def col(c):
                return vec[:, c:c + 1] if isinstance(c, int) else vec[:, bass.ds(c, 1)]

            def norm(i, gain, dst, rb, lo_before):
                def value(c):
                    if c >= 4 and lo_before:
                        dve.wait_ge(lo_pool if c % 2 else lo_dve, 4 * i + (c - 4) // 2 + 1)
                    V.scalar_tensor_tensor(out=dst(c), in0=xs[:, c, :], scalar=col(gain + c), in1=rb,
                                           op0=ALU.mult, op1=ALU.mult).then_inc(v_done, 1)

                value(0)
                for c in range(KT):
                    if c + 1 < KT:
                        value(c + 1)
                    if c % 2 == 0:
                        low(i, c, dst(c))

            def low(i, c, src):
                dve.wait_ge(hi_done, 8 * i + c + 1)
                V.tensor_tensor(h_lo[:, c, :], src, h_hi[:, c, :].bitcast(f32), ALU.subtract).then_inc(lo_dve, 1)

            def tap(acc, src, shift, c):
                return V.scalar_tensor_tensor(out=acc[:, shift:SEQ], in0=src[:, 0:SEQ - shift], scalar=col(c),
                                              in1=acc[:, shift:SEQ], op0=ALU.mult, op1=ALU.add)

            for q in range(4):
                V.memset(sign[32 * q:32 * q + 32, :], -1.0 if q % 2 == 0 else 1.0).then_inc(sign_done, 1)
            for n in range(NT - 1):
                if n % 2 == 0:
                    dve.wait_ge(x_in[n // 2], 16)
                if n >= 1:
                    dve.wait_ge(sumsq_dve, n)
                V.tensor_tensor_reduce(out=square_dve[:, :], in0=x_tok[:, n, :], in1=x_tok[:, n, :], scale=1.0,
                                       scalar=0.0, op0=ALU.mult, op1=ALU.add, accum_out=small[:, n:n + 1]
                                       ).then_inc(sumsq_dve, 1)
            dve.wait_ge(root_done, 1)
            V.reciprocal(rstd[:, :], small[:, 8:16]).then_inc(rstd_done, 1)
            dve.wait_ge(rows_in, 16 * 16)
            V.tensor_copy(pos_rows[0:NT, :], pos_rows_i[0:NT, :]).then_inc(pos_f_done, 1)
            dve.wait_ge(vec_done, 1)
            dve.wait_ge(rb_done, 1)
            dve.wait_ge(xt_copied, NT)
            norm(0, V_NORM1, lambda c: scr[c % 4][:, :], ps[2][:, :], True)
            step(V.scalar_tensor_tensor(out=small[:, 16:24], in0=vec[:, V_LAM:V_LAM + 8], scalar=-1.0,
                                        in1=vec[:, V_LAM:V_LAM + 8], op0=ALU.mult, op1=ALU.min))
            V.tensor_scalar(half_ba[:, :], vec[:, V_BA:V_BA + 8], 0.5, None, ALU.mult).then_inc(lam_abs, 1)
            step(V.tensor_scalar(half_bx[:, :], vec[:, V_BX:V_BX + 8], 0.5, None, ALU.mult))
            step(V.tensor_scalar(half_ps[:, :], vec[:, V_POOL:V_POOL + 4], 0.5, None, ALU.mult))
            dve.wait_ge(lam_exp, 1)
            e, z, z2, pl = small[:, 24:32], small[:, 32:40], small[:, 40:48], small[:, 16:24]
            step(V.tensor_scalar(z, e, 2.0, None, ALU.add))
            step(V.reciprocal(z2, z))
            step(V.tensor_tensor(z, e, z2, ALU.mult))
            step(V.tensor_tensor(z2, z, z, ALU.mult))
            step(V.tensor_scalar(pl, z2, 1.0 / 15, None, ALU.mult))
            for k in (13, 11, 9, 7, 5, 3):
                step(V.scalar_tensor_tensor(out=pl, in0=pl, scalar=1.0 / k, in1=z2, op0=ALU.add, op1=ALU.mult))
            step(V.scalar_tensor_tensor(out=pl, in0=pl, scalar=1.0, in1=z, op0=ALU.add, op1=ALU.mult))
            step(V.tensor_scalar(z, vec[:, V_LAM:V_LAM + 8], -2.0, 0.0, ALU.mult, ALU.max))
            step(V.scalar_tensor_tensor(out=kh[:, :], in0=pl, scalar=4.0, in1=z, op0=ALU.mult, op1=ALU.add))
            V.tensor_scalar(kx[:, :], kh[:, :], -2.0, None, ALU.mult).then_inc(params_done, 1)

            for j in range(SC_TILES):
                dve.wait_ge(block_done, read(3 * j + 1))
                dve.wait_ge(sc_c, j + 1)
                V.tensor_tensor(scr[1][:, :], ps[(3 * j + 1) % 4][:, :], scr[0][:, :], ALU.mult).then_inc(sc_p, 1)
                dve.wait_ge(sc_base, j + 1)
                step(tap(scr[2], scr[1], 1, V_SCW + 4 + j))
                step(tap(scr[2], scr[1], 2, V_SCW + j))
                dve.wait_ge(block_done, read(3 * j + 2))
                if j >= 1:
                    dve.wait_ge(sc_lo, j)
                V.tensor_tensor(scr[3][:, :], ps[(3 * j + 2) % 4][:, :], scr[2][:, :], ALU.mult).then_inc(sc_y, 1)

            def convolve(c, one):
                xc = xs[:, one, :].rearrange("p o t -> p (o t)")
                dve.wait_ge(conv_base, c + 1)
                step(tap(xc, ps[0], 1, V_CONVW + 16 + c))
                step(tap(xc, ps[0], 2, V_CONVW + 8 + c))
                tap(xc, ps[0], 3, V_CONVW + c).then_inc(conv_done, 1)

            def recur(c, one):
                xc = xs[:, one, :].rearrange("p o t -> p (o t)")
                dve.wait_ge(ex_done, c + 1)
                step(V.tensor_scalar(scr[3][:, :], scr[3][:, :], 0.5, 0.5, ALU.mult, ALU.add))
                step(V.scalar_tensor_tensor(out=scr[1][:, :], in0=scr[4][:, :], scalar=1.0, in1=scr[3][:, :],
                                            op0=ALU.add, op1=ALU.mult))
                step(V.scalar_tensor_tensor(out=scr[1][:, :], in0=scr[1][:, :], scalar=-2.0, in1=scr[3][:, :],
                                            op0=ALU.add, op1=ALU.mult))
                step(V.tensor_scalar(scr[3][:, :], scr[1][:, :], -2.0, -1.0, ALU.mult, ALU.add))
                dve.wait_ge(it_done, c + 1)
                step(V.scalar_tensor_tensor(out=scr[2][:, :], in0=scr[2][:, :], scalar=1.0, in1=xc,
                                            op0=ALU.add, op1=ALU.mult))
                dve.wait_ge(root_s, c + 1)
                step(V.tensor_tensor(root[:, :], scr[1][:, :], root[:, :], ALU.mult))
                step(V.tensor_tensor(root[:, :], root[:, :], scr[2][:, :], ALU.mult))
                step(V.tensor_tensor_scan(xc, scr[3][:, :], root[:, :], 0.0, ALU.mult, ALU.subtract))
                dve.wait_ge(gelu_done, c + 1)
                V.tensor_tensor(xc, xc, (gelu_last if one is last else gelu_gate)[:, :], ALU.mult).then_inc(y_done, 1)

            def second_parts(c, one):
                dve.wait_ge(bd_hi_done, c + 1)
                step(V.tensor_tensor(bd_lo[:, :, :], bd_raw[:, :, one, :].rearrange("p w o n -> p w (o n)"),
                                     bd_hi[:, :, :].bitcast(f32), ALU.subtract))
                dve.wait_ge(xc_hi_done, c + 1)
                V.tensor_tensor(xc_lo[:, :].unsqueeze(1), xs[:, one, :], xc_hi[:, :].bitcast(f32).unsqueeze(1),
                                ALU.subtract).then_inc(xc_lo_done, 1)

            first, last = slice(0, 1), slice(LRU_TILES - 1, LRU_TILES)
            convolve(0, first)
            second_parts(0, first)
            with step.of(11).loop(LRU_TILES - 2) as i:
                c = i + 1
                convolve(c, bass.ds(c, 1))
                recur(i, bass.ds(i, 1))
                second_parts(c, bass.ds(c, 1))
            c = LRU_TILES - 1
            convolve(c, last)
            second_parts(c, last)
            recur(c - 1, slice(c - 1, c))
            for i in (0, 2, 4):
                low(1, i, xs[:, i, :])
            recur(c, last)

            def add_square(squares, q, steps):
                dve.wait_ge(sq_done, squares)
                dve.wait_ge(acc_done, steps)
                V.tensor_tensor(scr[4][:, :], scr[4][:, :], scr[3 - q % 2][:, :], ALU.add).then_inc(acc_done, 1)

            low(1, 7, xs[:, 7, :])
            dve.wait_ge(hi_done, 16)
            dve.wait_ge(lo_pool, 8)
            with dve.Fori(0, 2) as r:
                for q in range(4):
                    dve.wait_ge(block_done, read(N_OUT + 2 + q, 3 * r))
                    dve.wait_ge(x_back[q % 2], 32 * r + 16 * (q // 2 + 1))
                    V.tensor_tensor(xs[:, bass.ds(4 * r + q, 1), :], ps[q][:, :].unsqueeze(1), scr[q % 2][:, :].unsqueeze(1),
                                    ALU.add).then_inc(x1_done, 1)
                    add_square(4 * r + q + 1, q, 4 * r + q + 3)
            add_square(9, 0, 11)

            def norm_scale(i):
                dve.wait_ge(root_done, i + 1)
                V.reciprocal(rstd[:, :], small[:, 8:16]).then_inc(rstd_done, 1)
                dve.wait_ge(rb_done, i + 1)

            norm_scale(1)
            norm(2, V_NORM2, lambda c: scr[c % 4][:, :], ps[3][:, :], True)

            def ff_group(g, h0, squares=False):
                with step.of(4).loop(FF_GROUP // 2) as fp:
                    for q in range(2):
                        f, turn = 8 * g + 2 * fp + q, 4 * g + fp
                        for part in range(2):
                            s, dst = 2 * q + part, scr[q + 2 * part]
                            dve.wait_ge(ff_base[s], turn + 1)
                            step(tap(dst, ps[s], 1, V_FFN + 48 + 24 * part + f))
                            tap(dst, ps[s], 2, V_FFN + 24 * part + f).then_inc(ff_conv[s], 1)
                        dve.wait_ge(ff_gelu[q], turn + 1)
                        dve.wait_ge(ff_conv[2 * q + 1], turn + 1 + 1)
                        V.tensor_tensor(scr[2 + q][:, :], scr[q][:, :], scr[2 + q][:, :], ALU.mult).then_inc(ff_v[q], 1)
                with dve.Fori(0, 2) as dp:
                    for b in range(4):
                        dve.wait_ge(block_done, read(N_FF + 16 + b, h0 + 2 * dp))
                        d = bass.ds(4 * dp + b, 1)
                        V.tensor_tensor(xs[:, d, :], ps[b][:, :].unsqueeze(1), xs[:, d, :], ALU.add).then_inc(dn_done[b], 1)
                        if squares:
                            add_square(8 + 4 * dp + b + 1, b, 14 + 4 * dp + b)

            with step.of(16).loop(GROUPS - 1) as g:
                ff_group(g, 12 * g)
            ff_group(GROUPS - 1, 12 * (GROUPS - 1), True)
            add_square(17, 0, 22)

            norm_scale(2)
            norm(3, V_FINAL, lambda c: xs[:, c, :], ps[3][:, :], False)

            dve.wait_ge(block_done, N_IN2)
            for i in range(Q_TILES + KV_TILES):
                dve.wait_ge(block_done, read(N_IN2 + i))
                V.tensor_copy(lat[:, i, :], ps[i % 2][:, :]).then_inc(lat_done, 1)
                if i == 0:
                    dve.wait_ge(pos_in, 16)
                    step(V.tensor_copy(pos_f[:, :], pos_i[:, :]))
                    step(V.tensor_scalar(scr[2][:, :], pos_f[:, :], freq[:, 0:1], None, ALU.mult))
                if i in (0, 1):
                    t = (sin_t, cos_t)[i]
                    step(V.tensor_scalar(scr[3][:, :], scr[2][:, :], float(1 / (2 * np.pi)), 0.25 * i,
                                         ALU.mult, ALU.add))
                    step(V.tensor_scalar(scr[3][:, :], scr[3][:, :], ROUND, None, ALU.add))
                    step(V.tensor_scalar(scr[3][:, :], scr[3][:, :], ROUND, None, ALU.subtract))
                    src = scr[2]
                    for part in (TWO_PI_A, TWO_PI_B, TWO_PI_C):
                        step(V.scalar_tensor_tensor(out=t[:, :], in0=scr[3][:, :], scalar=-part, in1=src[:, :],
                                                    op0=ALU.mult, op1=ALU.add))
                        src = t
                    step(V.tensor_scalar(t[:, :], t[:, :], float(np.pi / 2) * i, 3.1415925, ALU.add, ALU.min))
                    V.tensor_scalar(t[:, :], t[:, :], -3.1415925, None, ALU.max).then_inc(red_done, 1)

            for q in range(2):
                dve.wait_ge(res_parked[q], 16 * NT // 2)
            def pooled_gate(g):
                dve.wait_ge(pool_mm, g + 1)
                dve.wait_ge(gb_done, g + 1)
                V.scalar_tensor_tensor(out=y_pool[:, g, :], in0=ps[2][:, :], scalar=half_ps[:, g:g + 1],
                                       in1=y_pool[:, g, :], op0=ALU.mult, op1=ALU.mult).then_inc(yb_done, 1)

            for g, w in enumerate(WINDOWS):
                dve.wait_ge(block_done, read(N_POOL + 2 * g))
                V.tensor_copy(scr[0][:, :], ps[0][:, :]).then_inc(u_done, 1)
                dve.wait_ge(u_done, g + 1)
                src, shift, k = scr[0], 1, 0
                while shift < w:
                    dst = scr[1 + k % 2]
                    step(V.tensor_tensor(dst[:, shift:SEQ], src[:, shift:SEQ], src[:, 0:SEQ - shift], ALU.add))
                    step(V.tensor_copy(dst[:, 0:shift], src[:, 0:shift]))
                    src, shift, k = dst, 2 * shift, k + 1
                if g >= 1:
                    pooled_gate(g - 1)
                    dve.wait_ge(pl_lo, g)
                step(V.scalar_tensor_tensor(out=scr[3][:, :], in0=src[:, :], scalar=1.0 / w, in1=scr[0][:, :],
                                            op0=ALU.mult, op1=ALU.subtract))
                if g == 0:
                    dve.wait_ge(const_done, 21)
                step(V.tensor_tensor(small[:, 16:16 + w - 1], src[:, 0:w - 1], rc[:, 0:w - 1], ALU.mult))
                V.tensor_tensor(scr[3][:, 0:w - 1], small[:, 16:16 + w - 1], scr[0][:, 0:w - 1],
                                ALU.subtract).then_inc(pl_done, 1)
                dve.wait_ge(pw_hi_done, g + 1)
                step(V.tensor_tensor(pw_lo[:, :], pw_raw[:, g, :], pw_hi[:, :].bitcast(f32), ALU.subtract))
                if g < 2:
                    dve.wait_ge(root2_done, g + 1)
                    scale = (acc_q, acc_kv)[g]
                    V.reciprocal(scale[:, :], scale[:, :]).then_inc(rstd2_done, 1)
                dve.wait_ge(th_done, g + 1)
                V.scalar_tensor_tensor(out=y_pool[:, g, :], in0=y_pool[:, g, :], scalar=1.0, in1=ps[1][:, :],
                                       op0=ALU.add, op1=ALU.mult).then_inc(gb_done, 1)

            def gate(h):
                dve.wait_ge(ga_th, h + 1)
                V.scalar_tensor_tensor(out=scr[h % 2][:, :], in0=scr[h % 2][:, :], scalar=1.0, in1=ps[h % 2][:, :],
                                       op0=ALU.add, op1=ALU.mult).then_inc(ga_done, 1)

            gate(0)
            pooled_gate(3)
            gate(1)
            dve.wait_ge(rstd2_done, 2)
            for i in range(KV_TILES + Q_TILES):
                kv = i < KV_TILES
                V.scalar_tensor_tensor(out=lat_tile(i), in0=lat_tile(i),
                                       scalar=col(V_KVN + i if kv else V_QN + i - KV_TILES),
                                       in1=(acc_kv if kv else acc_q)[:, :], op0=ALU.mult, op1=ALU.mult
                                       ).then_inc(latn_done, 1)
            for i in range(0, KV_TILES + Q_TILES, 2):
                hi, lo = latents()[i]
                dve.wait_ge(latn_hi, i + 1)
                V.tensor_tensor(lo, lat_tile(i), hi.bitcast(f32), ALU.subtract).then_inc(latn_lo_d, 1)
            gate(2)
            gate(3)

            def rotate(r, src):
                if r == 0:
                    for q in range(2):
                        dve.wait_ge(gate_parked[q], 16 * HEADS // 2)
                dve.wait_ge(rope_sw, 4 * r + 4)
                V.tensor_tensor(scr[0][:, :], src[:, :], cos_t[:, :], ALU.mult).then_inc(rope_a, 1)
                sw = (scr[1], scr[3], scr[1])[r]
                step(V.tensor_tensor(sw[:, :], sw[:, :], sin_t[:, :], ALU.mult))
                dve.wait_ge(rope_a, r + 1)
                V.tensor_tensor(scr[2][:, :], scr[0][:, :], sw[:, :], ALU.add).then_inc(rope_v, 1)
                dve.wait_ge(rope_hi, 2 * r + 1)
                if r == 0:
                    V.tensor_tensor(kr_lo[:, :], scr[2][:, :], kr_hi[:, :].bitcast(f32), ALU.subtract).then_inc(rope_lo, 1)
                    return
                dve.wait_ge(rope_v, r + 1)
                step(V.tensor_tensor(sw[0:64, :], scr[2][0:64, :], qr[0:64, 2 * r - 2, :].bitcast(f32), ALU.subtract))
                V.tensor_tensor(sw[64:P, :], scr[2][64:P, :], qr[64:P, 2 * r - 1, :].bitcast(f32),
                                ALU.subtract).then_inc(rope_lo, 1)

            def up_low(j, hi, lo, **split):
                src = ps[(j + 1) % 4][:, :]
                dve.wait_ge(nope_hi, j - 2 + 1)
                V.tensor_tensor(lo, src.rearrange("p (t d) -> p t d", t=2) if split else src, hi.bitcast(f32),
                                ALU.subtract).then_inc(nope_lo, 1)

            dve.wait_ge(trig_done, 2)
            dve.wait_ge(block_done, read(N_KR))
            rotate(0, ps[0])
            for r in range(2):
                dve.wait_ge(*up_ready(r))
                rotate(r + 1, ps[r + 1])
            for h in range(HEADS):
                up_low(2 + h, qh_hi[:, h, :], qh_lo[:, h, :])
            for h in range(HEADS):
                up_low(6 + h, kn_hi[:, h, :], kn_lo[:, h, :])
            for i in range(4):
                up_low(10 + i, v_hi[:, 2 * i:2 * i + 2, :], v_lo[:, 2 * i:2 * i + 2, :], token_pairs=True)

            def z_low(n):
                dve.wait_ge(z_hi_done, n + 1)
                e, k, raw = z_tiles(n)
                V.tensor_tensor(wo_lo[e][:, k, :], raw, wo_hi[e][:, k, :].bitcast(f32),
                                ALU.subtract).then_inc(z_lo_done, 1)

            def even_mask(u):
                if u >= 2:
                    dve.wait_ge(smax_done, u - 1)
                V.tensor_scalar(mask[0][:, :], pos_f[:, :], col(V_POS + u % NT), MASKED, ALU.is_gt,
                                ALU.mult).then_inc(mask_done[0], 1)

            even_mask(0)
            for u in range(UNITS + 3):
                if u < UNITS:
                    s = u % 3
                    dve.wait_ge(score_done, u + 1)
                    dve.wait_ge(mask_done[u % 2], u // 2 + 1)
                    if u >= 3:
                        dve.wait_ge(pt_done, u - 2)
                    V.tensor_tensor_reduce(out=prob[s][:, :], in0=ps[u % 2][:, :], in1=mask[u % 2][:, :],
                                           scale=1.0, scalar=-3.0e38, op0=ALU.add, op1=ALU.max,
                                           accum_out=stat[:, s:s + 1]).then_inc(smax_done, 1)
                    dve.wait_ge(smax_done, u + 1)
                    V.tensor_scalar(stat[:, 3 + s:4 + s], stat[:, s:s + 1], -SCALE, None, ALU.mult
                                    ).then_inc(nmax_done, 1)
                    if u % 2 == 1 and u + 1 < UNITS:
                        even_mask(u + 1)
                if u in (18, 26):
                    z_low(0 if u == 18 else 2)
                if 2 <= u <= UNITS + 1:
                    w = u - 2
                    q = (w % 4) * P
                    dve.wait_ge(pt_hi_done, w + 1)
                    pt = ps[2][:, :].rearrange("p (k q) -> p k q", k=NT)
                    for k in (slice(0, NT // 2), slice(NT // 2, NT)):
                        V.tensor_tensor(pt_lo[:, k, q:q + P], pt[:, k, :], pt_hi[:, k, q:q + P].bitcast(f32),
                                        ALU.subtract).then_inc(pt_lo_done, 1)
                if u < UNITS:
                    dve.wait_ge(exp_done, u + 1)
                    V.reciprocal(stat[:, 9 + s:10 + s], stat[:, 6 + s:7 + s]).then_inc(inv_done, 1)
                if u == UNITS + 1:
                    for n in (4, 6):
                        z_low(n)
                if u >= 6 and (u - 2) % 4 == 0:
                    i = (u - 2) // 4 - 1
                    dve.wait_ge(pv_done, i + 1)
                    dve.wait_ge(gate_back[i % 2], 16 * (i // 2 + 1))
                    if i >= 2:
                        dve.wait_ge(ya_parked[i % 2], 16 * (i // 2))
                    V.scalar_tensor_tensor(out=ya_out[i % 2][:, :], in0=ps[3][:, (i % 2) * HALF:(i % 2 + 1) * HALF],
                                           scalar=0.5, in1=gate_in[i % 2][:, :], op0=ALU.mult, op1=ALU.mult
                                           ).then_inc(ya_done, 1)
            for n in range(8, 16, 2):
                z_low(n)
            dve.wait_ge(last_in, 16 * 4)

            def ln_first(t):
                q = t % 2
                dve.wait_ge(mix_done, t + 1)
                if t >= 2:
                    dve.wait_ge(stored[q], 16 * (t // 2))
                V.scalar_tensor_tensor(out=ln_v[q][:, :], in0=ps[t % 4][:, :], scalar=1.0,
                                       in1=resid[:, t, :] if t < 6 else resid_last[:, t - 6, :],
                                       op0=ALU.mult, op1=ALU.add, accum_out=stat[:, q:q + 1]).then_inc(ln_sum, 1)
                dve.wait_ge(ln_sum, t + 1)
                V.tensor_scalar(stat[:, 2 + q:3 + q], stat[:, q:q + 1], -1.0 / D, None, ALU.mult).then_inc(ln_mean, 1)

            ln_first(0)
            for t in range(NT):
                q = t % 2
                if t < 3:
                    ln_first(t + 1)
                if t >= 1:
                    dve.wait_ge(ln_out, t)
                dve.wait_ge(ln_mean, t + 1)
                step(V.scalar_tensor_tensor(out=ln_y[:, :], in0=ln_v[q][:, :], scalar=stat[:, 2 + q:3 + q],
                                            in1=ln_g[:, :], op0=ALU.add, op1=ALU.mult))
                dve.wait_ge(ln_root, t + 1)
                step(V.reciprocal(stat[:, 8 + q:9 + q], stat[:, 6 + q:7 + q]))
                for c in out_parts(t):
                    V.scalar_tensor_tensor(out=ln_v[q][:, c], in0=ln_y[:, c], scalar=stat[:, 8 + q:9 + q],
                                           in1=ln_b[:, c], op0=ALU.mult, op1=ALU.add).then_inc(ln_out, 1)
                if 3 <= t < NT - 1:
                    ln_first(t + 1)

        @block.tensor
        def _(pe):
            def blocked(n):
                return [w[n % 2][:, :].rearrange("p (k n) -> p k n", n=P) for w in (w_hi, w_lo)]

            def project(n, h, dst, x_h, x_l):
                pe.wait_ge(w_lo_done, n + 1 + 2 * h)
                wh, wl = blocked(n)
                for k in range(8):
                    mm = matmul3(pe, dst, wh[:, k, :], wl[:, k, :], x_h[:, k, :], x_l[:, k, :], k == 0, k == 7)
                mm.then_inc(block_done, 1)

            def mean_squares(acc, dst):
                for t in range(NT):
                    mm = nc.tensor.matmul(dst[:, t:t + 1], acc[:, t * P:(t + 1) * P], meanw[:, 0:1],
                                          start=True, stop=True)
                return mm

            def spread(dst):
                for t in range(NT):
                    mm = nc.tensor.matmul(dst[:, t * P:(t + 1) * P],
                                          rstd[:, t:t + 1].to_broadcast([P, P]),
                                          ident[:, :], start=True, stop=True)
                return mm

            pe.wait_ge(ident_done, 1)
            for t in range(NT):
                if t % 2 == 0:
                    pe.wait_ge(x_in[t // 2], 16)
                if t >= 3:
                    pe.wait_ge(xt_copied, t - 2)
                for c in range(KT):
                    mm = nc.tensor.transpose(ps[t % 3][:, c * P:(c + 1) * P], x_tok[:, t, c * P:(c + 1) * P], ident[:, :])
                mm.then_inc(xt_done, 1)
            pe.wait_ge(rows_in, 16 * 16)
            pe.wait_ge(pos_f_done, 1)
            for src, n, c in ((rows0, V_ROWS, 0), (rows1, 72, V_FFN), (rows2, 72, V_FFN + 72), (pos_rows, NT, V_POS)):
                mm = nc.tensor.transpose(ps[3][:, c:c + n], src[0:n, 0:P], ident[0:n, 0:n])
            mm.then_inc(vec_t, 1)
            pe.wait_ge(rstd_done, 1)
            spread(ps[2]).then_inc(rb_done, 1)

            def first_two(n, dsts, i):
                for k in range(8 + 3):
                    for b, j in ((0, k), (1, k - 3)):
                        if not 0 <= j < 8:
                            continue
                        if j == 0:
                            pe.wait_ge(w_lo_done, n + b + 1)
                        if b == 0:
                            pe.wait_ge(lo_dve if j % 2 == 0 else lo_pool, 4 * i + j // 2 + 1)
                        wh, wl = blocked(n + b)
                        mm = matmul3(pe, dsts[b], wh[:, j, :], wl[:, j, :], h_hi[:, j, :], h_lo[:, j, :], j == 0, j == 7)
                        if j == 7:
                            mm.then_inc(block_done, 1)

            pe.wait_ge(xt_copied, NT)
            first_two(0, (ps[0], ps[1]), 0)
            readers = (sc_c, sc_p, sc_y)
            for n in range(2, 3 * SC_TILES):
                if n == 2:
                    pe.wait_ge(v_done, 8)
                if n >= 4:
                    m = n - 4
                    pe.wait_ge(readers[m % 3], m // 3 + 1)
                project(n, 0, ps[n % 4], h_hi, h_lo)
            def gates():
                matmul3(pe, ps[2], bd_hi[:, 0, :], bd_lo[:, 0, :], xc_hi, xc_lo, True, True).then_inc(ri_done, 1)
                matmul3(pe, ps[3], bd_hi[:, 1, :], bd_lo[:, 1, :], xc_hi, xc_lo, True, True).then_inc(ri_done, 1)

            pe.wait_ge(sc_y, 3)
            project(N_LRU, 0, ps[0], h_hi, h_lo)
            pe.wait_ge(sc_c, 4)
            project(N_LRU + 1, 0, ps[1], h_hi, h_lo)
            pe.wait_ge(sc_y, 4)
            with pe.Fori(1, LRU_TILES) as c:
                pe.wait_ge(conv_done, c)
                project(N_LRU, c, ps[0], h_hi, h_lo)
                pe.wait_ge(xc_lo_done, c)
                gates()
                pe.wait_ge(gelu_done, c)
                project(N_LRU + 1, c, ps[1], h_hi, h_lo)
            pe.wait_ge(xc_lo_done, LRU_TILES)
            gates()
            pe.wait_ge(conv_done, LRU_TILES)
            pe.wait_ge(gelu_done, LRU_TILES)
            pe.wait_ge(sc_lo, SC_TILES)
            with pe.Fori(0, 2) as r:
                for b in range(6):
                    n = N_OUT + b
                    if b < 2:
                        if b == 1:
                            pe.wait_ge(it_done, LRU_TILES)
                        pe.wait_ge(x1_done, 2 * (b + 1) * r + 1)
                        pe.wait_ge(w_lo_done, n + 1 + 6 * r)
                        wh, wl = [w[n % 2][:, :].rearrange("p (k e n) -> p k e n", k=4, e=2) for w in (w_hi, w_lo)]
                        for e in range(2):
                            for k in range(4):
                                mm = matmul3(pe, ps[2 * b + e], wh[:, k, e, :], wl[:, k, e, :], ysc_hi[:, k, :],
                                             ysc_lo[:, k, :], k == 0, False)
                        mm.then_inc(block_done, 1)
                    else:
                        pe.wait_ge(w_lo_done, n + 1 + 6 * r)
                        wh, wl = blocked(n)
                        for k in range(8):
                            if b == 2:
                                vector_has, gpsimd_has = (0, 2, 4, 7), (1, 3, 5, 6)
                                if k in vector_has:
                                    pe.wait_ge(lo_dve, 4 + vector_has.index(k) + 1)
                                else:
                                    pe.wait_ge(lo_pool, 4 + gpsimd_has.index(k) + 1)
                            mm = matmul3(pe, ps[b - 2], wh[:, k, :], wl[:, k, :], h_hi[:, k, :], h_lo[:, k, :],
                                         False, k == 7)
                        mm.then_inc(block_done, 1)

            def norm(i, acc_value):
                pe.wait_ge(acc_done, acc_value)
                mean_squares(scr[4], ps[2]).then_inc(ms_done, 1)
                pe.wait_ge(rstd_done, i + 1)
                spread(ps[3]).then_inc(rb_done, 1)

            norm(1, 12)
            def ff_up(g, fp, blocks):
                for b in blocks:
                    pe.wait_ge(ff_conv[b], 4 * g + fp + 1)
                    pe.wait_ge(dn_done[b], 2 * g + 1)
                    project(N_FF + b, 12 * g + 2 * fp, ps[b], h_hi, h_lo)

            def ff_down(g):
                with pe.Fori(0, 2) as dp:
                    for pair in range(2):
                        d0, d1 = 2 * pair, 2 * pair + 1
                        for b, ks in ((d0, range(7)), (d1, range(4)), (d0, range(7, 8)), (d1, range(4, 8))):
                            n = N_FF + 2 * FF_GROUP + b
                            if ks[0] == 0:
                                pe.wait_ge(ff_conv[b], 4 * g + 4 + 1)
                                pe.wait_ge(dn_done[b], 2 * g + dp + 1)
                                pe.wait_ge(w_lo_done, n + 1 + 24 * g + 4 * dp)
                                pe.wait_ge(ff_lo[0], 4 * g + 4 + 1)
                                pe.wait_ge(ff_lo[1], 4 * g + 3 + 1)
                            elif ks[0] == 7:
                                pe.wait_ge(ff_lo[1], 4 * g + 4 + 1)
                            wh, wl = blocked(n)
                            for k in ks:
                                mm = matmul3(pe, ps[b], wh[:, k, :], wl[:, k, :], gu_hi[:, k, :], gu_lo[:, k, :],
                                             k == 0, k == 7)
                            if ks[-1] == 7:
                                mm.then_inc(block_done, 1)

            first_two(N_FF, (ps[0], ps[1]), 2)
            pe.wait_ge(v_done, 16)
            ff_up(0, 0, (2, 3))
            with pe.Fori(1, FF_GROUP // 2) as fp:
                ff_up(0, fp, range(4))
            ff_down(0)
            with pe.Fori(1, GROUPS) as g:
                with pe.Fori(0, FF_GROUP // 2) as fp:
                    ff_up(g, fp, range(4))
                ff_down(g)
            norm(2, 23)
            def by_token(t):
                if t >= 2:
                    pe.wait_ge(tok_copied, t - 1)
                for k in range(KT):
                    mm = nc.tensor.transpose(ps[2 + t % 2][:, k * P:(k + 1) * P], xs[:, k, t * P:(t + 1) * P], ident[:, :])
                mm.then_inc(tok_t, 1)

            first_two(N_IN2, (ps[0], ps[1]), 3)
            pe.wait_ge(v_done, 24)
            for i in range(2, Q_TILES + KV_TILES):
                by_token(2 * i - 4)
                by_token(2 * i - 3)
                pe.wait_ge(lat_done, i - 1)
                project(N_IN2 + i, 0, ps[i % 2], h_hi, h_lo)
            def pool_product():
                matmul3(pe, ps[2], pw_hi[:, :], pw_lo[:, :], pooled_hi, pooled_lo, True, True).then_inc(pool_mm, 1)

            pe.wait_ge(tok_copied, NT)
            pe.wait_ge(lat_done, 5)
            project(N_POOL, 0, ps[0], h_hi, h_lo)
            def spread_mean_squares(acc, which):
                for t in (slice(0, HALF), slice(HALF, SEQ)):
                    mm = nc.tensor.matmul(ps[3][:, t], meanw[:, which:which + 1].to_broadcast([P, P]), acc[:, t],
                                          start=True, stop=True)
                mm.then_inc(ms2_done, 1)

            pe.wait_ge(acc_q_done, Q_TILES + 1)
            spread_mean_squares(acc_q, 1)
            pe.wait_ge(lat_done, 6)
            project(N_POOL + 1, 0, ps[1], h_hi, h_lo)
            pe.wait_ge(acc_kv_done, KV_TILES + 1)
            pe.wait_ge(root2_done, 1)
            spread_mean_squares(acc_kv, 2)
            with pe.Fori(1, len(WINDOWS)) as g:
                pe.wait_ge(u_done, g)
                project(N_POOL, g, ps[0], h_hi, h_lo)
                pe.wait_ge(gb_done, g)
                pe.wait_ge(pl_lo, g)
                pool_product()
                project(N_POOL + 1, g, ps[1], h_hi, h_lo)
            for h in range(HEADS):
                if h == 0:
                    pe.wait_ge(u_done, 4)
                elif h == 1:
                    pe.wait_ge(pl_lo, 4)
                    pe.wait_ge(gb_done, 4)
                    pool_product()
                else:
                    pe.wait_ge(ga_done, h - 1)
                project(N_GATE + h, 0, ps[h % 2], h_hi, h_lo)
            pe.wait_ge(ga_done, 3)
            project(N_KR, 0, ps[0], h_hi, h_lo)
            def free_slot(j):
                if j == 0:
                    pe.wait_ge(ga_done, 4)
                elif j == 1:
                    pe.wait_ge(yb_done, 4)
                elif j == 2:
                    pe.wait_ge(root2_done, 2)
                elif 3 <= j <= 5:
                    pe.wait_ge(rope_a, j - 2)
                elif j >= 6:
                    pe.wait_ge(nope_lo, j - 5)

            pe.wait_ge(latn_lo_d, 3)
            pe.wait_ge(latn_lo_p, 3)
            for b in range(3):
                n = N_UQ + b
                pe.wait_ge(w_lo_done, n + 1)
                wh, wl = [w[n % 2][:, :].rearrange("p (k e n) -> p k e n", k=4, e=2) for w in (w_hi, w_lo)]
                for e in range(2):
                    j = 2 * b + e
                    free_slot(j)
                    for k in range(4):
                        mm = matmul3(pe, ps[(j + 1) % 4], wh[:, k, e, :], wl[:, k, e, :], qn_hi[:, k, :],
                                     qn_lo[:, k, :], k == 0, k == 3)
                    mm.then_inc(up_ready(j)[0], 1)
            n = N_UKV
            pe.wait_ge(w_lo_done, n + 1)
            wh, wl = [w[n % 2][:, :].rearrange("p (k h n) -> p k h n", k=2, h=HEADS) for w in (w_hi, w_lo)]
            for h in range(HEADS):
                free_slot(6 + h)
                for k in range(2):
                    mm = matmul3(pe, ps[(7 + h) % 4], wh[:, k, h, :], wl[:, k, h, :], kvn_hi[:, k, :],
                                 kvn_lo[:, k, :], k == 0, k == 1)
                mm.then_inc(up_ready(6 + h)[0], 1)
            n = N_UKV + 1
            pe.wait_ge(w_lo_done, n + 1)
            wh, wl = [w[n % 2][:, :].rearrange("p (k n) -> p k n", k=2) for w in (w_hi, w_lo)]
            for t in range(NT):
                j = 10 + t // 2
                if t % 2 == 0:
                    free_slot(j)
                dst = ps[(j + 1) % 4][:, (t % 2) * HALF:(t % 2 + 1) * HALF]
                cols_t = slice(t * P, (t + 1) * P)
                for k in range(2):
                    for a, b, first, last in ((kvn_hi, wh, k == 0, False), (kvn_hi, wl, False, False),
                                              (kvn_lo, wh, False, k == 1)):
                        mm = nc.tensor.matmul(dst, a[:, k, cols_t], b[:, k, :], start=first, stop=last)
                if t % 2 == 1:
                    mm.then_inc(up_ready(j)[0], 1)

            def scores(u):
                h, t = u // NT, slice((u % NT) * P, (u % NT + 1) * P)
                r = slice(64 * (h % 2), 64 * (h % 2) + 64)
                for half in range(2):
                    keys = slice(half * HALF, (half + 1) * HALF)
                    dst = ps[u % 2][:, keys]
                    for i, (q, k) in enumerate(((qh_hi, kn_hi), (qh_hi, kn_lo), (qh_lo, kn_hi))):
                        nc.tensor.matmul(dst, q[:, h, t], k[:, h, keys], start=i == 0, stop=False)
                    nc.tensor.matmul(dst, qr[:, h, t], kr_hi[:, keys], start=False, stop=False)
                    mm = nc.tensor.matmul(dst, qr[r, h, t], kr_lo[r, keys], start=False, stop=True)
                mm.then_inc(score_done, 1)

            def weigh(i):
                h = i // 2
                dst = ps[3][:, (i % 2) * HALF:(i % 2 + 1) * HALF]
                d = slice(h * VDIM, (h + 1) * VDIM)
                for k in range(NT):
                    if k % (NT // 2) == 0:
                        pe.wait_ge(pt_lo_done, 8 * (i + 1) - 1 + k // (NT // 2))
                    for a, b, first, last in ((v_hi, pt_hi, k == 0, False), (v_hi, pt_lo, False, False),
                                              (v_lo, pt_hi, False, k == NT - 1)):
                        mm = nc.tensor.matmul(dst, a[:, k, d], b[:, k, :], start=first, stop=last)
                mm.then_inc(pv_done, 1)

            def mix(t, js):
                cols_t = slice(t * P, (t + 1) * P)
                for j in js:
                    e, k = 1 - j // 4, j % 4
                    if t == 0:
                        pe.wait_ge(z_lo_done, j + 1)
                        pe.wait_ge(zp_lo_done, j + 1)
                    for a, b, first, last in ((z_hi, wo_hi, j == 0, False), (z_hi, wo_lo, False, False),
                                              (z_lo, wo_hi, False, j == KT - 1)):
                        for half in range(2):
                            c = slice(half * HALF, (half + 1) * HALF)
                            mm = nc.tensor.matmul(ps[t % 4][:, c], a[e][:, k, cols_t], b[e][:, k, c], start=first, stop=last)
                if j == KT - 1:
                    mm.then_inc(mix_done, 1)

            pe.wait_ge(rope_lo, 1)
            pe.wait_ge(rope_moved, 4)
            for u in range(UNITS + 3):
                if u < UNITS:
                    if u < 2:
                        pe.wait_ge(nope_lo, 10 + u)
                    else:
                        pe.wait_ge(smax_done, u - 1)
                    scores(u)
                if u in (UNITS, UNITS + 1):
                    pe.wait_ge(smax_done, u - 1)
                    mix(u - UNITS, range(2))
                if u >= 6 and (u - 2) % 4 == 0:
                    i = (u - 2) // 4 - 1
                    if i >= 2:
                        pe.wait_ge(ya_done, i - 1)
                    weigh(i)
                if 2 <= u <= UNITS + 1:
                    w = u - 2
                    pe.wait_ge(p_done, w + 1)
                    if w == 0:
                        pe.wait_ge(nope_lo, 12)
                    for k in range(NT):
                        if w >= 1 and k % (NT // 2) == 0:
                            pe.wait_ge(pt_lo_done, 2 * w - 1 + k // (NT // 2))
                        mm = nc.tensor.transpose(ps[2][:, k * P:(k + 1) * P], prob[w % 3][:, k * P:(k + 1) * P], ident[:, :])
                    mm.then_inc(pt_done, 1)
            for t in range(4):
                if t == 2:
                    pe.wait_ge(pt_lo_done, 2 * UNITS)
                if t == 3:
                    pe.wait_ge(ya_done, 2 * HEADS)
                mix(t, range(2 if t < 2 else 0, 4))
            for t in range(4):
                mix(t, range(4, 8))
            for t in range(4, NT):
                pe.wait_ge(ln_sum, t - 3)
                mix(t, range(8))

_INS = ["x", "norm1_g", "w_in", "lru_conv_w", "lru_conv_b", "lru_wa", "lru_ba", "lru_wx", "lru_bx", "lru_lambda",
        "sc_conv_w", "w_out", "norm2_g", "w_up", "ffn_conv_w", "w_down", "final_g", "positions_2", "w_in_2",
        "q_norm_g_2", "w_uq_2", "kv_norm_g_2", "w_ukv_2", "pool_w_2", "pool_scale_2", "w_out_2", "ln_g_2", "ln_b_2"]


def kernel(**inputs):
    import numpy as _np
    import concourse.bacc as _bacc
    from concourse import mybir as _mybir
    from concourse.bass_utils import run_bass_kernel_spmd as _run

    nc = _bacc.Bacc("TRN2", target_bir_lowering=False, num_devices=1)
    arrays = {name: _np.ascontiguousarray(inputs[name]) for name in _INS}
    half = ROPE // 2
    one = _np.float32(10000.0) ** (-_np.arange(half, dtype=_np.float32) / _np.float32(half))
    arrays["rope_freq"] = _np.tile(one.astype(_np.float32), P // half).reshape(P, 1)
    args = [nc.dram_tensor(f"in_{name}", a.shape, _mybir.dt.from_np(a.dtype), kind="ExternalInput").ap()
            for name, a in arrays.items()]
    out = nc.dram_tensor("out", (1, SEQ, D), _mybir.dt.float32, kind="ExternalOutput").ap()
    program(nc, *args, out)
    r = _run(nc, [{f"in_{name}": a for name, a in arrays.items()}], core_ids=[0])
    return r.results[0]["out"]
```
